# Optimizing a Trainium2 kernel written in Bass

```python
import math
import jax, jax.numpy as jnp
from jax import lax
import numpy as np

D_MODEL = 1024
BATCH = 1
SEQ = 512
DEPTH = 2

N_META = 16
RMS_EPS = 1e-6
D_FF = 4 * D_MODEL
N_EVEN = (DEPTH + 1) // 2
N_ODD = DEPTH // 2
RWKV_HEAD = 64
RWKV_WIDTH = D_MODEL // 2
RWKV_HEADS = RWKV_WIDTH // RWKV_HEAD
DECAY_RANK = 64
ICLR_RANK = 64
GATE_RANK = 128
GN_EPS = RWKV_HEAD * 1e-5
POOL_WIDTH = D_MODEL - RWKV_WIDTH
POOL_WINDOWS = (2, 4, 8, 16)
POOL_GROUPS = len(POOL_WINDOWS)
POOL_GROUP_W = POOL_WIDTH // POOL_GROUPS
SHIFT_WIDTH = 3 * RWKV_WIDTH + DECAY_RANK + ICLR_RANK + GATE_RANK
EVEN_IN = SHIFT_WIDTH + POOL_WIDTH
RWKV_SPLITS = (RWKV_WIDTH, 2 * RWKV_WIDTH, 3 * RWKV_WIDTH,
               3 * RWKV_WIDTH + DECAY_RANK, 3 * RWKV_WIDTH + DECAY_RANK + ICLR_RANK)
DIFF_HEADS = 8
DIFF_HEAD = D_MODEL // (2 * DIFF_HEADS)
DIFF_IN = 3 * D_MODEL
SUBLN_EPS = 1e-5
ROPE_THETA = 10000.0
Q_BLOCK = 128


def rmsnorm(t, g, eps=RMS_EPS):
    tf = t.astype(jnp.float32)
    tf = tf * lax.rsqrt(jnp.mean(tf * tf, axis=-1, keepdims=True) + eps)
    return (tf * g.astype(jnp.float32)).astype(t.dtype)

def rope_tables(length):
    pos = jnp.arange(length, dtype=jnp.float32)
    inv = ROPE_THETA ** (-jnp.arange(0, DIFF_HEAD, 2, dtype=jnp.float32) / DIFF_HEAD)
    ang = pos[:, None] * inv[None, :]
    ang = jnp.concatenate([ang, ang], axis=-1)
    return jnp.cos(ang), jnp.sin(ang)

def apply_rope(t, cos, sin):
    tf = t.astype(jnp.float32)
    t1, t2 = jnp.split(tf, 2, axis=-1)
    rot = jnp.concatenate([-t2, t1], axis=-1)
    c = cos[None, :, None, None, :]
    s = sin[None, :, None, None, :]
    return (tf * c + rot * s).astype(t.dtype)

def rwkv7_scan(r, decay, k, v, kk, a):
    B, L, H, N = r.shape

    def step(S, inp):
        r_t, w_t, k_t, v_t, kk_t, a_t = inp
        sa = jnp.einsum('bhvk,bhk->bhv', S, -kk_t)
        S = (S * w_t[:, :, None, :]
             + sa[..., None] * (kk_t * a_t)[:, :, None, :]
             + v_t[..., None] * k_t[:, :, None, :])
        o = jnp.einsum('bhvk,bhk->bhv', S, r_t)
        return S, o

    xs = tuple(jnp.moveaxis(t, 1, 0) for t in (r, decay, k, v, kk, a))
    S0 = jnp.zeros((B, H, N, N), jnp.float32)
    _, o = lax.scan(step, S0, xs)
    return jnp.moveaxis(o, 0, 1)

def rwkv_pool_mixer(h, w_in, mu, w0, w_up, a0, a_up, g_up, k_k, k_a, r_k,
                    ln_w, ln_b, pool_w, pool_scale, w_out):
    B, L, _ = h.shape
    f32 = jnp.float32
    y = h @ w_in
    ys = y[..., :SHIFT_WIDTH]
    prev = jnp.pad(ys, ((0, 0), (1, 0), (0, 0)))[:, :L]
    ys = ys + (prev - ys) * mu
    r, k, v, wd, ad, gd = jnp.split(ys, RWKV_SPLITS, axis=-1)
    wlog = -jax.nn.softplus(-(w0 + jnp.tanh(wd) @ w_up).astype(f32)) - 0.5
    decay = jnp.exp(-jnp.exp(wlog))
    a = jax.nn.sigmoid((a0 + ad @ a_up).astype(f32))
    g = (jax.nn.sigmoid(gd) @ g_up).astype(f32)
    hs = lambda t: t.reshape(B, L, RWKV_HEADS, RWKV_HEAD)
    kf = k.astype(f32)
    kk = hs(kf * k_k)
    kk = kk / jnp.maximum(jnp.linalg.norm(kk, axis=-1, keepdims=True), 1e-12)
    kf = kf * (1.0 + (a - 1.0) * k_a)
    rf, kf, vf, a_h, dec = hs(r.astype(f32)), hs(kf), hs(v.astype(f32)), hs(a), hs(decay)
    o = rwkv7_scan(rf, dec, kf, vf, kk, a_h)
    mean = jnp.mean(o, axis=-1, keepdims=True)
    var = jnp.mean(jnp.square(o - mean), axis=-1, keepdims=True)
    o = ((o - mean) * lax.rsqrt(var + GN_EPS)).reshape(B, L, RWKV_WIDTH) * ln_w + ln_b
    bonus = jnp.sum(rf * kf * r_k, axis=-1, keepdims=True) * vf
    o = ((o + bonus.reshape(B, L, RWKV_WIDTH)) * g).astype(h.dtype)
    u = y[..., SHIFT_WIDTH:].reshape(B, L, POOL_GROUPS, POOL_GROUP_W).astype(f32)
    t_idx = jnp.arange(L)
    diffs = []
    for gi, win in enumerate(POOL_WINDOWS):
        ug = u[:, :, gi]
        c = jnp.cumsum(ug, axis=1)
        lag = jnp.pad(c, ((0, 0), (win, 0), (0, 0)))[:, :L]
        cnt = jnp.minimum(t_idx + 1, win).astype(f32)[None, :, None]
        diffs.append((c - lag) / cnt - ug)
    d = jnp.stack(diffs, axis=2)
    z = jnp.einsum('blgc,gcd->blgd', d, pool_w.astype(f32)).reshape(B, L, POOL_WIDTH)
    z = (z * pool_scale).astype(h.dtype)
    return jnp.concatenate([o, z], axis=-1) @ w_out

def causal_diff_attention(q, k, v, lam):
    B, L, H, _, dh = q.shape
    nb = -(-L // Q_BLOCK)
    Lp = nb * Q_BLOCK
    pad = Lp - L
    q = jnp.pad(q, ((0, 0), (0, pad), (0, 0), (0, 0), (0, 0)))
    k = jnp.pad(k, ((0, 0), (0, pad), (0, 0), (0, 0), (0, 0)))
    v = jnp.pad(v, ((0, 0), (0, pad), (0, 0), (0, 0)))
    qb = jnp.moveaxis(q.reshape(B, nb, Q_BLOCK, H, 2, dh), 1, 0)
    kpos = jnp.arange(Lp)
    scale = DIFF_HEAD ** -0.5

    def one_block(args):
        qblk, start = args
        s = jnp.einsum('bqhcd,bkhcd->bhcqk', qblk, k).astype(jnp.float32) * scale
        qpos = start + jnp.arange(Q_BLOCK)
        mask = kpos[None, :] <= qpos[:, None]
        s = jnp.where(mask, s, -jnp.inf)
        p = jax.nn.softmax(s, axis=-1)
        attn = p[:, :, 0] - lam * p[:, :, 1]
        return jnp.einsum('bhqk,bkhe->bqhe', attn.astype(v.dtype), v)

    out = lax.map(one_block, (qb, jnp.arange(nb) * Q_BLOCK))
    out = jnp.moveaxis(out, 0, 1).reshape(B, Lp, H, 2 * dh)
    return out[:, :L]

def diff_attn_mixer(h, w_in, lam_vecs, subln_w, w_out, cos, sin, layer):
    B, L, _ = h.shape
    y = h @ w_in
    q, k, v = jnp.split(y, 3, axis=-1)
    q = apply_rope(q.reshape(B, L, DIFF_HEADS, 2, DIFF_HEAD), cos, sin)
    k = apply_rope(k.reshape(B, L, DIFF_HEADS, 2, DIFF_HEAD), cos, sin)
    v = v.reshape(B, L, DIFF_HEADS, 2 * DIFF_HEAD)
    lam_init = 0.8 - 0.6 * math.exp(-0.3 * layer)
    lv = lam_vecs.astype(jnp.float32)
    lam = jnp.exp(jnp.sum(lv[0] * lv[1])) - jnp.exp(jnp.sum(lv[2] * lv[3])) + lam_init
    o = causal_diff_attention(q, k, v, lam)
    o = rmsnorm(o, subln_w, SUBLN_EPS) * (1.0 - lam_init)
    return o.reshape(B, L, D_MODEL).astype(h.dtype) @ w_out

def sq_relu_mlp(h, w1, w2):
    return jnp.square(jax.nn.relu(h @ w1)) @ w2

def first_inputs(seed: int = 0) -> dict:
    key = jax.random.key(seed)
    ks = jax.random.split(key, 24)
    nrm = lambda i, shape, s: jax.random.normal(ks[i], shape, jnp.float32) * s
    RW = RWKV_WIDTH
    return {
        'x': nrm(0, (BATCH, SEQ, D_MODEL), 1.0),
        'meta': nrm(1, (N_META, D_MODEL), 1.0),
        'norm_g': 1.0 + nrm(2, (DEPTH, 4, D_MODEL), 0.1),
        'mlp_w1': nrm(3, (DEPTH, D_MODEL, D_FF), D_MODEL ** -0.5),
        'mlp_w2': nrm(4, (DEPTH, D_FF, D_MODEL), D_FF ** -0.5),
        'ev_w_in': nrm(5, (N_EVEN, D_MODEL, EVEN_IN), D_MODEL ** -0.5),
        'ev_mu': jax.random.uniform(ks[6], (N_EVEN, SHIFT_WIDTH), jnp.float32),
        'ev_w0': jax.random.uniform(ks[7], (N_EVEN, RW), jnp.float32, -4.0, 1.0),
        'ev_w_up': nrm(8, (N_EVEN, DECAY_RANK, RW), 0.5 * DECAY_RANK ** -0.5),
        'ev_a0': nrm(9, (N_EVEN, RW), 0.1),
        'ev_a_up': nrm(10, (N_EVEN, ICLR_RANK, RW), ICLR_RANK ** -0.5),
        'ev_g_up': nrm(11, (N_EVEN, GATE_RANK, RW), GATE_RANK ** -0.5),
        'ev_k_k': 0.85 + nrm(12, (N_EVEN, RW), 0.05),
        'ev_k_a': 1.0 + nrm(13, (N_EVEN, RW), 0.05),
        'ev_r_k': nrm(14, (N_EVEN, RWKV_HEADS, RWKV_HEAD), 0.1),
        'ev_ln_w': 1.0 + nrm(15, (N_EVEN, RW), 0.1),
        'ev_ln_b': nrm(16, (N_EVEN, RW), 0.02),
        'ev_pool_w': nrm(17, (N_EVEN, POOL_GROUPS, POOL_GROUP_W, POOL_GROUP_W), POOL_GROUP_W ** -0.5),
        'ev_pool_scale': 1.0 + nrm(18, (N_EVEN, POOL_WIDTH), 0.1),
        'ev_w_out': nrm(19, (N_EVEN, D_MODEL, D_MODEL), D_MODEL ** -0.5),
        'od_w_in': nrm(20, (N_ODD, D_MODEL, DIFF_IN), D_MODEL ** -0.5),
        'od_lambda': nrm(21, (N_ODD, 4, DIFF_HEAD), 0.1),
        'od_subln_w': 1.0 + nrm(22, (N_ODD, 2 * DIFF_HEAD), 0.1),
        'od_w_out': nrm(23, (N_ODD, D_MODEL, D_MODEL), D_MODEL ** -0.5),
    }

def first_block(x, meta, norm_g, mlp_w1, mlp_w2, ev_w_in, ev_mu, ev_w0, ev_w_up, ev_a0,
              ev_a_up, ev_g_up, ev_k_k, ev_k_a, ev_r_k, ev_ln_w, ev_ln_b, ev_pool_w,
              ev_pool_scale, ev_w_out, od_w_in, od_lambda, od_subln_w, od_w_out):
    B = x.shape[0]
    h = jnp.concatenate([jnp.broadcast_to(meta[None].astype(x.dtype), (B, N_META, D_MODEL)), x], axis=1)
    L = h.shape[1]
    cos, sin = rope_tables(L)
    for i in range(DEPTH):
        g = norm_g[i]
        j = i // 2
        hn = rmsnorm(h, g[0])
        if i % 2 == 0:
            m = rwkv_pool_mixer(hn, ev_w_in[j], ev_mu[j], ev_w0[j], ev_w_up[j], ev_a0[j],
                                ev_a_up[j], ev_g_up[j], ev_k_k[j], ev_k_a[j], ev_r_k[j],
                                ev_ln_w[j], ev_ln_b[j], ev_pool_w[j], ev_pool_scale[j], ev_w_out[j])
        else:
            m = diff_attn_mixer(hn, od_w_in[j], od_lambda[j], od_subln_w[j], od_w_out[j], cos, sin, i)
        h = h + rmsnorm(m, g[1])
        f = sq_relu_mlp(rmsnorm(h, g[2]), mlp_w1[i], mlp_w2[i])
        h = h + rmsnorm(f, g[3])
    return h[:, N_META:]


DEPTH_2 = 1

CHUNK = 64
N_MEM = 256
EPS = 1e-6

SSD_HEADS = 16
SSD_HEAD_DIM = 64
SSD_D_INNER = SSD_HEADS * SSD_HEAD_DIM
SSD_GROUPS = 4
SSD_STATE = 128
SSD_CONV = 4
SSD_XBC = SSD_D_INNER + 2 * SSD_GROUPS * SSD_STATE

MLA_HEADS = 16
MLA_Q_RANK = 384
MLA_KV_RANK = 256
MLA_NOPE = 64
MLA_ROPE = 32
MLA_V = 64

MIX_WIDTH = SSD_D_INNER + MLA_HEADS * MLA_V
IN_SSD = SSD_D_INNER + SSD_XBC + SSD_HEADS
IN_MLA = MLA_Q_RANK + MLA_KV_RANK + MLA_ROPE
IN_WIDTH = IN_SSD + IN_MLA

MEM_HEADS = 4
MEM_HEAD_DIM = D_MODEL // MEM_HEADS

D_FF_2 = 2816
FFN_CONV = 3


def rmsnorm_2(x, w):
    xf = x.astype(jnp.float32)
    y = xf * lax.rsqrt(jnp.mean(xf * xf, axis=-1, keepdims=True) + EPS)
    return (y * w.astype(jnp.float32)).astype(x.dtype)

def causal_depthwise_conv(x, w, b):
    k = w.shape[0]
    y = lax.conv_general_dilated(
        x, w[:, None, :].astype(x.dtype), window_strides=(1,), padding=[(k - 1, 0)],
        dimension_numbers=("NWC", "WIO", "NWC"), feature_group_count=x.shape[-1])
    return y + b.astype(x.dtype)

def segsum_exp(a_cum):
    l = a_cum.shape[-1]
    diff = a_cum[..., :, None] - a_cum[..., None, :]
    mask = jnp.tril(jnp.ones((l, l), dtype=bool))
    return jnp.where(mask, jnp.exp(jnp.where(mask, diff, 0.0)), 0.0)

def rope_cos_sin(positions, dim):
    inv_freq = 1.0 / (ROPE_THETA ** (jnp.arange(0, dim, 2, dtype=jnp.float32) / dim))
    ang = positions.astype(jnp.float32)[..., None] * inv_freq
    return jnp.cos(ang), jnp.sin(ang)

def apply_rope_2(t, cos, sin):
    t1, t2 = jnp.split(t.astype(jnp.float32), 2, axis=-1)
    return jnp.concatenate([t1 * cos - t2 * sin, t1 * sin + t2 * cos], axis=-1).astype(t.dtype)

def ssd_mixer(u, conv_w, conv_b, dt_bias, a_log, d_skip, norm_w):
    b, s, _ = u.shape
    nc = s // CHUNK
    e = SSD_HEADS // SSD_GROUPS
    z, xbc, dt = jnp.split(u, [SSD_D_INNER, SSD_D_INNER + SSD_XBC], axis=-1)
    xbc = jax.nn.silu(causal_depthwise_conv(xbc, conv_w, conv_b))
    xs, bm, cm = jnp.split(xbc, [SSD_D_INNER, SSD_D_INNER + SSD_GROUPS * SSD_STATE], axis=-1)
    xs = xs.reshape(b, nc, CHUNK, SSD_GROUPS, e, SSD_HEAD_DIM)
    bm = bm.reshape(b, nc, CHUNK, SSD_GROUPS, SSD_STATE)
    cm = cm.reshape(b, nc, CHUNK, SSD_GROUPS, SSD_STATE)
    dt = jax.nn.softplus(dt.astype(jnp.float32) + dt_bias.astype(jnp.float32))
    a = -jnp.exp(a_log.astype(jnp.float32))
    dt_c = dt.reshape(b, nc, CHUNK, SSD_GROUPS, e)
    a_dt = jnp.transpose(dt_c * a.reshape(SSD_GROUPS, e), (0, 3, 4, 1, 2))
    a_cum = jnp.cumsum(a_dt, axis=-1)
    x_dt = xs * dt_c[..., None]
    decay_in = segsum_exp(a_cum)
    cb = jnp.einsum("bclgn,bcsgn->bcgls", cm, bm)
    y_diag = jnp.einsum("bcgls,bgecls,bcsgep->bclgep", cb, decay_in, x_dt)
    decay_states = jnp.exp(a_cum[..., -1:] - a_cum)
    states = jnp.einsum("bclgn,bgecl,bclgep->bcgepn", bm, decay_states, x_dt)
    chunk_decay = jnp.exp(a_cum[..., -1])

    def step(h, inp):
        st, dec = inp
        return h * dec[..., None, None] + st, h

    h0 = jnp.zeros_like(states[:, 0])
    _, prev = lax.scan(step, h0, (jnp.moveaxis(states, 1, 0), jnp.moveaxis(chunk_decay, 3, 0)))
    prev = jnp.moveaxis(prev, 0, 1)
    y_off = jnp.einsum("bclgn,bcgepn,bgecl->bclgep", cm, prev, jnp.exp(a_cum))
    y = (y_diag + y_off).reshape(b, s, SSD_HEADS, SSD_HEAD_DIM)
    y = y + xs.reshape(b, s, SSD_HEADS, SSD_HEAD_DIM) * d_skip[:, None]
    y = y.reshape(b, s, SSD_D_INNER) * jax.nn.silu(z)
    y = rmsnorm_2(y.reshape(b, s, SSD_GROUPS, SSD_D_INNER // SSD_GROUPS),
                norm_w.reshape(SSD_GROUPS, SSD_D_INNER // SSD_GROUPS))
    return y.reshape(b, s, SSD_D_INNER).astype(u.dtype)

def mla_mixer(u, positions, q_norm_w, w_q_up, kv_norm_w, w_kv_up):
    b, s, _ = u.shape
    q_lat, kv_lat, k_rope = jnp.split(u, [MLA_Q_RANK, MLA_Q_RANK + MLA_KV_RANK], axis=-1)
    q = (rmsnorm_2(q_lat, q_norm_w) @ w_q_up).reshape(b, s, MLA_HEADS, MLA_NOPE + MLA_ROPE)
    q_nope, q_rope = jnp.split(q, [MLA_NOPE], axis=-1)
    kv = (rmsnorm_2(kv_lat, kv_norm_w) @ w_kv_up).reshape(b, s, MLA_HEADS, MLA_NOPE + MLA_V)
    k_nope, v = jnp.split(kv, [MLA_NOPE], axis=-1)
    cos, sin = rope_cos_sin(positions, MLA_ROPE)
    q_rope = apply_rope_2(q_rope, cos[:, :, None, :], sin[:, :, None, :])
    k_rope = apply_rope_2(k_rope, cos, sin)
    scale = (MLA_NOPE + MLA_ROPE) ** -0.5
    nb = s // Q_BLOCK
    k_chunk = jnp.arange(s) // CHUNK

    def blocks(t):
        return jnp.moveaxis(t.reshape(b, nb, Q_BLOCK, *t.shape[2:]), 1, 0)

    def attend(args):
        i, qn, qr = args
        sc = jnp.einsum("bqhd,bkhd->bhqk", qn, k_nope) + jnp.einsum("bqhr,bkr->bhqk", qr, k_rope)
        sc = sc.astype(jnp.float32) * scale
        q_chunk = (i * Q_BLOCK + jnp.arange(Q_BLOCK)) // CHUNK
        mask = k_chunk[None, :] <= q_chunk[:, None]
        sc = jnp.where(mask, sc, jnp.finfo(jnp.float32).min)
        p = jax.nn.softmax(sc, axis=-1).astype(v.dtype)
        return jnp.einsum("bhqk,bkhd->bqhd", p, v)

    o = lax.map(attend, (jnp.arange(nb), blocks(q_nope), blocks(q_rope)))
    return jnp.moveaxis(o, 0, 1).reshape(b, s, MLA_HEADS * MLA_V).astype(u.dtype)

def memory_attention(h, mem_h, wq, wk, wv, wo):
    b, s, _ = h.shape
    q = (h @ wq).reshape(b, s, MEM_HEADS, MEM_HEAD_DIM)
    k = (mem_h @ wk).reshape(b, -1, MEM_HEADS, MEM_HEAD_DIM)
    v = (mem_h @ wv).reshape(b, -1, MEM_HEADS, MEM_HEAD_DIM)
    sc = jnp.einsum("bqhd,bkhd->bhqk", q, k).astype(jnp.float32) * (MEM_HEAD_DIM ** -0.5)
    p = jax.nn.softmax(sc, axis=-1).astype(v.dtype)
    o = jnp.einsum("bhqk,bkhd->bqhd", p, v).reshape(b, s, D_MODEL)
    return o @ wo

def conv_ffn(h, w_up, conv_w, conv_b, w_down):
    u = causal_depthwise_conv(h @ w_up, conv_w, conv_b)
    g, val = jnp.split(u, 2, axis=-1)
    return (jax.nn.silu(g) * val) @ w_down

def second_inputs(seed: int = 0) -> dict:
    key = jax.random.key(seed)
    ks = iter(jax.random.split(key, 40))
    f32 = jnp.float32

    def dense(shape, fan_in):
        return jax.random.normal(next(ks), shape, f32) * (fan_in ** -0.5)

    def gain(shape):
        return 1.0 + 0.02 * jax.random.normal(next(ks), shape, f32)

    def small(shape):
        return 0.01 * jax.random.normal(next(ks), shape, f32)

    L = DEPTH_2
    x = jax.random.normal(next(ks), (BATCH, SEQ, D_MODEL), f32)
    mem = jax.random.normal(next(ks), (BATCH, N_MEM, D_MODEL), f32)
    offset = jax.random.randint(next(ks), (BATCH, 1), 0, 1024, dtype=jnp.int32)
    positions = offset + jnp.arange(SEQ, dtype=jnp.int32)[None, :]
    dt0 = jnp.exp(jax.random.uniform(next(ks), (L, SSD_HEADS), f32, np.log(1e-3), np.log(1e-1)))
    dt_bias = dt0 + jnp.log(-jnp.expm1(-dt0))
    a_log = jnp.log(jax.random.uniform(next(ks), (L, SSD_HEADS), f32, 1.0, 16.0))
    return {
        "x": x,
        "mem": mem,
        "positions": positions,
        "norm_mix_w": gain((L, D_MODEL)),
        "w_in": dense((L, D_MODEL, IN_WIDTH), D_MODEL),
        "ssd_conv_w": dense((L, SSD_CONV, SSD_XBC), SSD_CONV),
        "ssd_conv_b": small((L, SSD_XBC)),
        "ssd_dt_bias": dt_bias,
        "ssd_a_log": a_log,
        "ssd_d": 1.0 + 0.1 * jax.random.normal(next(ks), (L, SSD_HEADS), f32),
        "ssd_norm_w": gain((L, SSD_D_INNER)),
        "mla_q_norm_w": gain((L, MLA_Q_RANK)),
        "mla_w_q_up": dense((L, MLA_Q_RANK, MLA_HEADS * (MLA_NOPE + MLA_ROPE)), MLA_Q_RANK),
        "mla_kv_norm_w": gain((L, MLA_KV_RANK)),
        "mla_w_kv_up": dense((L, MLA_KV_RANK, MLA_HEADS * (MLA_NOPE + MLA_V)), MLA_KV_RANK),
        "w_out": dense((L, MIX_WIDTH, D_MODEL), MIX_WIDTH),
        "norm_memx_w": gain((L, D_MODEL)),
        "norm_mem_w": gain((L, D_MODEL)),
        "w_mem_q": dense((L, D_MODEL, D_MODEL), D_MODEL),
        "w_mem_k": dense((L, D_MODEL, D_MODEL), D_MODEL),
        "w_mem_v": dense((L, D_MODEL, D_MODEL), D_MODEL),
        "w_mem_o": dense((L, D_MODEL, D_MODEL), D_MODEL),
        "norm_ffn_w": gain((L, D_MODEL)),
        "w_ffn_up": dense((L, D_MODEL, 2 * D_FF_2), D_MODEL),
        "ffn_conv_w": dense((L, FFN_CONV, 2 * D_FF_2), FFN_CONV),
        "ffn_conv_b": small((L, 2 * D_FF_2)),
        "w_ffn_down": dense((L, D_FF_2, D_MODEL), D_FF_2),
        "norm_final_w": gain((D_MODEL,)),
    }

def second_block(x, mem, positions, norm_mix_w, w_in, ssd_conv_w, ssd_conv_b, ssd_dt_bias,
              ssd_a_log, ssd_d, ssd_norm_w, mla_q_norm_w, mla_w_q_up, mla_kv_norm_w,
              mla_w_kv_up, w_out, norm_memx_w, norm_mem_w, w_mem_q, w_mem_k, w_mem_v,
              w_mem_o, norm_ffn_w, w_ffn_up, ffn_conv_w, ffn_conv_b, w_ffn_down, norm_final_w):
    for l in range(DEPTH_2):
        h = rmsnorm_2(x, norm_mix_w[l])
        u = h @ w_in[l]
        u_ssd, u_mla = jnp.split(u, [IN_SSD], axis=-1)
        y_ssd = ssd_mixer(u_ssd, ssd_conv_w[l], ssd_conv_b[l], ssd_dt_bias[l], ssd_a_log[l],
                          ssd_d[l], ssd_norm_w[l])
        y_mla = mla_mixer(u_mla, positions, mla_q_norm_w[l], mla_w_q_up[l],
                          mla_kv_norm_w[l], mla_w_kv_up[l])
        x = x + jnp.concatenate([y_ssd, y_mla], axis=-1) @ w_out[l]
        x = x + memory_attention(rmsnorm_2(x, norm_memx_w[l]), rmsnorm_2(mem, norm_mem_w[l]),
                                 w_mem_q[l], w_mem_k[l], w_mem_v[l], w_mem_o[l])
        x = x + conv_ffn(rmsnorm_2(x, norm_ffn_w[l]), w_ffn_up[l], ffn_conv_w[l], ffn_conv_b[l],
                         w_ffn_down[l])
    return rmsnorm_2(x, norm_final_w)


def setup_inputs(seed=0):
    out = dict(first_inputs(seed))
    for name, value in second_inputs(seed + 1).items():
        if name != "x":
            out[name + "_2"] = value
    return out


def reference(
    x, meta, norm_g, mlp_w1, mlp_w2, ev_w_in, ev_mu, ev_w0, ev_w_up, ev_a0, ev_a_up, ev_g_up,
    ev_k_k, ev_k_a, ev_r_k, ev_ln_w, ev_ln_b, ev_pool_w, ev_pool_scale, ev_w_out, od_w_in,
    od_lambda, od_subln_w, od_w_out, mem_2, positions_2, norm_mix_w_2, w_in_2, ssd_conv_w_2,
    ssd_conv_b_2, ssd_dt_bias_2, ssd_a_log_2, ssd_d_2, ssd_norm_w_2, mla_q_norm_w_2,
    mla_w_q_up_2, mla_kv_norm_w_2, mla_w_kv_up_2, w_out_2, norm_memx_w_2, norm_mem_w_2,
    w_mem_q_2, w_mem_k_2, w_mem_v_2, w_mem_o_2, norm_ffn_w_2, w_ffn_up_2, ffn_conv_w_2,
    ffn_conv_b_2, w_ffn_down_2, norm_final_w_2,
):
    x = first_block(
        x, meta, norm_g, mlp_w1, mlp_w2, ev_w_in, ev_mu, ev_w0, ev_w_up, ev_a0, ev_a_up,
        ev_g_up, ev_k_k, ev_k_a, ev_r_k, ev_ln_w, ev_ln_b, ev_pool_w, ev_pool_scale, ev_w_out,
        od_w_in, od_lambda, od_subln_w, od_w_out,
    )
    return second_block(
        x, mem_2, positions_2, norm_mix_w_2, w_in_2, ssd_conv_w_2, ssd_conv_b_2, ssd_dt_bias_2,
        ssd_a_log_2, ssd_d_2, ssd_norm_w_2, mla_q_norm_w_2, mla_w_q_up_2, mla_kv_norm_w_2,
        mla_w_kv_up_2, w_out_2, norm_memx_w_2, norm_mem_w_2, w_mem_q_2, w_mem_k_2, w_mem_v_2,
        w_mem_o_2, norm_ffn_w_2, w_ffn_up_2, ffn_conv_w_2, ffn_conv_b_2, w_ffn_down_2,
        norm_final_w_2,
    )


_drawn_inputs = setup_inputs


def setup_inputs(seed=0):
    import zlib

    import numpy as np

    out = dict(_drawn_inputs(seed))
    spreads = {}
    factors = {'ev_w_up': 3.119,
     'ev_a0': 3.079,
     'ev_k_k': 5.25,
     'ev_ln_b': 4.228,
     'norm_mix_w_2': 5.71,
     'ssd_conv_b_2': 8.0,
     'ssd_d_2': 26.896,
     'ssd_norm_w_2': 8.0,
     'mla_q_norm_w_2': 8.0,
     'mla_kv_norm_w_2': 8.0,
     'norm_memx_w_2': 8.0,
     'norm_mem_w_2': 8.0,
     'norm_ffn_w_2': 8.0,
     'ffn_conv_b_2': 32.485,
     'norm_final_w_2': 7.943}
    for name, (base, spread) in spreads.items():
        noise = np.random.default_rng([zlib.crc32(name.encode()), seed]).standard_normal(out[name].shape)
        drawn = base * np.exp(spread * noise) if base else spread * noise
        out[name] = __import__('jax').numpy.asarray(drawn.astype(out[name].dtype))
    for name, factor in factors.items():
        out[name] = (out[name] * factor).astype(out[name].dtype)
    return out
```

```python
from contextlib import ExitStack

import numpy as np
import concourse.bass as bass
from concourse import mybir

F32 = mybir.dt.float32
I32 = mybir.dt.int32
F16 = mybir.dt.float16
ALU = mybir.AluOpType
ACT = mybir.ActivationFunctionType
AX = mybir.AxisListType.X

P = 128
D = 1024
DT = D // P
META = 16
SEQ = 512
T0 = META + SEQ
FF = 4 * D
MEM = 256
SLAB = 4096
WSCALE = 64.0
NW = 2
HALF = SLAB // 2
CH = 16
NCH = T0 // CH
PAIRS = 4
DECAY = float(np.exp(-0.5))
LAM_INIT = 0.8 - 0.6 * float(np.exp(-0.3))
NEG = -1.0e30
FF2 = 2816
FT2 = FF2 // P
SSD_CH = 128
SSD_NC = SEQ // SSD_CH
MLA_QK = 96


def slab_plan():
    plan = []

    def grid(name, kt, cols, per):
        for c in range(0, len(cols), per):
            plan.append((name, 0, kt, cols[c:c + per]))

    def deep(name, kt, mt, kper, mper):
        for m in range(0, mt, mper):
            for k in range(0, kt, kper):
                plan.append((name, k, min(kper, kt - k), [(x * P, P) for x in range(m, m + mper)]))

    tiles = lambda n: [(x * P, P) for x in range(n)]
    grid("ev_w_in", 8, tiles(18), 4)
    grid("ev_w_out", 8, tiles(8), 4)
    grid("mlp_w1_0", 8, tiles(32), 4)
    deep("mlp_w2_0", 32, 8, 16, 2)
    grid("od_w_in", 8, tiles(24), 4)
    grid("od_w_out", 8, tiles(8), 4)
    grid("mlp_w1_1", 8, tiles(32), 4)
    deep("mlp_w2_1", 32, 8, 16, 2)
    grid("w_in_2", 8, tiles(24) + [(3088 + x * P, P) for x in range(5)] + [(3072, 16, 3728, 32)], 4)
    for half in range(2):
        plan.append(("mla_w_kv_up_2", 0, 2, [(half * 1024, 1024)]))
        plan.append(("mla_w_q_up_2", 0, 3, [(half * 768, 768)]))
    deep("w_out_2", 16, 8, 16, 2)
    for n in "qkvo":
        grid(f"w_mem_{n}_2", 8, tiles(8), 4)
    grid("w_ffn_up_2", 8, [((x + h * FT2) * P, P) for j in range(0, FT2, 2) for h in (0, 1) for x in (j, j + 1)], 4)
    deep("w_ffn_down_2", 22, 8, 22, 1)
    return plan


def lay_slabs(inputs, plan):
    out = np.zeros((len(plan), P, SLAB), np.float32)
    for n, (name, k0, kt, cols) in enumerate(plan):
        if name.startswith("mlp_w"):
            w = inputs[name[:6]][int(name[7])]
        else:
            w = inputs[name][0]
        blk = w[k0 * P:(k0 + kt) * P].reshape(kt, P, -1).transpose(1, 0, 2)
        if len(cols[-1]) == 4:
            width = len(cols) * P
        else:
            width = sum(c[1] for c in cols)
        view = out[n, :, :kt * width].reshape(P, kt, width)
        at = 0
        for c in cols:
            if len(c) == 4:
                view[:, :, at:at + c[1]] = blk[:, :, c[0]:c[0] + c[1]]
                view[:, :, at + 64:at + 64 + c[3]] = blk[:, :, c[2]:c[2] + c[3]]
            else:
                view[:, :, at:at + c[1]] = blk[:, :, c[0]:c[0] + c[1]]
            at += c[1] if len(c) == 2 else P
    return out


PARAMS = [("norm_g", 64), ("ev_mu", 14), ("ev_w0", 4), ("ev_a0", 4), ("ev_k_k", 4), ("ev_k_a", 4),
          ("ev_r_k", 4), ("ev_ln_w", 4), ("ev_ln_b", 4), ("ev_pool_scale", 4), ("od_subln_w", 1),
          ("norm_mix_w_2", 8), ("ssd_conv_w_2", 64), ("ssd_conv_b_2", 16), ("ssd_norm_w_2", 8),
          ("mla_q_norm_w_2", 3), ("mla_kv_norm_w_2", 2), ("norm_memx_w_2", 8), ("norm_mem_w_2", 8),
          ("norm_ffn_w_2", 8), ("ffn_conv_w_2", 132), ("ffn_conv_b_2", 44), ("norm_final_w_2", 8),
          ("ssd_d_2", 8), ("ssd_dt_bias_2", 1), ("ssd_a_log_2", 1)]
COL = {}
_at = 0
for _n, _k in PARAMS:
    COL[_n] = _at
    _at += _k
NPAR = _at


def lay_params(inputs):
    out = np.zeros((P, NPAR), np.float32)
    for name, k in PARAMS:
        a = inputs[name]
        if name == "ssd_d_2":
            a = np.repeat(a.reshape(-1), 64)
        if name in ("ssd_dt_bias_2", "ssd_a_log_2"):
            out[:16, COL[name]] = a.reshape(-1)
        else:
            out[:, COL[name]:COL[name] + k] = a.reshape(k, P).T
    return out


def lay_small(inputs):
    out = np.zeros((P, 3, 512), np.float32)
    out[:64, 0] = inputs["ev_w_up"][0]
    out[64:, 0] = inputs["ev_a_up"][0]
    out[:, 1] = inputs["ev_g_up"][0]
    out[:, 2] = inputs["ev_pool_w"][0].transpose(1, 0, 2).reshape(P, 512)
    return out


CONST = [("ident", 128), ("ones", 128), ("bones", 128), ("stack", 64), ("mask_m", 128), ("mask4", 512),
         ("causal", 128), ("mla_mask", 128), ("ssd_mask", 512), ("triu", 128), ("rot", 128),
         ("rot96", 96), ("invcnt", 64), ("invfreq", 1)]
CC = {}
_at = 0
for _n, _k in CONST:
    CC[_n] = (_at, _k)
    _at += _k
NCONST = _at


def constants():
    c = {}
    i = np.arange(P)
    c["ident"] = np.eye(P)
    c["ones"] = np.ones((P, P))
    c["bones"] = (i[:, None] // 64 == i[None] // 64) * 1.0
    c["stack"] = (i[:, None] % 64 == np.arange(64)[None]) * 1.0
    same = i[:, None] // CH == i[None] // CH
    up = same & (i[:, None] % CH < i[None] % CH)
    upi = same & (i[:, None] % CH <= i[None] % CH)
    c["mask_m"] = up.T * 1.0
    c["mask4"] = np.concatenate([up, upi, up, upi], 1) * 1.0
    c["causal"] = np.where(i[None] > i[:, None], NEG, 0.0)
    c["mla_mask"] = np.where(i[None] // 64 > i[:, None] // 64, NEG, 0.0)
    c["ssd_mask"] = np.tile(np.where(i[:, None] > i[None], NEG, 0.0), (1, 4))
    c["triu"] = (i[:, None] <= i[None]) * 1.0

    def rot(base, half, n):
        m = np.zeros((P, n))
        for b in base:
            for j in range(half):
                m[b + half + j, b + j] = -1.0
                m[b + j, b + half + j] = 1.0
        return m
    c["rot"] = rot((0, 64), 32, 128)
    c["rot96"] = rot((64,), 16, 96)
    t = np.arange(16)
    c["invcnt"] = np.tile(np.concatenate([1.0 / np.minimum(t + 1, w) for w in (2, 4, 8, 16)])[None], (P, 1))
    inv = 1.0 / (10000.0 ** (np.arange(0, 32, 2, dtype=np.float32) / np.float32(32)))
    f = np.zeros((P, 1))
    f[64:80, 0] = inv
    f[80:96, 0] = inv
    c["invfreq"] = f
    out = np.zeros((P, NCONST), np.float32)
    for name, k in CONST:
        out[:, CC[name][0]:CC[name][0] + k] = c[name]
    return out


def rope_constants():
    inv = 10000.0 ** (-np.arange(0, 64, 2, dtype=np.float32) / np.float32(64))
    ang = (np.arange(T0, dtype=np.float32)[None] * inv.astype(np.float32)[:, None]).astype(np.float32)
    ang = np.tile(ang, (4, 1))
    return np.concatenate([np.cos(ang), np.sin(ang)], 1).astype(np.float32)


class Line:

    def __init__(self, eng, sems, own):
        self.eng, self.sems, self.own = eng, sems, own
        self.made, self.taken = {}, {}

    def put(self, ins, name):
        self.made[name] = self.made.get(name, 0) + 1
        ins.then_inc(self.sems(name), 1)

    def fin(self, ins, name):
        self.put(ins, name)
        self.eng.wait_ge(self.sems(name), self.made[name])

    def step(self, ins):
        self.fin(ins, self.own)

    def tell(self, name, k=1):
        self.made[name] = self.made.get(name, 0) + k
        self.eng.sem_inc(self.sems(name), k)

    def take(self, name, k=1):
        if k:
            self.taken[name] = self.taken.get(name, 0) + k
            self.eng.wait_ge(self.sems(name), self.taken[name])


class Build:
    def __init__(self, nc, ctx):
        self.nc, self.ctx, self._sems = nc, ctx, {}

    def sem(self, name):
        if name not in self._sems:
            self._sems[name] = self.ctx.enter_context(self.nc.semaphore(name))
        return self._sems[name]


def build(nc, slabs, xin, params, small, consts, ropes, lamv, memx, pos, out, plan):
    with ExitStack() as ctx:
        B = Build(nc, ctx)
        sem = B.sem

        def sb(name, shape, dt=F32):
            return ctx.enter_context(nc.sbuf_tensor(name, shape, dt))

        h = sb("h", [P, DT, T0])
        hn = sb("hn", [P, DT, T0])
        BIGN = 17970
        big = sb("big", [P, BIGN])
        raw_w = sb("raw_w", [P, 2, HALF])
        wsp = sb("wsp", [P, NW, 2, SLAB], F16)
        cst = sb("cst", [P, NCONST])
        par = sb("par", [P, NPAR])
        sml = sb("sml", [P, 3, 512])
        WKN = 9312
        wk = sb("wk", [P, WKN])
        tiny = sb("tiny", [P, 64])
        ps = ctx.enter_context(nc.psum_tensor("ps", [P, 8, 512], F32))

        def C(name):
            a, k = CC[name]
            return cst[:, a:a + k]

        def V(name, j=0):
            return par[:, COL[name] + j:COL[name] + j + 1]

        ident, ones, bones = C("ident"), C("ones"), C("bones")

        class Carve:
            def __init__(self, t, at, end):
                self.t, self.at, self.end = t, at, end

            def __call__(self, *shape):
                n = int(np.prod(shape))
                assert self.at + n <= self.end, (self.at, n, self.end)
                v = self.t[:, self.at:self.at + n]
                self.at += n
                if len(shape) > 1:
                    names = "abcd"[:len(shape)]
                    v = v.rearrange(f"p ({' '.join(names)}) -> p {' '.join(names)}",
                                    **{c: s for c, s in zip(names[1:], shape[1:])})
                return v

        def halves(ap, T):
            return ap.rearrange("p (a b) -> p a b", a=2) if T == T0 else ap

        def bank(b, T, rows=P):
            return ps[:rows, b:b + 2, 0:T0 // 2] if T == T0 else ps[:rows, b, 0:T]

        base = Carve(wk, 0, WKN)
        sq = base(2, T0)
        rs = base(T0)
        sc = base(2, T0)
        WK0 = base.at

        freed = {}
        rms_done = []
        units_at = []

        def acc_slot(n):
            return 2 * (n % 3)

        def acc_open(L, cnt):
            n = cnt["acc"]
            cnt["acc"] += 1
            L.take("acc_free", max(0, n - 2 - L.taken.get("acc_free", 0)))
            return acc_slot(n)

        def acc_in(L, cnt):
            n = cnt["acc"]
            cnt["acc"] += 1
            L.eng.wait_ge(sem("acc_full"), n + 1)
            return acc_slot(n)

        def acc_drain(L, cnt):
            L.take("acc_free", cnt["acc"] - L.taken.get("acc_free", 0))

        def st_drain(L, cnt):
            L.take("st_free", cnt["st"] - L.taken.get("st_free", 0))

        def st_open(L, cnt):
            st_drain(L, cnt)
            cnt["st"] += 1

        def hl(ap):
            b = ap.bitcast(F16)
            T = b.shape[-1] // 2
            return b[:, 0:T], b[:, T:2 * T]

        def split_dve(L, src, dst, name):
            hi, lo = hl(dst)
            L.step(L.eng.tensor_copy(hi, src))
            L.fin(L.eng.tensor_tensor(lo, src, hi, ALU.subtract), name)

        def mm_split(L, b, w, x, T, start, stop, rows=P):
            (wh, wl), (xh, xl) = w, hl(x)
            mm_T(L, b, wh, xh, T, start, False, rows)
            mm_T(L, b, wh, xl, T, False, False, rows)
            return mm_T(L, b, wl, xh, T, False, stop, rows)

        def split_hi(L, cnt):
            n = cnt["split"] = cnt.get("split", -1) + 1
            if n >= len(plan):
                return
            if n >= NW:
                done, count = freed[n - NW]
                L.eng.wait_ge(sem(done), count)
            for lo, hi in halves_of(n):
                q = cnt["half"] = cnt.get("half", -1) + 1
                L.eng.wait_ge(sem(f"half{q % 2}"), 16 * (q // 2 + 1))
                L.fin(L.eng.activation(wsp[:, n % NW, 0, lo:hi], raw_w[:, q % 2, 0:hi - lo], ACT.Copy,
                                       scale=WSCALE), "hi")

        def split_lo(L, cnt):
            n = cnt["split"] = cnt.get("split", -1) + 1
            if n >= len(plan):
                return
            for lo, hi in halves_of(n):
                q = cnt["half"] = cnt.get("half", -1) + 1
                L.take("hi")
                L.fin(L.eng.scalar_tensor_tensor(wsp[:, n % NW, 1, lo:hi], raw_w[:, q % 2, 0:hi - lo], WSCALE,
                                                 wsp[:, n % NW, 0, lo:hi], ALU.mult, ALU.subtract), "half_used")
            L.tell("split")

        def unscaled(L, dst, src):
            return L.eng.activation(dst, src, ACT.Copy, scale=1.0 / WSCALE)

        def slab_view(n, kt, width):
            return [wsp[:, n % NW, z, 0:kt * width].rearrange("p (k c) -> p k c", c=width) for z in range(2)]

        def mm_T(L, b, lhsT, rhs, T, start, stop, rows=P):
            if T == T0:
                for z in range(2):
                    m = L.eng.matmul(ps[:rows, b + z, 0:T0 // 2], lhsT, rhs[:, z * (T0 // 2):(z + 1) * (T0 // 2)],
                                     start=start, stop=stop)
                return m
            return L.eng.matmul(ps[:rows, b, 0:T], lhsT, rhs, start=start, stop=stop)

        def slab_in(L, cnt):
            n = cnt["slab"]
            cnt["slab"] += 1
            L.eng.wait_ge(sem("split"), n + 1)
            return n

        def gemm_grid(L, cnt, kt, nm, rhs, T, src=None, after=None, widths=None):
            for m in range(nm):
                if m % 4 == 0:
                    n = slab_in(L, cnt)
                width = min(4, nm - 4 * (m // 4)) * P
                w = slab_view(n, kt, width)
                b = acc_open(L, cnt)
                for k in range(kt):
                    if m == 0 and src:
                        L.take(src)
                    mm = mm_split(L, b, [z[:, k, (m % 4) * P:(m % 4 + 1) * P] for z in w], rhs(k), T,
                                  k == 0, k == kt - 1)
                L.put(mm, "acc_full")
                if m % 4 == 3 or m == nm - 1:
                    freed[n] = ("acc_full", L.made["acc_full"])
                if after:
                    after(m)

        def gemm_deep(L, cnt, kt, kper, mper, rhs, T, src=None):
            first = True
            for m0 in range(0, 8, mper):
                bs = [acc_open(L, cnt) for _ in range(mper)]
                for k0 in range(0, kt, kper):
                    n = slab_in(L, cnt)
                    kk = min(kper, kt - k0)
                    w = slab_view(n, kk, mper * P)
                    for j in range(mper):
                        for k in range(kk):
                            if first and j == 0 and src:
                                L.take(src)
                            mm = mm_split(L, bs[j], [z[:, k, j * P:(j + 1) * P] for z in w], rhs(k0 + k), T,
                                          k0 + k == 0, k0 + k == kt - 1)
                        if k0 + kk == kt:
                            L.put(mm, "acc_full")
                            freed[n] = ("acc_full", L.made["acc_full"])
                        elif j == mper - 1:
                            L.put(mm, "slab_mid")
                            freed[n] = ("slab_mid", L.made["slab_mid"])
                first = False

        def evac(L, cnt, T, write, rows=P):
            b = acc_in(L, cnt)
            L.fin(write(bank(b, T, rows)), "acc_free")

        def rms_act(L, cnt, src, nt, T, ready=None, each=1):
            k = cnt["rms"] = cnt.get("rms", -1) + 1
            if k:
                L.eng.wait_ge(sem("st_full"), rms_done[k - 1])
            for j in range(nt):
                if ready:
                    L.take(ready, each)
                if j >= 2:
                    L.take("sq_free")
                L.fin(L.eng.activation(sq[:, j % 2, 0:T], src(j), ACT.Square), "sq")
            root_act(L, T)

        def rms_pe(L, cnt, nt, T):
            st_open(L, cnt)
            for j in range(nt):
                L.take("sq")
                mm = mm_T(L, 6, ones, sq[:, j % 2, 0:T], T, j == 0, j == nt - 1)
                if j < nt - 2:
                    L.put(mm, "sq_free")
                if j == nt - 1:
                    L.put(mm, "st_full")
                    rms_done.append(L.made["st_full"])

        def root_act(L, T):
            L.take("var")
            L.fin(L.eng.activation(rs[:, 0:T], rs[:, 0:T], ACT.Sqrt), "root")

        def invert_dve(L, T):
            L.tell("var")
            L.take("root")
            L.step(L.eng.reciprocal(rs[:, 0:T], rs[:, 0:T]))

        def rms_dve(L, width, T, eps):
            L.take("st_full")
            L.fin(L.eng.tensor_scalar(halves(rs[:, 0:T], T), bank(6, T), 1.0 / width, eps, ALU.mult, ALU.add),
                  "st_free")
            invert_dve(L, T)

        def scale_dve(L, dst, src, nt, T, gain, tell):
            for j in range(nt):
                t = sc[:, j % 2, 0:T]
                L.step(L.eng.scalar_tensor_tensor(t, src(j), gain(j), rs[:, 0:T], ALU.mult, ALU.mult))
                split_dve(L, t, dst(j), tell)

        def add_dve(L, src, T, gain, dst, tell):
            for j in range(DT):
                t = sc[:, 0, 0:T]
                L.step(L.eng.scalar_tensor_tensor(t, src(j), gain(j), rs[:, 0:T], ALU.mult, ALU.mult))
                L.fin(L.eng.tensor_tensor(dst(j), dst(j), t, ALU.add), tell)

        h1 = lambda j: h[:, j, :]
        h2 = lambda j: h[:, j, META:T0]
        n1 = lambda j: hn[:, j, :]
        n2 = lambda j: hn[:, j, 0:SEQ]

        YW = T0 + 1
        yv = big[:, 0:18 * YW].rearrange("p (m t) -> p m t", t=YW)
        y = lambda m: yv[:, m, 1:YW]
        X = [big[:, 18 * YW + i * 4 * T0:18 * YW + (i + 1) * 4 * T0].rearrange("p (m t) -> p m t", t=T0)
             for i in range(4)]
        AR = hn.rearrange("p (q a) t -> p q a t", a=2) if hasattr(hn, "rearrange") else \
            hn[:, :, :].rearrange("p (q a) t -> p q a t", a=2)
        mo = lambda m: X[2 + m // 4][:, m % 4, :]
        Rk, Kk, Vk = yv[:, 0:4, 1:YW], yv[:, 4:8, 1:YW], yv[:, 8:12, 1:YW]

        rk_c = Carve(wk, 0, WKN)
        Ae = rk_c(2, 4, P)
        Re = rk_c(2, 4, P)
        Be = rk_c(4, P)
        Ke = rk_c(4, P)
        Ve = rk_c(4, P)
        EXPS = wk[:, 0:rk_c.at]
        G4 = rk_c(2, 4, P)
        Bt = rk_c(2, 4, P)
        Kt = rk_c(2, 4, P)
        Vc = rk_c(2, 64)
        Q8 = rk_c(2, P)
        Mb = rk_c(P)
        M2 = rk_c(2, P)
        M4 = rk_c(2, P)
        M8 = rk_c(P)
        Q1 = rk_c(P)
        Q2 = rk_c(P)
        Q4 = rk_c(P)
        Wc = rk_c(64)
        Uc = rk_c(64)
        Oc = rk_c(2, 64)
        St = rk_c(2, 4, 64)
        PC = rk_c(4, NCH)

        qkv = big[:, 0:24 * T0].rearrange("p (m t) -> p m t", t=T0)
        Vtok = big[:, 24 * T0:24 * T0 + 5 * D].rearrange("p (b c) -> p b c", c=D)
        at_c = Carve(wk, WK0, WKN)
        PW = T0
        Pc = at_c(2, 2, PW)
        aT = at_c(2, 5, P)
        stt = at_c(2, 8)
        rope1 = at_c(2, T0)
        lamt = at_c(256)
        lam = tiny[:, 0:1]
        subw = tiny[:, 1:2]
        omka = tiny[:, 4:8]

        zt = lambda m: big[:, m * SEQ:(m + 1) * SEQ]
        Ytk = big[:, 30 * SEQ:30 * SEQ + D]
        prev = big[:, 30 * SEQ + D:30 * SEQ + 2 * D].rearrange("p (g c) -> p g c", g=4)
        adT = big[0:16, 30 * SEQ + 2 * D:30 * SEQ + 2 * D + SEQ]
        ss_c = Carve(wk, WK0, WKN)
        xdt = ss_c(16, 64)
        xw = ss_c(16, 64)
        Btk = ss_c(4, P)
        Dm = ss_c(2, 4, P)
        Mx = ss_c(2, 4, P)
        cumT = ss_c(4, P)
        dtk = ss_c(4, 16)
        adk = ss_c(4, 16)
        cumk = ss_c(4, 16)
        ncum = ss_c(4, 16)
        ecum = ss_c(4, 16)
        dlast = ss_c(4, 16)
        cdec = ss_c(4, 16)
        ml_c = Carve(wk, WK0, WKN)
        qh = ml_c(2, SEQ)
        Kh = ml_c(2, SEQ)
        vT = ml_c(SEQ)
        Vh = ml_c(2, 4, 64)
        cosT = ml_c(SEQ)
        sinT = ml_c(SEQ)
        angT = ml_c(SEQ)
        Pm = ml_c(2, SEQ)
        pT = ml_c(2, 4, P)
        stm = ml_c(2, 4)
        ym = lambda j: big[:, (8 + j) * SEQ:(9 + j) * SEQ]
        memt = big[:, 16 * SEQ:20 * SEQ].rearrange("p (j t) -> p j t", t=MEM)
        kmT = big[:, 20 * SEQ:24 * SEQ].rearrange("p (j t) -> p j t", t=MEM)
        vmT = big[:, 24 * SEQ:28 * SEQ].rearrange("p (j t) -> p j t", t=MEM)
        Vm = big[:, 28 * SEQ:32 * SEQ].rearrange("p (b c) -> p b c", c=D)

        NOB = [0, 512]

        def st_prod(L, cnt, lhsT, rhs, T, src=None, rows=P):
            if src:
                L.take(src)
            st_open(L, cnt)
            L.put(mm_T(L, 6, lhsT, rhs, T, True, True, rows=rows), "st_full")

        def l1_keys(i):
            return 496, 512 + P * (i + 1)

        def halves_of(n):
            _, _, kt, cols = plan[n]
            width = len(cols) * P if len(cols[-1]) == 4 else sum(c[1] for c in cols)
            return [(lo, min(kt * width, lo + HALF)) for lo in range(0, kt * width, HALF)]

        block = ctx.enter_context(nc.Block())

        def mlp_pe(L, cnt, src, T):
            rms_pe(L, cnt, DT, T)
            gemm_grid(L, cnt, 8, 32, src, T, src="hn")
            gemm_deep(L, cnt, 32, 16, 2, lambda k: big[:, k * T:(k + 1) * T], T, src="hid")
            rms_pe(L, cnt, DT, T)

        def second_pe(L, cnt):
            pe = L.eng
            rms_pe(L, cnt, DT, SEQ)
            gemm_grid(L, cnt, 8, 30, n2, SEQ, src="hn")
            L.take("dtT", 2)
            b = acc_open(L, cnt)
            for c in range(4):
                pe.transpose(ps[:, b, c * 16:(c + 1) * 16], big[0:16, 29 * SEQ + c * P:29 * SEQ + (c + 1) * P],
                             ident[0:16, 0:16])
            for c in range(4):
                mm = pe.transpose(ps[:, b, 64 + c * 16:64 + (c + 1) * 16], adT[:, c * P:(c + 1) * P],
                                  ident[0:16, 0:16])
            L.put(mm, "acc_full")
            L.take("dtk", 2)
            b = acc_open(L, cnt)
            for c in range(4):
                pe.matmul(ps[:, b, c * 16:(c + 1) * 16], C("triu"), adk[:, c, :], start=True, stop=True)
            for c in range(4):
                pe.matmul(ps[:, b, 64 + c * 16:64 + (c + 1) * 16], ones, adk[:, c, :], start=True, stop=True)
            for c in range(4):
                mm = pe.matmul(ps[0:16, b + 1, c * P:(c + 1) * P], adk[:, c, :], C("triu"), start=True, stop=True)
            L.put(mm, "acc_full")
            L.take("xbc", 16)
            L.take("cum", 6)
            acc_drain(L, cnt)
            st_drain(L, cnt)
            for c in range(SSD_NC):
                s0 = c * P
                for q in range(2):
                    if c or q:
                        L.take("xdt")
                    for j in range(4):
                        mm = pe.transpose(ps[:, 4, j * P:(j + 1) * P], zt(8 + 4 * q + j)[:, s0:s0 + P], ident)
                    L.put(mm, "px")
                if c:
                    L.take("btk")
                for g in range(4):
                    mm = pe.transpose(ps[:, 5, g * P:(g + 1) * P], zt(16 + g)[:, s0:s0 + P], ident)
                L.put(mm, "pb")
                for g in range(4):
                    n = 4 * c + g
                    r = n % 2
                    if n >= 2:
                        L.take("mx")
                    pe.matmul(ps[:, 2 + r, 0:P], zt(16 + g)[:, s0:s0 + P], zt(20 + g)[:, s0:s0 + P],
                              start=True, stop=True)
                    pe.matmul(ps[:, r, :], ident, C("ssd_mask"), start=True, stop=False)
                    for e in range(4):
                        hd = 4 * g + e
                        mm = pe.matmul(ps[:, r, e * P:(e + 1) * P], ident[0:16, hd:hd + 1].to_broadcast([16, P]),
                                       cumT[0:16, c, :], start=False, stop=e == 3)
                    L.put(mm, "pd")
                    if g == 0:
                        pe.wait_ge(sem("xdt"), 2 * (c + 1))
                        pe.wait_ge(sem("xw"), c + 1)
                        pe.wait_ge(sem("btk"), c + 1)
                    pe.wait_ge(sem("mx"), n + 1)
                    pe.wait_ge(sem("ysum"), n) if n else None
                    for e in range(4):
                        hd = 4 * g + e
                        mm = pe.matmul(ps[:, 6, e * 64:(e + 1) * 64], Mx[:, r, e, :], xdt[:, hd, :],
                                       start=True, stop=True)
                    if c:
                        mm = pe.matmul(ps[:, 7, 0:256], zt(20 + g)[:, s0:s0 + P], prev[:, g, :],
                                       start=True, stop=True)
                    if c < SSD_NC - 1:
                        mm = pe.matmul(ps[:, 7, 256:512], Btk[:, g, :],
                                       xw[:, 4 * g:4 * g + 4, :].rearrange("p a b -> p (a b)"), start=True, stop=True)
                    L.put(mm, "py")
                pe.wait_ge(sem("ysum"), 4 * (c + 1))
                for q in range(2):
                    if q:
                        pe.wait_ge(sem("yT"), 2 * c + 1)
                    for j in range(4):
                        mm = pe.transpose(ps[:, 6, j * P:(j + 1) * P], Ytk[:, (4 * q + j) * P:(4 * q + j + 1) * P],
                                          ident)
                    L.put(mm, "pyT")
                if c < SSD_NC - 1:
                    pe.wait_ge(sem("yT"), 2 * c + 2)
            L.take("yT", 8)
            L.take("xdt")
            L.take("btk")
            L.take("mx", 2)
            for g in range(4):
                rms_pe(L, cnt, 2, SEQ)
            rms_pe(L, cnt, 3, SEQ)
            rms_pe(L, cnt, 2, SEQ)
            ups = {}
            L.take("lat", 5)

            def head_up(hd):
                if hd % 8 == 0:
                    ups["n"] = slab_in(L, cnt), slab_in(L, cnt)
                    ups["w"] = slab_view(ups["n"][0], 2, 1024), slab_view(ups["n"][1], 3, 768)
                wkv, wq = ups["w"]
                b = acc_open(L, cnt)
                for k in range(3):
                    mm = mm_split(L, b, [z[:, k, (hd % 8) * MLA_QK:(hd % 8 + 1) * MLA_QK] for z in wq],
                                  zt(24 + k), SEQ, k == 0, k == 2, MLA_QK)
                L.put(mm, "acc_full")
                b = acc_open(L, cnt)
                for k in range(2):
                    mm = mm_split(L, b, [z[:, k, (hd % 8) * P:(hd % 8 + 1) * P] for z in wkv], zt(27 + k), SEQ,
                                  k == 0, k == 1)
                L.put(mm, "acc_full")
                if hd % 8 == 7:
                    for n in ups["n"]:
                        freed[n] = ("acc_full", L.made["acc_full"])
                L.take("qh")
                st_open(L, cnt)
                L.put(pe.matmul(ps[0:MLA_QK, 5, :], C("rot96")[0:MLA_QK, :], qh[0:MLA_QK, hd % 2, :],
                                start=True, stop=True), "st_full")
                L.take("kvh")
                b = acc_open(L, cnt)
                for i in range(4):
                    mm = pe.transpose(ps[:, b, i * 64:(i + 1) * 64], vT[64:P, i * P:(i + 1) * P], ident[64:P, 64:P])
                L.put(mm, "acc_full")

            def mla_scores(n):
                hd, i = n // 4, n % 4
                if i == 0:
                    L.take("qrope")
                    L.take("vh")
                units_at.append(cnt["acc"])
                b = acc_open(L, cnt)
                k = (i + 1) * P
                pe.matmul(ps[:, b, 0:k], qh[0:MLA_QK, hd % 2, i * P:k], Kh[0:MLA_QK, hd % 2, 0:k],
                          start=True, stop=False)
                L.put(pe.matmul(ps[:, b, i * P:k], ident, C("mla_mask"), start=False, stop=True), "acc_full")

            L.take("krope")
            st_open(L, cnt)
            L.put(pe.matmul(ps[0:MLA_QK, 5, :], C("rot96")[0:MLA_QK, :], Kh[0:MLA_QK, 0, :], start=True, stop=True),
                  "st_full")
            L.take("krope", 1)
            head_up(0)
            mla_scores(0)
            for n in range(64):
                hd, i = n // 4, n % 4
                if i == 1 and hd + 1 < 16:
                    head_up(hd + 1)
                if n + 1 < 64:
                    mla_scores(n + 1)
                values_pe(L, n, i + 1, Pm, pT, [(Vh, hd)], 64 * (hd % 2))
            pe.wait_ge(sem("mT"), 2 * 64)
            L.take("mix2", 16)
            gemm_deep(L, cnt, 16, 16, 2, lambda k: zt(k), SEQ)
            rms_pe(L, cnt, DT, SEQ)
            rms_pe(L, cnt, DT, MEM)
            gemm_grid(L, cnt, 8, 8, n2, SEQ, src="hn")
            gemm_grid(L, cnt, 8, 8, lambda k: memt[:, k, :], MEM, src="memn")
            gemm_grid(L, cnt, 8, 8, lambda k: memt[:, k, :], MEM)
            L.take("qm", 24)
            for j in range(8):
                b = acc_open(L, cnt)
                for i in range(2):
                    mm = pe.transpose(ps[:, b, i * P:(i + 1) * P], vmT[:, j, i * P:(i + 1) * P], ident)
                L.put(mm, "acc_full")
            L.take("vm", 8)

            def mem_scores(n):
                hd, i = n // 4, n % 4
                units_at.append(cnt["acc"])
                b = acc_open(L, cnt)
                for k in range(2):
                    mm = pe.matmul(ps[:, b, 0:MEM], zt(2 * hd + k)[:, i * P:(i + 1) * P], kmT[:, 2 * hd + k, :],
                                   start=k == 0, stop=k == 1)
                L.put(mm, "acc_full")
            mem_scores(0)
            st_drain(L, cnt)
            for n in range(16):
                if n + 1 < 16:
                    mem_scores(n + 1)
                values_pe(L, 64 + n, 2, Pm, pT, [(Vm, 2 * (n // 4)), (Vm, 2 * (n // 4) + 1)], 0)
            pe.wait_ge(sem("mT"), 2 * 80)
            gemm_grid(L, cnt, 8, 8, n2, SEQ, src="memo")
            rms_pe(L, cnt, DT, SEQ)
            gemm_grid(L, cnt, 8, 44, n2, SEQ, src="hn")
            gemm_deep(L, cnt, FT2, FT2, 1, lambda k: zt(k), SEQ, src="hid2")
            rms_pe(L, cnt, DT, SEQ)

        def values_pe(L, n, nb, Pb, Tb, vals, row):
            pe = L.eng
            L.take("prob")
            if n >= 1:
                pe.wait_ge(sem("mT"), 2 * n)
            for b in range(nb):
                mm = pe.transpose(ps[:, 6, b * P:(b + 1) * P], Pb[:, n % 2, b * P:(b + 1) * P], ident)
            L.put(mm, "pT")
            pe.wait_ge(sem("mT"), 2 * n + 1)
            for x, (Vx, j) in enumerate(vals):
                for b in range(nb):
                    if Vx is Vh:
                        mm = pe.matmul(ps[row:row + 64, 7, 0:P], Vh[:, j % 2, b, :], Tb[:, n % 2, b, :],
                                       start=b == 0, stop=b == nb - 1)
                    else:
                        mm = pe.matmul(ps[:, 7, x * P:(x + 1) * P], Vm[:, b, j * P:(j + 1) * P], Tb[:, n % 2, b, :],
                                       start=b == 0, stop=b == nb - 1)
            L.put(mm, "pv2")

        @block.tensor
        def _(pe):
            L = Line(pe, sem, "pe_step")
            cnt = {"acc": 0, "slab": 0, "st": 0}
            pe.wait_ge(sem("in_c"), 48)
            rms_pe(L, cnt, DT, T0)
            gemm_grid(L, cnt, 8, 18, n1, T0, src="hn")
            L.take("ys", 14)
            for j in range(4):
                st_prod(L, cnt, bones, sq[:, j % 2, :], T0, src="kks")
            L.take("tg", 2)
            for j in range(4):
                b = acc_open(L, cnt)
                L.put(mm_T(L, b, sml[0:64, 0, j * P:(j + 1) * P], yv[0:64, 12, 1:YW], T0, True, True), "acc_full")
            for j in range(4):
                b = acc_open(L, cnt)
                L.put(mm_T(L, b, sml[64:P, 0, j * P:(j + 1) * P], yv[64:P, 12, 1:YW], T0, True, True), "acc_full")
            for j in range(4):
                b = acc_open(L, cnt)
                L.put(mm_T(L, b, sml[:, 1, j * P:(j + 1) * P], y(13), T0, True, True), "acc_full")
            for j in range(4):
                st_prod(L, cnt, bones, sq[:, j % 2, :], T0, src="rkr")
            for g in range(4):
                L.take("pool")
                b = acc_open(L, cnt)
                L.put(mm_T(L, b, sml[:, 2, g * P:(g + 1) * P], y(14 + g), T0, True, True), "acc_full")
            acc_drain(L, cnt)
            for c in range(NCH + 1):
                r, t0 = c % 2, c * CH
                rp = (c - 1) % 2
                if c < NCH:
                    L.take("exp")
                    if c == 0:
                        st_drain(L, cnt)
                    if c >= 1:
                        pe.wait_ge(sem("m"), 3 * c)
                    for p in range(4):
                        pe.matmul(ps[:, 0, 0:16], Ae[:, r, p, :], X[2][:, p, t0:t0 + CH], start=p == 0, stop=p == 3)
                    for p in range(4):
                        pe.matmul(ps[:, 0, 16:48], Be[:, p, :], AR[:, p, :, t0:t0 + CH], start=p == 0, stop=p == 3)
                    for p in range(4):
                        pe.matmul(ps[:, 0, 48:80], Ke[:, p, :], AR[:, p, :, t0:t0 + CH], start=p == 0, stop=p == 3)
                    for p in range(4):
                        mm = pe.matmul(ps[:, 0, 80:144], Ve[:, p, :], C("stack"), start=p == 0, stop=p == 3)
                    L.put(mm, "pm")
                    if c >= 1:
                        pe.wait_ge(sem("tok"), 2 * c)
                    for p in range(4):
                        pe.transpose(ps[:, 1, p * P:(p + 1) * P], Be[:, p, :], ident)
                    for p in range(4):
                        mm = pe.transpose(ps[:, 2, p * P:(p + 1) * P], Ke[:, p, :], ident)
                    L.put(mm, "ptok")
                if c >= 1:
                    if c >= 2:
                        L.take("S", 1)
                        pe.wait_ge(sem("wuo"), 3 * (c - 1))
                    for p in range(4):
                        pe.matmul(ps[:, 5, 0:64], Ae[:, rp, p, :], St[:, rp, p, :], start=p == 0, stop=False)
                    L.put(pe.matmul(ps[:, 5, 0:64], G4[:, rp, 2, :], Vc[:, rp, :], start=False, stop=True), "pW")
                if c < NCH:
                    pe.wait_ge(sem("m"), 3 * (c + 1))
                    if c:
                        pe.wait_ge(sem("mpow"), 3 * c)
                        pe.wait_ge(sem("q"), 3 * c)
                    pe.matmul(ps[:, 3, 0:P], G4[:, r, 0, :], Mb, start=True, stop=True)
                    L.put(pe.matmul(ps[:, 3, P:2 * P], Mb, G4[:, r, 0, :], start=True, stop=True), "pm2")
                if c >= 1:
                    pe.wait_ge(sem("wuo"), 3 * (c - 1) + 1)
                    pe.wait_ge(sem("q"), 3 * c)
                    L.put(pe.matmul(ps[:, 5, 64:128], Q8[:, rp, :], Wc, start=True, stop=True), "pU")
                if c < NCH:
                    pe.wait_ge(sem("mpow"), 3 * c + 1)
                    pe.matmul(ps[:, 3, 2 * P:3 * P], M2[:, 1, :], M2[:, 0, :], start=True, stop=True)
                    L.put(pe.matmul(ps[:, 3, 3 * P:4 * P], M2[:, 0, :], M2[:, 1, :], start=True, stop=True), "pm2")
                    L.put(pe.matmul(ps[:, 4, 0:P], M2[:, 0, :], Q1, start=True, stop=True), "pq")
                if c >= 1:
                    pe.wait_ge(sem("wuo"), 3 * (c - 1) + 2)
                    pe.wait_ge(sem("tok"), 2 * c)
                    for p in range(4):
                        pe.matmul(ps[:, 6, p * 64:(p + 1) * 64], Bt[:, rp, p, :], Uc, start=True, stop=False)
                        mm = pe.matmul(ps[:, 6, p * 64:(p + 1) * 64], Kt[:, rp, p, :], Vc[:, rp, :],
                                       start=False, stop=True)
                    L.put(mm, "pS")
                    for p in range(4):
                        pe.matmul(ps[:, 5, 128:192], Re[:, rp, p, :], St[:, rp, p, :], start=p == 0, stop=False)
                    pe.matmul(ps[:, 5, 128:192], G4[:, rp, 1, :], Uc, start=False, stop=False)
                    L.put(pe.matmul(ps[:, 5, 128:192], G4[:, rp, 3, :], Vc[:, rp, :], start=False, stop=True), "pO")
                if c < NCH:
                    pe.wait_ge(sem("mpow"), 3 * c + 2)
                    L.put(pe.matmul(ps[:, 3, 0:P], M4[:, 1, :], M4[:, 0, :], start=True, stop=True), "pm2")
                    pe.wait_ge(sem("q"), 3 * c + 1)
                    L.put(pe.matmul(ps[:, 4, P:2 * P], M4[:, 0, :], Q2, start=True, stop=True), "pq")
                if c >= 1:
                    pe.wait_ge(sem("wuo"), 3 * (c - 1) + 3)
                    if c >= 2:
                        L.take("oT", 2)
                    L.put(pe.transpose(ps[:, 7, 0:P], Oc.rearrange("p a b -> p (a b)"), ident), "pOT")
                if c < NCH:
                    pe.wait_ge(sem("mpow"), 3 * c + 3)
                    pe.wait_ge(sem("q"), 3 * c + 2)
                    L.put(pe.matmul(ps[:, 4, 2 * P:3 * P], M8, Q4, start=True, stop=True), "pq")
            L.take("S", 1)
            L.take("oT", 2)
            pe.wait_ge(sem("mpow"), 3 * NCH)
            for j in range(4):
                st_prod(L, cnt, bones, X[1][:, j, :], T0)
                st_prod(L, cnt, bones, sq[:, 0, :], T0, src="sqg")
            gemm_grid(L, cnt, 8, 8, lambda k: X[1][:, k, :] if k < 4 else X[0][:, k - 4, :], T0, src="mix")
            rms_pe(L, cnt, DT, T0)
            mlp_pe(L, cnt, n1, T0)
            rms_pe(L, cnt, DT, T0)

            def rope_after(m):
                if 1 <= m <= 16:
                    L.take("qk")
                    st_prod(L, cnt, C("rot"), qkv[:, m - 1, :], T0)
            gemm_grid(L, cnt, 8, 24, n1, T0, src="hn", after=rope_after)
            L.take("qk", 8)
            for hd in range(8):
                b = acc_open(L, cnt)
                for i in range(4):
                    pe.transpose(ps[:, b, i * P:(i + 1) * P], qkv[:, 16 + hd, META + i * P:META + (i + 1) * P], ident)
                L.put(pe.transpose(ps[0:META, b + 1, 0:P], qkv[:, 16 + hd, 0:META], ident), "acc_full")
            L.take("rope", 16)
            L.take("vtok", 16)
            st_drain(L, cnt)

            def l1_scores(n):
                hd, i = n // 4, n % 4
                q0 = META + i * P
                for c in range(2):
                    units_at.append(cnt["acc"])
                    b = acc_open(L, cnt)
                    q = qkv[c * 64:(c + 1) * 64, hd, q0:q0 + P]
                    pe.matmul(ps[:, b, 496:512], q, qkv[c * 64:(c + 1) * 64, 8 + hd, 0:META], start=True, stop=True)
                    pe.matmul(ps[:, b + 1, 0:(i + 1) * P], q, qkv[c * 64:(c + 1) * 64, 8 + hd, META:META + (i + 1) * P],
                              start=True, stop=False)
                    L.put(pe.matmul(ps[:, b + 1, i * P:(i + 1) * P], ident, C("causal"), start=False, stop=True),
                          "acc_full")

            def l1_values(n):
                hd, i = n // 4, n % 4
                L.take("attn")
                if n >= 1:
                    L.take("aT", 3)
                A = Pc[:, n % 2, 0, :]
                for b in range(i + 1):
                    pe.transpose(ps[:, 6, b * P:(b + 1) * P], A[:, META + b * P:META + (b + 1) * P], ident)
                L.put(pe.transpose(ps[0:META, 7, 0:P], A[:, 0:META], ident), "tT")
                pe.wait_ge(sem("aT"), 3 * n + 2)
                for b in range(i + 1):
                    pe.matmul(ps[:, 7, P:2 * P], Vtok[:, b, hd * P:(hd + 1) * P], aT[:, n % 2, b, :],
                              start=b == 0, stop=False)
                L.put(pe.matmul(ps[:, 7, P:2 * P], Vtok[0:META, 4, hd * P:(hd + 1) * P], aT[0:META, n % 2, 4, :],
                                start=False, stop=True), "pv")
            l1_scores(0)
            for n in range(32):
                if n + 1 < 32:
                    l1_scores(n + 1)
                l1_values(n)
            L.take("aT", 3)
            for hd in range(8):
                st_prod(L, cnt, ones, sq[:, hd % 2, 0:SEQ], SEQ, src="sqh")
            gemm_grid(L, cnt, 8, 8, n2, SEQ, src="hn2")
            rms_pe(L, cnt, DT, SEQ)
            mlp_pe(L, cnt, n2, SEQ)
            second_pe(L, cnt)

        @block.sync
        def _(sp):
            sp.dma_start(h[:, :, :], xin).then_inc(sem("in_x"), 16)
            sp.dma_start(cst[:, :], consts).then_inc(sem("in_c"), 16)
            sp.dma_start(par[:, :], params).then_inc(sem("in_c"), 16)
            sp.dma_start(sml[:, :, :], small).then_inc(sem("in_c"), 16)
            q = 0
            for n in range(len(plan)):
                for lo, hi in halves_of(n):
                    if q >= 2:
                        sp.wait_ge(sem("half_used"), q - 1)
                    sp.dma_start(raw_w[:, q % 2, 0:hi - lo], slabs[n, :, lo:hi]).then_inc(sem(f"half{q % 2}"), 16)
                    q += 1
            sp.wait_ge(sem("yo"), DT)
            for j in range(DT):
                sp.dma_start(out[:, j, :], hn[:, j, 0:SEQ]).then_inc(sem("stored"), 16)
            sp.wait_ge(sem("stored"), 16 * DT)

        def mlp_act(L, cnt, hx, nx, T):
            act = L.eng
            rms_act(L, cnt, hx, DT, T, ready="hx")
            for m in range(32):
                if m >= 2:
                    L.take("hid")
                evac(L, cnt, T, lambda v: act.activation(halves(sq[:, m % 2, 0:T], T), v, ACT.Relu,
                                                         scale=1.0 / WSCALE))
                L.tell("relu")
                if m % 4 == 3:
                    split_hi(L, cnt)
            L.take("hid", 2)
            for m in range(8):
                if m % 2 == 0:
                    split_hi(L, cnt)
                evac(L, cnt, T, lambda v: unscaled(L, halves(nx(m), T), v))
                if m % 2:
                    split_hi(L, cnt)
            rms_act(L, cnt, nx, DT, T)

        def second_act(L, cnt):
            act = L.eng
            rms_act(L, cnt, h2, DT, SEQ, ready="hx")
            for m in range(30):
                b = acc_in(L, cnt)
                if m < 8:
                    L.fin(act.activation(zt(m), ps[:, b, :], ACT.Silu, scale=1.0 / WSCALE), "acc_free")
                elif m < 29:
                    L.fin(unscaled(L, zt(m), ps[:, b, :]), "acc_free")
                else:
                    L.fin(act.activation(zt(m)[0:16, :], ps[0:16, b, :], ACT.Identity,
                                         bias=V("ssd_dt_bias_2")[0:16, :], scale=1.0 / WSCALE), "misc")
                    L.fin(unscaled(L, zt(m)[64:96, :], ps[64:96, b, :]), "acc_free")
                L.tell("win")
                if 9 <= m < 25:
                    L.take("conv")
                    L.fin(act.activation(zt(m - 1), sc[:, (m - 1) % 2, 0:SEQ], ACT.Silu), "xbc")
                if m % 4 == 3 or m == 29:
                    split_hi(L, cnt)
            L.take("absx")
            L.step(act.activation(adT, adT, ACT.Exp, scale=-1.0))
            L.fin(act.activation(adT, adT, ACT.Ln, bias=1.0), "lnx")
            L.fin(act.activation(tiny[0:16, 9:10], V("ssd_a_log_2")[0:16, :], ACT.Exp), "lnx")
            b = acc_in(L, cnt)
            L.fin(act.copy(dtk.rearrange("p a b -> p (a b)"), ps[:, b, 0:64]), "dtk")
            L.fin(act.copy(adk.rearrange("p a b -> p (a b)"), ps[:, b, 64:128]), "dtk")
            L.tell("acc_free")
            b = acc_in(L, cnt)
            flat = lambda t: t.rearrange("p a b -> p (a b)")
            L.fin(act.copy(flat(cumk), ps[:, b, 0:64]), "cum")
            L.fin(act.activation(flat(ncum), ps[:, b, 0:64], ACT.Copy, scale=-1.0), "cum")
            L.fin(act.activation(flat(ecum), ps[:, b, 0:64], ACT.Exp), "cum")
            L.fin(act.activation(flat(cdec), ps[:, b, 64:128], ACT.Exp), "cum")
            L.fin(act.copy(flat(dlast), ps[:, b, 64:128]), "cum")
            L.fin(act.copy(cumT[0:16, :, :], ps[0:16, b + 1, :].rearrange("p (a b) -> p a b", a=4)), "cum")
            L.tell("acc_free")
            L.take("dl")
            L.fin(act.activation(flat(dlast), flat(dlast), ACT.Exp), "dle")
            for c in range(SSD_NC):
                L.take("pb")
                L.fin(act.copy(Btk, ps[:, 5, :].rearrange("p (a b) -> p a b", a=4)), "btk")
                for g in range(4):
                    n = 4 * c + g
                    L.take("pd")
                    if n >= 2:
                        L.take("mx")
                    for e in range(4):
                        L.step(act.activation(Dm[:, n % 2, e, :], ps[:, n % 2, e * P:(e + 1) * P], ACT.Exp,
                                              bias=ncum[:, c, 4 * g + e:4 * g + e + 1]))
                    L.tell("dm")
            L.take("gated", 8)
            for g in range(4):
                rms_act(L, cnt, lambda j: zt(2 * g + j), 2, SEQ)
            rms_act(L, cnt, lambda j: zt(24 + j), 3, SEQ)
            rms_act(L, cnt, lambda j: zt(27 + j), 2, SEQ)
            L.take("mla")
            act.dma_start(sc[64:96, 1, 0:SEQ].bitcast(I32), pos.partition_broadcast(32)).then_inc(sem("in_p"), 16)
            act.dma_start(memt, memx).then_inc(sem("in_m"), 16)
            L.take("ang")
            L.fin(act.activation(sinT[64:96, :], sinT[64:96, :], ACT.Sin), "sincos")
            L.fin(act.activation(cosT[64:96, :], cosT[64:96, :], ACT.Sin), "sincos")
            L.take("krope", 2)

            def head_act(hd):
                b = acc_in(L, cnt)
                L.fin(unscaled(L, qh[0:MLA_QK, hd % 2, :], ps[0:MLA_QK, b, :]), "acc_free")
                L.tell("qh")
                b = acc_in(L, cnt)
                L.step(unscaled(L, Kh[0:64, hd % 2, :], ps[0:64, b, :]))
                L.fin(unscaled(L, vT[64:P, :], ps[64:P, b, :]), "acc_free")
                L.tell("kvh")
                b = acc_in(L, cnt)
                L.fin(act.copy(Vh[:, hd % 2, :, :], ps[:, b, 0:256].rearrange("p (a b) -> p a b", a=4)), "acc_free")
                L.tell("vh")
                if hd % 8 == 7:
                    split_hi(L, cnt)
                    split_hi(L, cnt)

            def unit_exp(n, keys, scale):
                L.take("mx2")
                b = acc_slot(cnt["acc"])
                cnt["acc"] += 1
                L.fin(act.activation(Pm[:, n % 2, 0:keys], ps[:, b, 0:keys], ACT.Exp, bias=stm[:, n % 2, 0:1],
                                     scale=scale, accum_out=stm[:, n % 2, 1:2]), "acc_free")
                L.tell("ex2")

            def unit_turn(n, nb, outs):
                L.take("pT")
                L.fin(act.copy(pT[:, n % 2, 0:nb, :], ps[:, 6, 0:nb * P].rearrange("p (a b) -> p a b", b=P)), "mT")
                L.take("pv2")
                for dst, src in outs[:-1]:
                    L.step(act.copy(dst, src))
                L.fin(act.copy(*outs[-1]), "mT")
            head_act(0)
            unit_exp(0, P, MLA_QK ** -0.5)
            for n in range(64):
                hd, i = n // 4, n % 4
                if i == 1 and hd + 1 < 16:
                    head_act(hd + 1)
                if n + 1 < 64:
                    unit_exp(n + 1, ((n + 1) % 4 + 1) * P, MLA_QK ** -0.5)
                row = 64 * (hd % 2)
                unit_turn(n, i + 1, [(ym(hd // 2)[row:row + 64, i * P:(i + 1) * P], ps[row:row + 64, 7, 0:P])])
            mt_act(L, cnt, 2)
            rms_act(L, cnt, h2, DT, SEQ, ready="hx")
            act.wait_ge(sem("in_m"), 16)
            rms_act(L, cnt, lambda j: memt[:, j, :], DT, MEM)
            for m in range(24):
                T = SEQ if m < 8 else MEM
                dst = zt(m) if m < 8 else kmT[:, m - 8, :] if m < 16 else vmT[:, m - 16, :]
                evac(L, cnt, T, lambda v: unscaled(L, dst, v))
                L.tell("qm")
                if m % 4 == 3:
                    split_hi(L, cnt)
            for j in range(8):
                b = acc_in(L, cnt)
                L.fin(act.copy(Vm[:, :, j * P:(j + 1) * P], ps[:, b, 0:256].rearrange("p (a b) -> p a b", a=2)),
                      "acc_free")
                L.tell("vm")
            unit_exp(64, MEM, 1.0 / 16.0)
            for n in range(64, 80):
                hd, i = (n - 64) // 4, n % 4
                if n + 1 < 80:
                    unit_exp(n + 1, MEM, 1.0 / 16.0)
                unit_turn(n, 2, [(hn[:, 2 * hd + x, i * P:(i + 1) * P], ps[:, 7, x * P:(x + 1) * P])
                                 for x in range(2)])
            mt_act(L, cnt, 4)
            rms_act(L, cnt, h2, DT, SEQ, ready="hx")
            raw = wk[:, WK0:WK0 + 4 * SEQ].rearrange("p (a b) -> p a b", a=4)
            gat = wk[:, WK0 + 8 * SEQ:WK0 + 12 * SEQ].rearrange("p (a b) -> p a b", a=4)

            def gate(m):
                if m % 4 < 2:
                    L.take("gconv")
                    L.fin(act.activation(gat[:, m % 4, :], gat[:, m % 4, :], ACT.Silu), "gsilu")
            for m in range(44):
                b = acc_in(L, cnt)
                if m >= 4:
                    L.take("rawfree")
                L.fin(unscaled(L, raw[:, m % 4, :], ps[:, b, :]), "acc_free")
                L.tell("raw")
                if m >= 1:
                    gate(m - 1)
                if m % 4 == 3:
                    split_hi(L, cnt)
            gate(43)
            mt_act(L, cnt, 1)
            rms_act(L, cnt, h2, DT, SEQ, ready="hx")

        def mt_act(L, cnt, per):
            for m in range(8):
                b = acc_in(L, cnt)
                if m >= 2:
                    L.take("mtfree")
                L.fin(unscaled(L, sq[:, m % 2, 0:SEQ], ps[:, b, :]), "acc_free")
                L.tell("mt")
                if m % per == per - 1:
                    split_hi(L, cnt)
            L.take("mtfree", 2)

        @block.scalar
        def _(act):
            L = Line(act, sem, "act_step")
            cnt = {"acc": 0}
            act.wait_ge(sem("in_x"), 16)
            act.wait_ge(sem("in_c"), 48)
            rms_act(L, cnt, h1, DT, T0)
            for n in range(NW):
                split_hi(L, cnt)
            for m in range(18):
                evac(L, cnt, T0, lambda v: unscaled(L, halves(y(m), T0), v))
                if m % 4 == 3 or m == 17:
                    split_hi(L, cnt)
            L.take("ys", 14)
            L.fin(act.activation(yv[0:64, 12, 1:YW], yv[0:64, 12, 1:YW], ACT.Tanh), "tg")
            L.fin(act.activation(y(13), y(13), ACT.Sigmoid), "tg")
            for j in range(4):
                root_act(L, T0)
            for j in range(4):
                evac(L, cnt, T0, lambda v: act.activation(halves(X[0][:, j, :], T0), v, ACT.Sigmoid,
                                                          bias=V("ev_w0", j)))
            for j in range(4):
                evac(L, cnt, T0, lambda v: act.activation(halves(X[2][:, j, :], T0), v, ACT.Sigmoid,
                                                          bias=V("ev_a0", j)))
            for j in range(4):
                evac(L, cnt, T0, lambda v: act.copy(halves(X[3][:, j, :], T0), v))
            L.tell("waG")
            L.take("cumd")
            L.fin(act.activation(X[1][:, :, :], X[0][:, :, :], ACT.Exp, scale=-DECAY), "ecum1")
            L.fin(act.activation(X[0][:, :, :], X[0][:, :, :], ACT.Exp, scale=DECAY), "ecum1")
            L.take("bk")
            for g in range(4):
                evac(L, cnt, T0, lambda v: act.activation(halves(X[0][:, g, :], T0), v, ACT.Copy,
                                                          scale=V("ev_pool_scale", g)))
            for c in range(NCH + 1):
                r = c % 2
                t0p = (c - 1) * CH
                if c < NCH:
                    L.take("ptok")
                    L.fin(act.copy(Bt[:, r, :, :], ps[:, 1, :].rearrange("p (a b) -> p a b", a=4)), "tok")
                    L.fin(act.copy(Kt[:, r, :, :], ps[:, 2, :].rearrange("p (a b) -> p a b", a=4)), "tok")
                if c >= 1:
                    L.take("pW")
                    L.fin(act.copy(Wc, ps[:, 5, 0:64]), "wuo")
                if c < NCH:
                    L.take("pm2")
                    L.fin(act.copy(M2, ps[:, 3, 0:2 * P].rearrange("p (a b) -> p a b", a=2)), "mpow")
                if c >= 1:
                    L.take("pU")
                    L.fin(act.copy(Uc, ps[:, 5, 64:128]), "wuo")
                if c < NCH:
                    L.take("pm2")
                    L.fin(act.copy(M4, ps[:, 3, 2 * P:4 * P].rearrange("p (a b) -> p a b", a=2)), "mpow")
                if c >= 1:
                    L.take("pO")
                    L.fin(act.copy(Oc, ps[:, 5, 128:192].unsqueeze(1).to_broadcast([P, 2, 64])), "wuo")
                if c < NCH:
                    L.take("pm2")
                    L.fin(act.copy(M8, ps[:, 3, 0:P]), "mpow")
                if c >= 1:
                    L.take("pOT")
                    oh = ps[:, 7, 0:P].rearrange("p (q a t) -> p q a t", q=4, a=2)
                    L.fin(act.copy(X[1][0:64, :, t0p:t0p + CH], oh[0:64, :, 0, :]), "oT")
                    L.fin(act.copy(X[1][64:P, :, t0p:t0p + CH], oh[64:P, :, 1, :]), "oT")
            for j in range(4):
                L.take("cen")
                L.fin(act.activation(sq[:, 0, :], X[1][:, j, :], ACT.Square), "sqg")
                root_act(L, T0)
            for m in range(8):
                evac(L, cnt, T0, lambda v: unscaled(L, halves(mo(m), T0), v))
                if m % 4 == 3:
                    split_hi(L, cnt)
            rms_act(L, cnt, mo, DT, T0)
            mlp_act(L, cnt, h1, n1, T0)
            rms_act(L, cnt, h1, DT, T0, ready="hx")
            act.dma_start(rope1, ropes).then_inc(sem("in_r"), 16)
            act.dma_start(lamt, lamv.rearrange("a b -> (a b)").partition_broadcast(P)).then_inc(sem("in_r"), 16)
            for m in range(24):
                b = acc_in(L, cnt)
                L.fin(unscaled(L, halves(qkv[:, m, :], T0), bank(b, T0)), "acc_free")
                L.tell("qk")
                if m % 4 == 3:
                    split_hi(L, cnt)
            for hd in range(8):
                b = acc_in(L, cnt)
                L.fin(act.copy(Vtok[:, 0:4, hd * P:(hd + 1) * P], ps[:, b, :].rearrange("p (a b) -> p a b", a=4)),
                      "vtok")
                L.fin(act.copy(Vtok[0:META, 4, hd * P:(hd + 1) * P], ps[0:META, b + 1, 0:P]), "vtok")
                L.tell("acc_free")

            L.take("lamsum")
            L.fin(act.activation(tiny[:, 10:12], tiny[:, 10:12], ACT.Exp), "lamexp")

            def l1_exp(n):
                i = n % 4
                lo, hi = l1_keys(i)
                for c in range(2):
                    L.take("mx1")
                    b = acc_slot(cnt["acc"])
                    cnt["acc"] += 1
                    flat = ps[:, b:b + 2, :].rearrange("p a b -> p (a b)")
                    L.fin(act.activation(Pc[:, n % 2, c, 0:hi - lo], flat[:, lo:hi], ACT.Exp,
                                         bias=stt[:, n % 2, c:c + 1], scale=0.125,
                                         accum_out=stt[:, n % 2, 2 + c:3 + c]), "acc_free")
                L.tell("ex1")

            def l1_turn(n):
                hd, i = n // 4, n % 4
                L.take("tT")
                L.fin(act.copy(aT[:, n % 2, 0:i + 1, :],
                               ps[:, 6, 0:(i + 1) * P].rearrange("p (a b) -> p a b", b=P)), "aT")
                L.fin(act.copy(aT[0:META, n % 2, 4, :], ps[0:META, 7, 0:P]), "aT")
                L.take("pv")
                L.fin(act.copy(hn[:, hd, i * P:(i + 1) * P], ps[:, 7, P:2 * P]), "aT")
            l1_exp(0)
            for n in range(32):
                if n + 1 < 32:
                    l1_exp(n + 1)
                l1_turn(n)
            for hd in range(8):
                L.fin(act.activation(sq[:, hd % 2, 0:SEQ], n2(hd), ACT.Square), "sqh")
                root_act(L, SEQ)
            for m in range(8):
                evac(L, cnt, SEQ, lambda v: unscaled(L, zt(m), v))
                if m % 4 == 3:
                    split_hi(L, cnt)
            rms_act(L, cnt, zt, DT, SEQ)
            mlp_act(L, cnt, h2, n2, SEQ)
            second_act(L, cnt)

        dcnt = {}

        def kk_norm(L, j):
            L.take("st_full")
            L.fin(L.eng.tensor_scalar(halves(rs, T0), bank(6, T0), 1e-24, None, ALU.max), "st_free")
            invert_dve(L, T0)
            L.step(L.eng.tensor_tensor(AR[:, j, 0, :], AR[:, j, 0, :], rs, ALU.mult))

        def mlp_dve(L, hx, nx, T, g):
            rms_dve(L, D, T, 1e-6)
            scale_dve(L, nx, hx, DT, T, lambda j: V("norm_g", g + j), "hn")
            for m in range(32):
                L.take("relu")
                L.step(L.eng.tensor_tensor(sc[:, m % 2, 0:T], sq[:, m % 2, 0:T], sq[:, m % 2, 0:T], ALU.mult))
                split_dve(L, sc[:, m % 2, 0:T], big[:, m * T:(m + 1) * T], "hid")
                if m % 4 == 3:
                    split_lo(L, dcnt)
            for n in range(8):
                split_lo(L, dcnt)
            rms_dve(L, D, T, 1e-6)
            add_dve(L, nx, T, lambda j: V("norm_g", g + 8 + j), hx, "hx")

        def mt_dve(L, per):
            for m in range(8):
                L.take("mt")
                L.fin(L.eng.tensor_tensor(h2(m), h2(m), sq[:, m % 2, 0:SEQ], ALU.add), "hx")
                L.tell("mtfree")
                if m % per == per - 1:
                    split_lo(L, dcnt)

        def conv_dve(L, dst, src, name, tile, ntile, taps, bias):
            w = lambda j: V(name, j * ntile + tile)
            last = L.eng.tensor_scalar(dst, src, w(taps - 1), V(bias, tile), ALU.mult, ALU.add)
            for d in range(1, taps):
                L.step(last)
                last = L.eng.scalar_tensor_tensor(dst[:, d:SEQ], src[:, 0:SEQ - d], w(taps - 1 - d), dst[:, d:SEQ],
                                                  ALU.mult, ALU.add)
            return last

        def second_dve(L, acc_next):
            dve = L.eng
            tt, ts, stt_ = dve.tensor_tensor, dve.tensor_scalar, dve.scalar_tensor_tensor
            rms_dve(L, D, SEQ, 1e-6)
            scale_dve(L, n2, h2, DT, SEQ, lambda j: V("norm_mix_w_2", j), "hn")
            split_lo(L, dcnt)
            split_lo(L, dcnt)
            for m in range(8, 24):
                dve.wait_ge(sem("win"), m + 1)
                if m >= 10:
                    L.take("xbc")
                L.fin(conv_dve(L, sc[:, m % 2, 0:SEQ], zt(m), "ssd_conv_w_2", m - 8, 16, 4, "ssd_conv_b_2"), "conv")
                if m % 4 == 3:
                    split_lo(L, dcnt)
            split_lo(L, dcnt)
            dve.wait_ge(sem("win"), 30)
            split_lo(L, dcnt)
            dt = zt(29)[0:16, :]
            L.step(ts(adT, dt, -1.0, None, ALU.mult))
            L.step(tt(adT, adT, dt, ALU.max))
            L.tell("absx")
            L.take("lnx", 2)
            L.fin(stt_(dt, dt, 0.0, adT, ALU.max, ALU.add), "dtT")
            L.fin(ts(adT, dt, tiny[0:16, 9:10], -1.0, ALU.mult, ALU.mult), "dtT")
            L.take("cum", 6)
            flat = lambda t: t.rearrange("p a b -> p (a b)")
            L.step(tt(flat(dlast), flat(dlast), flat(cumk), ALU.subtract))
            L.tell("dl")
            L.take("dle")
            L.take("xbc", 2)
            for c in range(SSD_NC):
                for q in range(2):
                    L.take("px")
                    L.fin(tt(xdt[:, 8 * q:8 * q + 8, :], ps[:, 4, :].rearrange("p (a b) -> p a b", a=8),
                             dtk[:, c, 8 * q:8 * q + 8].unsqueeze(2).to_broadcast([P, 8, 64]), ALU.mult), "xdt")
                L.fin(tt(xw, xdt, dlast[:, c, :].unsqueeze(2).to_broadcast([P, 16, 64]), ALU.mult), "xw")
                for g in range(4):
                    n = 4 * c + g
                    L.take("dm")
                    L.fin(tt(Mx[:, n % 2, :, :], Dm[:, n % 2, :, :],
                             ps[:, 2 + n % 2, 0:P].unsqueeze(1).to_broadcast([P, 4, P]), ALU.mult), "mx")
                    L.take("py")
                    hs = slice(4 * g, 4 * g + 4)
                    yg = Ytk[:, g * 256:(g + 1) * 256]
                    v4 = lambda t: t.rearrange("p (a b) -> p a b", a=4)
                    if c:
                        L.step(tt(v4(yg), v4(ps[:, 7, 0:256]), ecum[:, c, hs].unsqueeze(2).to_broadcast([P, 4, 64]),
                                  ALU.mult))
                        last = tt(yg, yg, ps[:, 6, 0:256], ALU.add)
                    else:
                        last = dve.tensor_copy(yg, ps[:, 6, 0:256])
                    if c < SSD_NC - 1:
                        L.step(last)
                        if c:
                            L.step(tt(v4(prev[:, g, :]), v4(prev[:, g, :]),
                                      cdec[:, c, hs].unsqueeze(2).to_broadcast([P, 4, 64]), ALU.mult))
                            last = tt(prev[:, g, :], prev[:, g, :], ps[:, 7, 256:512], ALU.add)
                        else:
                            last = dve.tensor_copy(prev[:, g, :], ps[:, 7, 256:512])
                    L.fin(last, "ysum")
                for q in range(2):
                    L.take("pyT")
                    s0 = c * P
                    for j in range(4):
                        m = 4 * q + j
                        ins = stt_(sc[:, 0, j * P:(j + 1) * P], zt(8 + m)[:, s0:s0 + P], V("ssd_d_2", m),
                                   ps[:, 6, j * P:(j + 1) * P], ALU.mult, ALU.add)
                        L.fin(ins, "yT") if j == 3 else L.step(ins)
                    for j in range(4):
                        m = 4 * q + j
                        L.step(tt(zt(m)[:, s0:s0 + P], zt(m)[:, s0:s0 + P], sc[:, 0, j * P:(j + 1) * P], ALU.mult))
                    L.tell("gated")
            for g in range(4):
                rms_dve(L, 256, SEQ, 1e-6)
                for j in range(2):
                    m = 2 * g + j
                    L.step(stt_(sc[:, 0, 0:SEQ], zt(m), V("ssd_norm_w_2", m), rs[:, 0:SEQ], ALU.mult, ALU.mult))
                    split_dve(L, sc[:, 0, 0:SEQ], zt(m), "mix2")
            rms_dve(L, 384, SEQ, 1e-6)
            for j in range(3):
                L.step(stt_(sc[:, 0, 0:SEQ], zt(24 + j), V("mla_q_norm_w_2", j), rs[:, 0:SEQ], ALU.mult, ALU.mult))
                split_dve(L, sc[:, 0, 0:SEQ], zt(24 + j), "lat")
            rms_dve(L, 256, SEQ, 1e-6)
            for j in range(2):
                L.step(stt_(sc[:, 0, 0:SEQ], zt(27 + j), V("mla_kv_norm_w_2", j), rs[:, 0:SEQ], ALU.mult, ALU.mult))
                split_dve(L, sc[:, 0, 0:SEQ], zt(27 + j), "lat")
            L.tell("mla")
            dve.wait_ge(sem("in_p"), 16)
            R = slice(64, 96)
            A, S, Co, t = angT[R, :], sinT[R, :], cosT[R, :], sc[R, 0, 0:SEQ]
            L.step(dve.tensor_copy(A, sc[R, 1, 0:SEQ].bitcast(I32)))
            L.step(ts(A, A, C("invfreq")[R, :], None, ALU.mult))
            MAGIC = 12582912.0
            PI = 3.1415925
            C1 = 6.28125
            C2 = float(np.float32(np.floor((2 * np.pi - C1) * 2 ** 22) / 2 ** 22))
            C3 = float(np.float32(2 * np.pi - C1 - C2))
            for dst, quarter in ((S, 0.0), (Co, 0.25)):
                L.step(ts(t, A, 1.0 / (2 * np.pi), quarter, ALU.mult, ALU.add))
                L.step(ts(t, t, MAGIC, None, ALU.add))
                L.step(ts(t, t, -MAGIC, None, ALU.add))
                L.step(stt_(dst, t, -C1, A, ALU.mult, ALU.add))
                L.step(stt_(dst, t, -C2, dst, ALU.mult, ALU.add))
                L.step(stt_(dst, t, -C3, dst, ALU.mult, ALU.add))
                if quarter:
                    L.step(ts(dst, dst, np.pi / 2, None, ALU.add))
                L.step(ts(dst, dst, PI, -PI, ALU.min, ALU.max))
            L.tell("ang")
            L.step(dve.memset(Kh[0:64, 0, :], 0.0))
            L.fin(dve.tensor_copy(Kh[R, 0, :], zt(29)[R, :]), "krope")
            L.take("sincos", 2)
            L.take("st_full")
            L.fin(tt(t, ps[R, 5, :], S, ALU.mult), "st_free")
            L.step(tt(Kh[R, 0, :], Kh[R, 0, :], Co, ALU.mult))
            L.step(tt(Kh[R, 0, :], Kh[R, 0, :], t, ALU.add))
            L.fin(dve.tensor_copy(Kh[R, 1, :], Kh[R, 0, :]), "krope")

            def head_dve(hd):
                L.take("st_full")
                L.fin(tt(t, ps[R, 5, :], S, ALU.mult), "st_free")
                q = qh[R, hd % 2, :]
                L.step(tt(q, q, Co, ALU.mult))
                L.fin(tt(q, q, t, ALU.add), "qrope")
                if hd % 8 == 7:
                    split_lo(L, dcnt)
                    split_lo(L, dcnt)

            def unit_max(n, keys, scale, b):
                L.step(dve.tensor_reduce(stm[:, n % 2, 2:3], ps[:, b, 0:keys], AX, ALU.max))
                L.fin(ts(stm[:, n % 2, 0:1], stm[:, n % 2, 2:3], -scale, None, ALU.mult), "mx2")

            def unit_norm(n, keys):
                L.take("ex2")
                L.step(dve.reciprocal(stm[:, n % 2, 3:4], stm[:, n % 2, 1:2]))
                L.fin(ts(Pm[:, n % 2, 0:keys], Pm[:, n % 2, 0:keys], stm[:, n % 2, 3:4], None, ALU.mult), "prob")

            sq_ = MLA_QK ** -0.5
            head_dve(0)
            unit_max(0, P, sq_, acc_next())
            for n in range(64):
                hd, i = n // 4, n % 4
                if i == 1 and hd + 1 < 16:
                    head_dve(hd + 1)
                if n + 1 < 64:
                    unit_max(n + 1, ((n + 1) % 4 + 1) * P, sq_, acc_next())
                unit_norm(n, (i + 1) * P)
            for j in range(8):
                if j == 0:
                    dve.wait_ge(sem("mT"), 2 * 64)
                L.step(dve.tensor_copy(sc[:, j % 2, 0:SEQ], ym(j)))
                split_dve(L, sc[:, j % 2, 0:SEQ], ym(j), "mix2")
            mt_dve(L, 2)
            rms_dve(L, D, SEQ, 1e-6)
            scale_dve(L, n2, h2, DT, SEQ, lambda j: V("norm_memx_w_2", j), "hn")
            dve.wait_ge(sem("in_m"), 16)
            rms_dve(L, D, MEM, 1e-6)
            scale_dve(L, lambda j: memt[:, j, :], lambda j: memt[:, j, :], DT, MEM,
                      lambda j: V("norm_mem_w_2", j), "memn")
            for n in range(6):
                split_lo(L, dcnt)
            unit_max(64, MEM, 1.0 / 16, acc_next())
            for n in range(64, 80):
                if n + 1 < 80:
                    unit_max(n + 1, MEM, 1.0 / 16, acc_next())
                unit_norm(n, MEM)
            dve.wait_ge(sem("mT"), 2 * 80)
            for j in range(8):
                L.step(dve.tensor_copy(sc[:, j % 2, 0:SEQ], n2(j)))
                split_dve(L, sc[:, j % 2, 0:SEQ], n2(j), "memo")
            mt_dve(L, 4)
            rms_dve(L, D, SEQ, 1e-6)
            scale_dve(L, n2, h2, DT, SEQ, lambda j: V("norm_ffn_w_2", j), "hn")
            raw = wk[:, WK0:WK0 + 4 * SEQ].rearrange("p (a b) -> p a b", a=4)
            gat = wk[:, WK0 + 8 * SEQ:WK0 + 12 * SEQ].rearrange("p (a b) -> p a b", a=4)
            for m in range(44):
                j = 2 * (m // 4) + m % 2
                tile = j + (FT2 if m % 4 >= 2 else 0)
                L.take("raw")
                ins = conv_dve(L, gat[:, m % 4, :], raw[:, m % 4, :], "ffn_conv_w_2", tile, 44, 3, "ffn_conv_b_2")
                if m % 4 < 2:
                    L.fin(ins, "gconv")
                else:
                    L.step(ins)
                if m < 40:
                    L.tell("rawfree")
                if m % 4 >= 2:
                    L.take("gsilu")
                    L.step(tt(gat[:, m % 4, :], gat[:, m % 4 - 2, :], gat[:, m % 4, :], ALU.mult))
                    split_dve(L, gat[:, m % 4, :], zt(j), "hid2")
                if m % 4 == 3:
                    split_lo(L, dcnt)
            mt_dve(L, 1)
            rms_dve(L, D, SEQ, 1e-6)
            for j in range(DT):
                L.fin(stt_(n2(j), h2(j), V("norm_final_w_2", j), rs[:, 0:SEQ], ALU.mult, ALU.mult), "yo")

        @block.vector
        def _(dve):
            L = Line(dve, sem, "dve_step")
            tt, ts, stt_ = dve.tensor_tensor, dve.tensor_scalar, dve.scalar_tensor_tensor
            dve.wait_ge(sem("in_x"), 16)
            dve.wait_ge(sem("in_c"), 48)
            L.step(dve.memset(tiny[:, :], 0.0))
            L.step(dve.memset(yv[:, :, 0:1], 0.0))
            L.step(ts(omka, par[:, COL["ev_k_a"]:COL["ev_k_a"] + 4], -1.0, 1.0, ALU.mult, ALU.add))
            rms_dve(L, D, T0, 1e-6)
            scale_dve(L, n1, h1, DT, T0, lambda j: V("norm_g", j), "hn")
            for n in range(NW):
                split_lo(L, dcnt)
            for m in range(18):
                dve.wait_ge(sem("acc_free"), m + 1)
                if m < 14:
                    L.step(tt(sc[:, 0, :], yv[:, m, 0:T0], y(m), ALU.subtract))
                    L.fin(stt_(y(m), sc[:, 0, :], V("ev_mu", m), y(m), ALU.mult, ALU.add), "ys")
                if m % 4 == 3 or m == 17:
                    split_lo(L, dcnt)
            L.tell("uin")
            for j in range(4):
                L.step(ts(AR[:, j, 0, :], y(4 + j), V("ev_k_k", j), None, ALU.mult))
                if j >= 2:
                    L.eng.wait_ge(sem("st_full"), 1 + j - 1)
                L.fin(tt(sq[:, j % 2, :], AR[:, j, 0, :], AR[:, j, 0, :], ALU.mult), "kks")
                if j >= 1:
                    kk_norm(L, j - 1)
            kk_norm(L, 3)
            L.take("waG")
            ch = lambda i: X[i].rearrange("p m (c t) -> p (m c) t", t=CH)
            a, b = 0, 1
            for s in (1, 2, 4, 8):
                L.step(dve.tensor_copy(ch(b)[:, :, 0:s], ch(a)[:, :, 0:s]))
                L.step(tt(ch(b)[:, :, s:CH], ch(a)[:, :, s:CH], ch(a)[:, :, 0:CH - s], ALU.add))
                a, b = b, a
            L.tell("cumd")
            A_, R_ = AR[:, :, 0, :], AR[:, :, 1, :]
            for j in range(4):
                L.step(ts(sc[:, 0, :], X[2][:, j, :], V("ev_k_a", j), omka[:, j:j + 1], ALU.mult, ALU.add))
                L.step(tt(y(4 + j), y(4 + j), sc[:, 0, :], ALU.mult))
            L.step(tt(X[2], X[2], A_, ALU.mult))
            L.take("ecum1", 2)
            L.step(tt(X[2], X[2], X[0], ALU.mult))
            L.step(tt(R_, Rk, X[1], ALU.mult))
            for j in range(4):
                L.step(ts(sc[:, 0, :], y(j), V("ev_r_k", j), None, ALU.mult))
                L.fin(tt(sq[:, j % 2, :], sc[:, 0, :], y(4 + j), ALU.mult), "rkr")
                L.take("st_full")
                L.fin(tt(halves(y(j), T0), bank(6, T0), halves(y(8 + j), T0), ALU.mult), "st_free")
            L.step(tt(Kk, Kk, X[0], ALU.mult))
            L.tell("bk")
            for p in range(4):
                ac = AR[:, p, 0, :].rearrange("p (c t) -> p c t", t=CH)
                ec = X[1][:, p, :].rearrange("p (c t) -> p c t", t=CH)
                L.step(stt_(ac[:, :, 1:CH], ac[:, :, 1:CH], -1.0, ec[:, :, 0:CH - 1], ALU.mult, ALU.mult))
                L.step(ts(ac[:, :, 0:1], ac[:, :, 0:1], -1.0, None, ALU.mult))
                L.step(dve.tensor_copy(PC[:, p, :], ec[:, :, CH - 1]))
            L.step(dve.memset(St[:, 0, :, :], 0.0))
            L.take("pool", 4)
            L.step(dve.memset(EXPS, 0.0))
            L.tell("elem")
            for c in range(NCH + 1):
                r = c % 2
                rp = (c - 1) % 2
                if c < NCH:
                    L.take("pm")
                    L.fin(tt(G4[:, r, :, :].rearrange("p g (h s) -> p g h s", s=CH),
                             ps[:, 0, 16:80].rearrange("p (g s) -> p g s", g=4).unsqueeze(2)
                             .to_broadcast([P, 4, 8, CH]),
                             C("mask4").rearrange("p (g h s) -> p g h s", g=4, s=CH), ALU.mult), "m")
                    L.fin(tt(Mb.rearrange("p (h s) -> p h s", s=CH),
                             ps[:, 0, 0:16].unsqueeze(1).to_broadcast([P, 8, CH]),
                             C("mask_m").rearrange("p (h s) -> p h s", s=CH), ALU.mult), "m")
                    L.step(tt(Q1, G4[:, r, 0, :], ident, ALU.add))
                    L.fin(dve.tensor_copy(Vc[:, r, :], ps[:, 0, 80:144]), "m")
                    L.take("pq")
                    L.fin(tt(Q2, ps[:, 4, 0:P], Q1, ALU.add), "q")
                if c >= 1:
                    L.take("pS")
                    L.step(tt(St[:, r, :, :], ps[:, 6, 0:256].rearrange("p (a b) -> p a b", a=4), St[:, rp, :, :],
                              ALU.add))
                    L.fin(tt(St[:, r, :, :], St[:, r, :, :],
                             PC[:, :, c - 1].unsqueeze(2).to_broadcast([P, 4, 64]), ALU.mult), "S")
                if c < NCH:
                    L.take("pq")
                    L.fin(tt(Q4, ps[:, 4, P:2 * P], Q2, ALU.add), "q")
                    L.take("pq")
                    L.fin(tt(Q8[:, r, :], ps[:, 4, 2 * P:3 * P], Q4, ALU.add), "q")
            L.take("oT", 2 * NCH)
            for j in range(4):
                o = X[1][:, j, :]
                L.take("st_full")
                L.fin(stt_(halves(o, T0), bank(6, T0), -1.0 / 64, halves(o, T0), ALU.mult, ALU.add), "st_free")
                L.tell("cen")
                L.take("st_full")
                L.fin(ts(halves(rs, T0), bank(6, T0), 1.0 / 64, 64e-5, ALU.mult, ALU.add), "st_free")
                invert_dve(L, T0)
                L.step(tt(o, o, rs, ALU.mult))
                L.step(ts(o, o, V("ev_ln_w", j), V("ev_ln_b", j), ALU.mult, ALU.add))
                L.step(tt(o, o, y(j), ALU.add))
                L.step(tt(sc[:, 1, :], o, X[3][:, j, :], ALU.mult))
                split_dve(L, sc[:, 1, :], o, "mix")
            for j in range(4):
                L.step(dve.tensor_copy(sc[:, 1, :], X[0][:, j, :]))
                split_dve(L, sc[:, 1, :], X[0][:, j, :], "mix")
            split_lo(L, dcnt)
            split_lo(L, dcnt)
            rms_dve(L, D, T0, 1e-6)
            add_dve(L, mo, T0, lambda j: V("norm_g", 8 + j), h1, "hx")
            mlp_dve(L, h1, n1, T0, 16)
            rms_dve(L, D, T0, 1e-6)
            scale_dve(L, n1, h1, DT, T0, lambda j: V("norm_g", 32 + j), "hn")
            dve.wait_ge(sem("in_r"), 32)
            for m in range(16):
                L.take("st_full")
                t = sc[:, 0, :]
                L.fin(tt(halves(t, T0), bank(6, T0), halves(rope1[:, 1, :], T0), ALU.mult), "st_free")
                L.step(tt(qkv[:, m, :], qkv[:, m, :], rope1[:, 0, :], ALU.mult))
                L.fin(tt(qkv[:, m, :], qkv[:, m, :], t, ALU.add), "rope")
                if m % 4 == 3:
                    split_lo(L, dcnt)
            split_lo(L, dcnt)
            split_lo(L, dcnt)
            L.step(tt(lamt[:, 0:64], lamt[:, 0:64], lamt[:, 64:128], ALU.mult))
            L.step(tt(lamt[:, 128:192], lamt[:, 128:192], lamt[:, 192:256], ALU.mult))
            L.step(dve.tensor_reduce(tiny[:, 10:11], lamt[:, 0:64], AX, ALU.add))
            L.step(dve.tensor_reduce(tiny[:, 11:12], lamt[:, 128:192], AX, ALU.add))
            L.tell("lamsum")
            L.take("lamexp")
            L.step(stt_(lam, tiny[:, 10:11], LAM_INIT, tiny[:, 11:12], ALU.add, ALU.subtract))
            L.step(ts(lam, lam, -1.0, None, ALU.mult))
            L.step(ts(subw, V("od_subln_w"), 1.0 - LAM_INIT, None, ALU.mult))

            def l1_max(n):
                lo, hi = l1_keys(n % 4)
                for c in range(2):
                    b = acc_next()
                    flat = ps[:, b:b + 2, :].rearrange("p a b -> p (a b)")
                    L.step(dve.tensor_reduce(stt[:, n % 2, 4 + c:5 + c], flat[:, lo:hi], AX, ALU.max))
                    L.fin(ts(stt[:, n % 2, c:c + 1], stt[:, n % 2, 4 + c:5 + c], -0.125, None, ALU.mult), "mx1")

            def l1_mix(n):
                i = n % 4
                w = META + (i + 1) * P
                L.take("ex1")
                s = stt[:, n % 2, :]
                L.step(dve.reciprocal(s[:, 6:8], s[:, 2:4]))
                L.step(tt(s[:, 7:8], s[:, 7:8], lam, ALU.mult))
                L.step(ts(Pc[:, n % 2, 1, 0:w], Pc[:, n % 2, 1, 0:w], s[:, 7:8], None, ALU.mult))
                L.fin(stt_(Pc[:, n % 2, 0, 0:w], Pc[:, n % 2, 0, 0:w], s[:, 6:7], Pc[:, n % 2, 1, 0:w],
                           ALU.mult, ALU.add), "attn")
            units = iter(units_at)

            def acc_next():
                k = next(units)
                dve.wait_ge(sem("acc_full"), k + 1)
                return acc_slot(k)
            l1_max(0)
            for n in range(32):
                if n + 1 < 32:
                    l1_max(n + 1)
                l1_mix(n)
            for hd in range(8):
                rms_dve(L, P, SEQ, 1e-5)
                t = sc[:, hd % 2, 0:SEQ]
                L.step(stt_(t, n2(hd), subw, rs[:, 0:SEQ], ALU.mult, ALU.mult))
                split_dve(L, t, n2(hd), "hn2")
            split_lo(L, dcnt)
            split_lo(L, dcnt)
            rms_dve(L, D, SEQ, 1e-6)
            add_dve(L, zt, SEQ, lambda j: V("norm_g", 40 + j), h2, "hx")
            mlp_dve(L, h2, n2, SEQ, 48)
            second_dve(L, acc_next)

        def wk_strided(flat, rows, half):
            v = flat[rows, half * CH:half * CH + CH]
            return bass.AP(tensor=v.tensor, offset=v.offset, ap=[list(v.ap[0]), [160, 4], [1, CH]])

        @block.gpsimd
        def _(pool):
            L = Line(pool, sem, "pool_step")
            pool.wait_ge(sem("in_c"), 48)
            L.take("uin")
            tmp = [wk[:, WK0 + i * T0:WK0 + (i + 1) * T0] for i in range(2)]
            for g in range(4):
                u = y(14 + g)
                cur = u
                for i in range(g + 1):
                    s = 1 << i
                    nxt = tmp[i % 2]
                    L.step(pool.tensor_copy(nxt[:, 0:s], cur[:, 0:s]))
                    L.step(pool.tensor_tensor(nxt[:, s:T0], cur[:, s:T0], cur[:, 0:T0 - s], ALU.add))
                    cur = nxt
                w = 2 << g
                L.step(pool.tensor_tensor(cur[:, 0:16], cur[:, 0:16], C("invcnt")[:, g * 16:(g + 1) * 16], ALU.mult))
                L.step(pool.tensor_scalar(cur[:, 16:T0], cur[:, 16:T0], 1.0 / w, None, ALU.mult))
                L.fin(pool.tensor_tensor(u, cur, u, ALU.subtract), "pool")
            L.take("elem")
            views = [(Ae, AR[:, :, 0, :]), (Re, AR[:, :, 1, :]), (Be, X[2]), (Ke, Kk), (Ve, Vk)]
            for c in range(NCH):
                t0 = c * CH
                if c >= 1:
                    L.take("ptok")
                if c >= 2:
                    L.take("pO")
                for x, (dst, src) in enumerate(views):
                    d = dst[:, c % 2, :, :] if x < 2 else dst
                    flat = d.rearrange("p q n -> p (q n)")
                    for half in range(2):
                        rows = slice(64 * half, 64 * half + 64)
                        o = wk_strided(flat, rows, half)
                        ins = pool.tensor_copy(o, src[rows, :, t0:t0 + CH])
                        if x == 4 and half == 1:
                            L.fin(ins, "exp")
                        else:
                            L.step(ins)




def kernel(**inputs):
    import concourse.bacc as bacc
    from concourse.bass_utils import run_bass_kernel_spmd

    inputs = {k: np.ascontiguousarray(v) for k, v in inputs.items()}
    plan = slab_plan()
    feat = lambda a: np.ascontiguousarray(a.T.reshape(-1, P, a.shape[0]).transpose(1, 0, 2))
    arrays = {
        "slabs": lay_slabs(inputs, plan),
        "xin": feat(np.concatenate([inputs["meta"], inputs["x"][0]], 0)),
        "params": lay_params(inputs),
        "small": lay_small(inputs),
        "consts": constants(),
        "ropes": rope_constants().reshape(P, 2, T0),
        "lamv": inputs["od_lambda"][0],
        "memx": feat(inputs["mem_2"][0]),
        "pos": inputs["positions_2"][0].astype(np.int32),
    }
    nc = bacc.Bacc("TRN2", target_bir_lowering=False, num_devices=1)
    args = [nc.dram_tensor(n, a.shape, mybir.dt.from_np(a.dtype), kind="ExternalInput").ap()
            for n, a in arrays.items()]
    out = nc.dram_tensor("out", (P, DT, SEQ), F32, kind="ExternalOutput").ap()
    build(nc, *args, out, plan)
    r = run_bass_kernel_spmd(nc, [arrays], core_ids=[0]).results[0]["out"]
    return np.ascontiguousarray(r.transpose(2, 1, 0).reshape(1, SEQ, D))
```

```python
from contextlib import ExitStack

import numpy as np
import concourse.bass as bass
from concourse import mybir

F32 = mybir.dt.float32
I32 = mybir.dt.int32
F16 = mybir.dt.float16
ALU = mybir.AluOpType
ACT = mybir.ActivationFunctionType
AX = mybir.AxisListType.X

P = 128
D = 1024
DT = D // P
META = 16
SEQ = 512
T0 = META + SEQ
FF = 4 * D
MEM = 256
SLAB = 4096
WSCALE = 64.0
NW = 2
HALF = SLAB // 2
CH = 16
NCH = T0 // CH
PAIRS = 4
DECAY = float(np.exp(-0.5))
LAM_INIT = 0.8 - 0.6 * float(np.exp(-0.3))
NEG = -1.0e30
FF2 = 2816
FT2 = FF2 // P
SSD_CH = 128
SSD_NC = SEQ // SSD_CH
MLA_QK = 96


def slab_plan():
    plan = []

    def grid(name, kt, cols, per):
        for c in range(0, len(cols), per):
            plan.append((name, 0, kt, cols[c:c + per]))

    def deep(name, kt, mt, kper, mper):
        for m in range(0, mt, mper):
            for k in range(0, kt, kper):
                plan.append((name, k, min(kper, kt - k), [(x * P, P) for x in range(m, m + mper)]))

    tiles = lambda n: [(x * P, P) for x in range(n)]
    grid("ev_w_in", 8, tiles(18), 4)
    grid("ev_w_out", 8, tiles(8), 4)
    grid("mlp_w1_0", 8, tiles(32), 4)
    deep("mlp_w2_0", 32, 8, 16, 2)
    grid("od_w_in", 8, tiles(24), 4)
    grid("od_w_out", 8, tiles(8), 4)
    grid("mlp_w1_1", 8, tiles(32), 4)
    deep("mlp_w2_1", 32, 8, 16, 2)
    grid("w_in_2", 8, tiles(24) + [(3088 + x * P, P) for x in range(5)] + [(3072, 16, 3728, 32)], 4)
    for half in range(2):
        plan.append(("mla_w_kv_up_2", 0, 2, [(half * 1024, 1024)]))
        plan.append(("mla_w_q_up_2", 0, 3, [(half * 768, 768)]))
    deep("w_out_2", 16, 8, 16, 2)
    for n in "qkvo":
        grid(f"w_mem_{n}_2", 8, tiles(8), 4)
    grid("w_ffn_up_2", 8, [((x + h * FT2) * P, P) for j in range(0, FT2, 2) for h in (0, 1) for x in (j, j + 1)], 4)
    deep("w_ffn_down_2", 22, 8, 22, 1)
    return plan


def lay_slabs(inputs, plan):
    out = np.zeros((len(plan), P, SLAB), np.float32)
    for n, (name, k0, kt, cols) in enumerate(plan):
        if name.startswith("mlp_w"):
            w = inputs[name[:6]][int(name[7])]
        else:
            w = inputs[name][0]
        blk = w[k0 * P:(k0 + kt) * P].reshape(kt, P, -1).transpose(1, 0, 2)
        if len(cols[-1]) == 4:
            width = len(cols) * P
        else:
            width = sum(c[1] for c in cols)
        view = out[n, :, :kt * width].reshape(P, kt, width)
        at = 0
        for c in cols:
            if len(c) == 4:
                view[:, :, at:at + c[1]] = blk[:, :, c[0]:c[0] + c[1]]
                view[:, :, at + 64:at + 64 + c[3]] = blk[:, :, c[2]:c[2] + c[3]]
            else:
                view[:, :, at:at + c[1]] = blk[:, :, c[0]:c[0] + c[1]]
            at += c[1] if len(c) == 2 else P
    return out


PARAMS = [("norm_g", 64), ("ev_mu", 14), ("ev_w0", 4), ("ev_a0", 4), ("ev_k_k", 4), ("ev_k_a", 4),
          ("ev_r_k", 4), ("ev_ln_w", 4), ("ev_ln_b", 4), ("ev_pool_scale", 4), ("od_subln_w", 1),
          ("norm_mix_w_2", 8), ("ssd_conv_w_2", 64), ("ssd_conv_b_2", 16), ("ssd_norm_w_2", 8),
          ("mla_q_norm_w_2", 3), ("mla_kv_norm_w_2", 2), ("norm_memx_w_2", 8), ("norm_mem_w_2", 8),
          ("norm_ffn_w_2", 8), ("ffn_conv_w_2", 132), ("ffn_conv_b_2", 44), ("norm_final_w_2", 8),
          ("ssd_d_2", 8), ("ssd_dt_bias_2", 1), ("ssd_a_log_2", 1)]
COL = {}
_at = 0
for _n, _k in PARAMS:
    COL[_n] = _at
    _at += _k
NPAR = _at


def lay_params(inputs):
    out = np.zeros((P, NPAR), np.float32)
    for name, k in PARAMS:
        a = inputs[name]
        if name == "ssd_d_2":
            a = np.repeat(a.reshape(-1), 64)
        if name in ("ssd_dt_bias_2", "ssd_a_log_2"):
            out[:16, COL[name]] = a.reshape(-1)
        else:
            out[:, COL[name]:COL[name] + k] = a.reshape(k, P).T
    return out


def lay_small(inputs):
    out = np.zeros((P, 3, 512), np.float32)
    out[:64, 0] = inputs["ev_w_up"][0]
    out[64:, 0] = inputs["ev_a_up"][0]
    out[:, 1] = inputs["ev_g_up"][0]
    out[:, 2] = inputs["ev_pool_w"][0].transpose(1, 0, 2).reshape(P, 512)
    return out


CONST = [("ident", 128), ("ones", 128), ("bones", 128), ("stack", 64), ("mask_g", 256),
         ("causal", 128), ("mla_mask", 128), ("ssd_mask", 512), ("triu", 128), ("rot", 128),
         ("rot96", 96), ("invcnt", 64), ("invfreq", 1)]
CC = {}
_at = 0
for _n, _k in CONST:
    CC[_n] = (_at, _k)
    _at += _k
NCONST = _at


def constants():
    c = {}
    i = np.arange(P)
    c["ident"] = np.eye(P)
    c["ones"] = np.ones((P, P))
    c["bones"] = (i[:, None] // 64 == i[None] // 64) * 1.0
    c["stack"] = (i[:, None] % 64 == np.arange(64)[None]) * 1.0
    j = np.arange(64)
    same = (i[:, None] // CH) % 4 == j[None] // CH
    up = same & (i[:, None] % CH < j[None] % CH)
    upi = same & (i[:, None] % CH <= j[None] % CH)
    c["mask_g"] = np.concatenate([up, upi, up, upi], 1) * 1.0
    c["causal"] = np.where(i[None] > i[:, None], NEG, 0.0)
    c["mla_mask"] = np.where(i[None] // 64 > i[:, None] // 64, NEG, 0.0)
    c["ssd_mask"] = np.tile(np.where(i[:, None] > i[None], NEG, 0.0), (1, 4))
    c["triu"] = (i[:, None] <= i[None]) * 1.0

    def rot(base, half, n):
        m = np.zeros((P, n))
        for b in base:
            for j in range(half):
                m[b + half + j, b + j] = -1.0
                m[b + j, b + half + j] = 1.0
        return m
    c["rot"] = rot((0, 64), 32, 128)
    c["rot96"] = rot((64,), 16, 96)
    t = np.arange(16)
    c["invcnt"] = np.tile(np.concatenate([1.0 / np.minimum(t + 1, w) for w in (2, 4, 8, 16)])[None], (P, 1))
    inv = 1.0 / (10000.0 ** (np.arange(0, 32, 2, dtype=np.float32) / np.float32(32)))
    f = np.zeros((P, 1))
    f[64:80, 0] = inv
    f[80:96, 0] = inv
    c["invfreq"] = f
    out = np.zeros((P, NCONST), np.float32)
    for name, k in CONST:
        out[:, CC[name][0]:CC[name][0] + k] = c[name]
    return out


def rope_constants():
    inv = 10000.0 ** (-np.arange(0, 64, 2, dtype=np.float32) / np.float32(64))
    ang = (np.arange(T0, dtype=np.float32)[None] * inv.astype(np.float32)[:, None]).astype(np.float32)
    ang = np.tile(ang, (4, 1))
    return np.concatenate([np.cos(ang), np.sin(ang)], 1).astype(np.float32)


class Line:

    def __init__(self, eng, sems, own):
        self.eng, self.sems, self.own = eng, sems, own
        self.made, self.taken = {}, {}

    def put(self, ins, name):
        self.made[name] = self.made.get(name, 0) + 1
        ins.then_inc(self.sems(name), 1)

    def fin(self, ins, name):
        self.put(ins, name)
        self.eng.wait_ge(self.sems(name), self.made[name])

    def step(self, ins):
        self.fin(ins, self.own)

    def tell(self, name, k=1):
        self.made[name] = self.made.get(name, 0) + k
        self.eng.sem_inc(self.sems(name), k)

    def take(self, name, k=1):
        if k:
            self.taken[name] = self.taken.get(name, 0) + k
            self.eng.wait_ge(self.sems(name), self.taken[name])


class Build:
    def __init__(self, nc, ctx):
        self.nc, self.ctx, self._sems = nc, ctx, {}

    def sem(self, name):
        if name not in self._sems:
            self._sems[name] = self.ctx.enter_context(self.nc.semaphore(name))
        return self._sems[name]


def build(nc, slabs, xin, params, small, consts, ropes, lamv, memx, pos, out, plan):
    with ExitStack() as ctx:
        B = Build(nc, ctx)
        sem = B.sem

        def sb(name, shape, dt=F32):
            return ctx.enter_context(nc.sbuf_tensor(name, shape, dt))

        h = sb("h", [P, DT, T0])
        hn = sb("hn", [P, DT, T0])
        BIGN = 17970
        big = sb("big", [P, BIGN])
        raw_w = sb("raw_w", [P, 2, HALF])
        wsp = sb("wsp", [P, NW, 2, SLAB], F16)
        cst = sb("cst", [P, NCONST])
        par = sb("par", [P, NPAR])
        sml = sb("sml", [P, 3, 512])
        WKN = 9312
        wk = sb("wk", [P, WKN])
        tiny = sb("tiny", [P, 64])
        ps = ctx.enter_context(nc.psum_tensor("ps", [P, 8, 512], F32))

        def C(name):
            a, k = CC[name]
            return cst[:, a:a + k]

        def V(name, j=0):
            return par[:, COL[name] + j:COL[name] + j + 1]

        ident, ones, bones = C("ident"), C("ones"), C("bones")

        class Carve:
            def __init__(self, t, at, end):
                self.t, self.at, self.end = t, at, end

            def __call__(self, *shape):
                n = int(np.prod(shape))
                assert self.at + n <= self.end, (self.at, n, self.end)
                v = self.t[:, self.at:self.at + n]
                self.at += n
                if len(shape) > 1:
                    names = "abcd"[:len(shape)]
                    v = v.rearrange(f"p ({' '.join(names)}) -> p {' '.join(names)}",
                                    **{c: s for c, s in zip(names[1:], shape[1:])})
                return v

        def halves(ap, T):
            return ap.rearrange("p (a b) -> p a b", a=2) if T == T0 else ap

        def bank(b, T, rows=P):
            return ps[:rows, b:b + 2, 0:T0 // 2] if T == T0 else ps[:rows, b, 0:T]

        base = Carve(wk, 0, WKN)
        sq = base(2, T0)
        rs = base(T0)
        sc = base(2, T0)
        WK0 = base.at

        freed = {}
        rms_done = []
        sub_full = []
        units_at = []

        def acc_slot(n):
            return 2 * (n % 3)

        def acc_open(L, cnt):
            n = cnt["acc"]
            cnt["acc"] += 1
            L.take("acc_free", max(0, n - 2 - L.taken.get("acc_free", 0)))
            return acc_slot(n)

        def acc_in(L, cnt):
            n = cnt["acc"]
            cnt["acc"] += 1
            L.eng.wait_ge(sem("acc_full"), n + 1)
            return acc_slot(n)

        def acc_drain(L, cnt):
            L.take("acc_free", cnt["acc"] - L.taken.get("acc_free", 0))

        def st_drain(L, cnt):
            L.take("st_free", cnt["st"] - L.taken.get("st_free", 0))

        def st_open(L, cnt):
            st_drain(L, cnt)
            cnt["st"] += 1

        def hl(ap):
            b = ap.bitcast(F16)
            T = b.shape[-1] // 2
            return b[:, 0:T], b[:, T:2 * T]

        def split_dve(L, src, dst, name):
            hi, lo = hl(dst)
            L.step(L.eng.tensor_copy(hi, src))
            L.fin(L.eng.tensor_tensor(lo, src, hi, ALU.subtract), name)

        def mm_split(L, b, w, x, T, start, stop, rows=P):
            (wh, wl), (xh, xl) = w, hl(x)
            mm_T(L, b, wh, xh, T, start, False, rows)
            mm_T(L, b, wh, xl, T, False, False, rows)
            return mm_T(L, b, wl, xh, T, False, stop, rows)

        def split_hi(L, cnt):
            n = cnt["split"] = cnt.get("split", -1) + 1
            if n >= len(plan):
                return
            if n >= NW:
                done, count = freed[n - NW]
                L.eng.wait_ge(sem(done), count)
            for lo, hi in halves_of(n):
                q = cnt["half"] = cnt.get("half", -1) + 1
                L.eng.wait_ge(sem(f"half{q % 2}"), 16 * (q // 2 + 1))
                L.fin(L.eng.activation(wsp[:, n % NW, 0, lo:hi], raw_w[:, q % 2, 0:hi - lo], ACT.Copy,
                                       scale=WSCALE), "hi")

        def split_lo(L, cnt):
            n = cnt["split"] = cnt.get("split", -1) + 1
            if n >= len(plan):
                return
            for lo, hi in halves_of(n):
                q = cnt["half"] = cnt.get("half", -1) + 1
                L.take("hi")
                L.fin(L.eng.scalar_tensor_tensor(wsp[:, n % NW, 1, lo:hi], raw_w[:, q % 2, 0:hi - lo], WSCALE,
                                                 wsp[:, n % NW, 0, lo:hi], ALU.mult, ALU.subtract), "half_used")
            L.tell("split")

        def unscaled(L, dst, src):
            return L.eng.activation(dst, src, ACT.Copy, scale=1.0 / WSCALE)

        def slab_view(n, kt, width):
            return [wsp[:, n % NW, z, 0:kt * width].rearrange("p (k c) -> p k c", c=width) for z in range(2)]

        def mm_T(L, b, lhsT, rhs, T, start, stop, rows=P):
            if T == T0:
                for z in range(2):
                    m = L.eng.matmul(ps[:rows, b + z, 0:T0 // 2], lhsT, rhs[:, z * (T0 // 2):(z + 1) * (T0 // 2)],
                                     start=start, stop=stop)
                return m
            return L.eng.matmul(ps[:rows, b, 0:T], lhsT, rhs, start=start, stop=stop)

        def slab_in(L, cnt):
            n = cnt["slab"]
            cnt["slab"] += 1
            L.eng.wait_ge(sem("split"), n + 1)
            return n

        def gemm_grid(L, cnt, kt, nm, rhs, T, src=None, after=None, widths=None):
            for ms in ([[0, 1]] if src else [[0], [1]]) + [[m] for m in range(2, nm)]:
                if ms[0] % 4 == 0:
                    n = slab_in(L, cnt)
                width = min(4, nm - 4 * (ms[0] // 4)) * P
                w = slab_view(n, kt, width)
                bs = [acc_open(L, cnt) for _ in ms]
                for k in range(kt):
                    if ms[0] == 0 and src:
                        L.take(src)
                    for m, b in zip(ms, bs):
                        mm = mm_split(L, b, [z[:, k, (m % 4) * P:(m % 4 + 1) * P] for z in w], rhs(k), T,
                                      k == 0, k == kt - 1)
                        if k == kt - 1:
                            L.put(mm, "acc_full")
                if ms[-1] % 4 == 3 or ms[-1] == nm - 1:
                    freed[n] = ("acc_full", L.made["acc_full"])
                if after:
                    for m in ms:
                        after(m)

        def gemm_deep(L, cnt, kt, kper, mper, rhs, T, src=None):
            first = True
            for m0 in range(0, 8, mper):
                bs = [acc_open(L, cnt) for _ in range(mper)]
                for k0 in range(0, kt, kper):
                    n = slab_in(L, cnt)
                    kk = min(kper, kt - k0)
                    w = slab_view(n, kk, mper * P)
                    for j in range(mper):
                        for k in range(kk):
                            if first and j == 0 and src:
                                L.take(src)
                            mm = mm_split(L, bs[j], [z[:, k, j * P:(j + 1) * P] for z in w], rhs(k0 + k), T,
                                          k0 + k == 0, k0 + k == kt - 1)
                        if k0 + kk == kt:
                            L.put(mm, "acc_full")
                            freed[n] = ("acc_full", L.made["acc_full"])
                        elif j == mper - 1:
                            L.put(mm, "slab_mid")
                            freed[n] = ("slab_mid", L.made["slab_mid"])
                first = False

        def evac(L, cnt, T, write, rows=P):
            b = acc_in(L, cnt)
            L.fin(write(bank(b, T, rows)), "acc_free")

        def rms_act(L, cnt, src, nt, T, ready=None, each=1):
            k = cnt["rms"] = cnt.get("rms", -1) + 1
            if k:
                L.eng.wait_ge(sem("st_full"), rms_done[k - 1])
            for j in range(nt):
                if ready:
                    L.take(ready, each)
                if j >= 2:
                    L.take("sq_free")
                L.fin(L.eng.activation(sq[:, j % 2, 0:T], src(j), ACT.Square), "sq")
            root_act(L, T)

        def rms_pe(L, cnt, nt, T):
            st_open(L, cnt)
            for j in range(nt):
                L.take("sq")
                mm = mm_T(L, 6, ones, sq[:, j % 2, 0:T], T, j == 0, j == nt - 1)
                if j < nt - 2:
                    L.put(mm, "sq_free")
                if j == nt - 1:
                    L.put(mm, "st_full")
                    rms_done.append(L.made["st_full"])

        def root_act(L, T):
            L.take("var")
            L.fin(L.eng.activation(rs[:, 0:T], rs[:, 0:T], ACT.Sqrt), "root")

        def invert_dve(L, T):
            L.tell("var")
            L.take("root")
            L.step(L.eng.reciprocal(rs[:, 0:T], rs[:, 0:T]))

        def rms_dve(L, width, T, eps):
            L.take("st_full")
            L.fin(L.eng.tensor_scalar(halves(rs[:, 0:T], T), bank(6, T), 1.0 / width, eps, ALU.mult, ALU.add),
                  "st_free")
            invert_dve(L, T)

        def scale_dve(L, dst, src, nt, T, gain, tell):
            for j in range(nt):
                t = sc[:, j % 2, 0:T]
                L.step(L.eng.scalar_tensor_tensor(t, src(j), gain(j), rs[:, 0:T], ALU.mult, ALU.mult))
                split_dve(L, t, dst(j), tell)

        def add_dve(L, src, T, gain, dst, tell):
            for j in range(DT):
                t = sc[:, 0, 0:T]
                L.step(L.eng.scalar_tensor_tensor(t, src(j), gain(j), rs[:, 0:T], ALU.mult, ALU.mult))
                L.fin(L.eng.tensor_tensor(dst(j), dst(j), t, ALU.add), tell)

        h1 = lambda j: h[:, j, :]
        h2 = lambda j: h[:, j, META:T0]
        n1 = lambda j: hn[:, j, :]
        n2 = lambda j: hn[:, j, 0:SEQ]

        YW = T0 + 1
        yv = big[:, 0:18 * YW].rearrange("p (m t) -> p m t", t=YW)
        y = lambda m: yv[:, m, 1:YW]
        X = [big[:, 18 * YW + i * 4 * T0:18 * YW + (i + 1) * 4 * T0].rearrange("p (m t) -> p m t", t=T0)
             for i in range(4)]
        AR = hn[:, :, :].rearrange("p (q a) t -> p q a t", a=2)
        mo = lambda m: X[2 + m // 4][:, m % 4, :]
        Rk, Kk, Vk = yv[:, 0:4, 1:YW], yv[:, 4:8, 1:YW], yv[:, 8:12, 1:YW]

        rk_c = Carve(wk, 0, WKN)
        ARe = rk_c(2, 4, 64)
        BKe = rk_c(2, 4, P)
        Ve = rk_c(2, 4, 64)
        MT = rk_c(P)
        EXPS = wk[:, 0:rk_c.at]
        G = rk_c(2, 2, 2, 64)
        Bt = rk_c(2, 4, P)
        UV = rk_c(2, 2, 64)
        AS = rk_c(P)
        Q8 = rk_c(2, P)
        Mb = rk_c(P)
        M2 = rk_c(2, P)
        M4 = rk_c(2, P)
        M8 = rk_c(P)
        Q1 = rk_c(P)
        Q2 = rk_c(P)
        Q4 = rk_c(P)
        Wc = rk_c(64)
        St = rk_c(2, 4, 64)
        PC = rk_c(4, NCH)

        qkv = big[:, 0:24 * T0].rearrange("p (m t) -> p m t", t=T0)
        Vtok = big[:, 24 * T0:24 * T0 + 5 * D].rearrange("p (b c) -> p b c", c=D)
        at_c = Carve(wk, WK0, WKN)
        PW = T0
        Pc = at_c(2, 2, PW)
        aT = at_c(2, 5, P)
        stt = at_c(2, 8)
        rope1 = at_c(2, T0)
        lamt = at_c(256)
        lam = tiny[:, 0:1]
        subw = tiny[:, 1:2]
        omka = tiny[:, 4:8]

        zt = lambda m: big[:, m * SEQ:(m + 1) * SEQ]
        Ytk = big[:, 30 * SEQ:30 * SEQ + D]
        prev = big[:, 30 * SEQ + D:30 * SEQ + 2 * D].rearrange("p (g c) -> p g c", g=4)
        adT = big[0:16, 30 * SEQ + 2 * D:30 * SEQ + 2 * D + SEQ]
        ss_c = Carve(wk, WK0, WKN)
        xdt = ss_c(16, 64)
        xw = ss_c(16, 64)
        Btk = ss_c(4, P)
        Dm = ss_c(2, 4, P)
        Mx = ss_c(2, 4, P)
        cumT = ss_c(4, P)
        dtk = ss_c(4, 16)
        adk = ss_c(4, 16)
        cumk = ss_c(4, 16)
        ncum = ss_c(4, 16)
        ecum = ss_c(4, 16)
        dlast = ss_c(4, 16)
        cdec = ss_c(4, 16)
        ml_c = Carve(wk, WK0, WKN)
        qh = ml_c(2, SEQ)
        Kh = ml_c(2, SEQ)
        vT = ml_c(SEQ)
        Vh = ml_c(2, 4, 64)
        cosT = ml_c(SEQ)
        sinT = ml_c(SEQ)
        angT = ml_c(SEQ)
        Pm = ml_c(2, SEQ)
        pT = ml_c(2, 4, P)
        stm = ml_c(2, 4)
        ym = lambda j: big[:, (8 + j) * SEQ:(9 + j) * SEQ]
        memt = big[:, 16 * SEQ:20 * SEQ].rearrange("p (j t) -> p j t", t=MEM)
        kmT = big[:, 20 * SEQ:24 * SEQ].rearrange("p (j t) -> p j t", t=MEM)
        vmT = big[:, 24 * SEQ:28 * SEQ].rearrange("p (j t) -> p j t", t=MEM)
        Vm = big[:, 28 * SEQ:32 * SEQ].rearrange("p (b c) -> p b c", c=D)

        def st_prod(L, cnt, lhsT, rhs, T, src=None, rows=P):
            if src:
                L.take(src)
            st_open(L, cnt)
            L.put(mm_T(L, 6, lhsT, rhs, T, True, True, rows=rows), "st_full")

        def l1_keys(i):
            return 496, 512 + P * (i + 1)

        def halves_of(n):
            _, _, kt, cols = plan[n]
            width = len(cols) * P if len(cols[-1]) == 4 else sum(c[1] for c in cols)
            return [(lo, min(kt * width, lo + HALF)) for lo in range(0, kt * width, HALF)]

        block = ctx.enter_context(nc.Block())

        def mlp_pe(L, cnt, src, T):
            rms_pe(L, cnt, DT, T)
            gemm_grid(L, cnt, 8, 32, src, T, src="hn")
            gemm_deep(L, cnt, 32, 16, 2, lambda k: big[:, k * T:(k + 1) * T], T, src="hid")
            rms_pe(L, cnt, DT, T)

        def second_pe(L, cnt):
            pe = L.eng
            rms_pe(L, cnt, DT, SEQ)
            gemm_grid(L, cnt, 8, 30, n2, SEQ, src="hn")
            L.take("dtT", 2)
            b = acc_open(L, cnt)
            for c in range(4):
                pe.transpose(ps[:, b, c * 16:(c + 1) * 16], big[0:16, 29 * SEQ + c * P:29 * SEQ + (c + 1) * P],
                             ident[0:16, 0:16])
            for c in range(4):
                mm = pe.transpose(ps[:, b, 64 + c * 16:64 + (c + 1) * 16], adT[:, c * P:(c + 1) * P],
                                  ident[0:16, 0:16])
            L.put(mm, "acc_full")
            L.take("dtk", 2)
            b = acc_open(L, cnt)
            for c in range(4):
                pe.matmul(ps[:, b, c * 16:(c + 1) * 16], C("triu"), adk[:, c, :], start=True, stop=True)
            for c in range(4):
                pe.matmul(ps[:, b, 64 + c * 16:64 + (c + 1) * 16], ones, adk[:, c, :], start=True, stop=True)
            for c in range(4):
                mm = pe.matmul(ps[0:16, b + 1, c * P:(c + 1) * P], adk[:, c, :], C("triu"), start=True, stop=True)
            L.put(mm, "acc_full")
            L.take("xbc", 16)
            L.take("cum", 6)
            acc_drain(L, cnt)
            st_drain(L, cnt)
            def ssd_decays(c, g):
                s0 = c * P
                n = 4 * c + g
                r = n % 2
                if n >= 2:
                    L.take("mx")
                pe.matmul(ps[:, 2 + r, 0:P], zt(16 + g)[:, s0:s0 + P], zt(20 + g)[:, s0:s0 + P],
                          start=True, stop=True)
                pe.matmul(ps[:, r, :], ident, C("ssd_mask"), start=True, stop=False)
                for e in range(4):
                    hd = 4 * g + e
                    mm = pe.matmul(ps[:, r, e * P:(e + 1) * P], ident[0:16, hd:hd + 1].to_broadcast([16, P]),
                                   cumT[0:16, c, :], start=False, stop=e == 3)
                L.put(mm, "pd")

            for c in range(SSD_NC):
                s0 = c * P
                for q in range(2):
                    if c or q:
                        L.take("xdt")
                    for j in range(4):
                        mm = pe.transpose(ps[:, 4, j * P:(j + 1) * P], zt(8 + 4 * q + j)[:, s0:s0 + P], ident)
                    L.put(mm, "px")
                if c:
                    L.take("btk")
                for g in range(4):
                    mm = pe.transpose(ps[:, 5, g * P:(g + 1) * P], zt(16 + g)[:, s0:s0 + P], ident)
                L.put(mm, "pb")
                ssd_decays(c, 0)
                for g in range(4):
                    n = 4 * c + g
                    r = n % 2
                    if g < 3:
                        ssd_decays(c, g + 1)
                    if g == 0:
                        pe.wait_ge(sem("xdt"), 2 * (c + 1))
                        pe.wait_ge(sem("xw"), c + 1)
                        pe.wait_ge(sem("btk"), c + 1)
                    pe.wait_ge(sem("mx"), n + 1)
                    pe.wait_ge(sem("ysum"), n) if n else None
                    for e in range(4):
                        hd = 4 * g + e
                        mm = pe.matmul(ps[:, 6, e * 64:(e + 1) * 64], Mx[:, r, e, :], xdt[:, hd, :],
                                       start=True, stop=True)
                    if c:
                        mm = pe.matmul(ps[:, 7, 0:256], zt(20 + g)[:, s0:s0 + P], prev[:, g, :],
                                       start=True, stop=True)
                    if c < SSD_NC - 1:
                        mm = pe.matmul(ps[:, 7, 256:512], Btk[:, g, :],
                                       xw[:, 4 * g:4 * g + 4, :].rearrange("p a b -> p (a b)"), start=True, stop=True)
                    L.put(mm, "py")
                pe.wait_ge(sem("ysum"), 4 * (c + 1))
                for q in range(2):
                    if q:
                        pe.wait_ge(sem("yT"), 2 * c + 1)
                    for j in range(4):
                        mm = pe.transpose(ps[:, 6, j * P:(j + 1) * P], Ytk[:, (4 * q + j) * P:(4 * q + j + 1) * P],
                                          ident)
                    L.put(mm, "pyT")
                if c < SSD_NC - 1:
                    pe.wait_ge(sem("yT"), 2 * c + 2)
            L.take("yT", 8)
            L.take("xdt")
            L.take("btk")
            L.take("mx", 2)
            for g in range(4):
                rms_pe(L, cnt, 2, SEQ)
            rms_pe(L, cnt, 3, SEQ)
            rms_pe(L, cnt, 2, SEQ)
            ups = {}
            L.take("lat", 5)

            def head_up(hd):
                if hd % 8 == 0:
                    ups["n"] = slab_in(L, cnt), slab_in(L, cnt)
                    ups["w"] = slab_view(ups["n"][0], 2, 1024), slab_view(ups["n"][1], 3, 768)
                wkv, wq = ups["w"]
                b = acc_open(L, cnt)
                for k in range(3):
                    mm = mm_split(L, b, [z[:, k, (hd % 8) * MLA_QK:(hd % 8 + 1) * MLA_QK] for z in wq],
                                  zt(24 + k), SEQ, k == 0, k == 2, MLA_QK)
                L.put(mm, "acc_full")
                b = acc_open(L, cnt)
                for k in range(2):
                    mm = mm_split(L, b, [z[:, k, (hd % 8) * P:(hd % 8 + 1) * P] for z in wkv], zt(27 + k), SEQ,
                                  k == 0, k == 1)
                L.put(mm, "acc_full")
                if hd % 8 == 7:
                    for n in ups["n"]:
                        freed[n] = ("acc_full", L.made["acc_full"])
                L.take("qh")
                st_open(L, cnt)
                L.put(pe.matmul(ps[0:MLA_QK, 5, :], C("rot96")[0:MLA_QK, :], qh[0:MLA_QK, hd % 2, :],
                                start=True, stop=True), "st_full")
                L.take("kvh")
                b = acc_open(L, cnt)
                for i in range(4):
                    mm = pe.transpose(ps[:, b, i * 64:(i + 1) * 64], vT[64:P, i * P:(i + 1) * P], ident[64:P, 64:P])
                L.put(mm, "acc_full")

            def mla_scores(n):
                hd, i = n // 4, n % 4
                if i == 0:
                    L.take("qrope")
                    L.take("vh")
                units_at.append(cnt["acc"])
                b = acc_open(L, cnt)
                k = (i + 1) * P
                pe.matmul(ps[:, b, 0:k], qh[0:MLA_QK, hd % 2, i * P:k], Kh[0:MLA_QK, hd % 2, 0:k],
                          start=True, stop=False)
                L.put(pe.matmul(ps[:, b, i * P:k], ident, C("mla_mask"), start=False, stop=True), "acc_full")

            L.take("krope")
            st_open(L, cnt)
            L.put(pe.matmul(ps[0:MLA_QK, 5, :], C("rot96")[0:MLA_QK, :], Kh[0:MLA_QK, 0, :], start=True, stop=True),
                  "st_full")
            L.take("krope", 1)
            head_up(0)
            mla_scores(0)
            mla_scores(1)
            turn_pe(L, 0, 1)
            for n in range(64):
                hd, i = n // 4, n % 4
                if i == 1 and hd + 1 < 16:
                    head_up(hd + 1)
                if n + 2 < 64:
                    mla_scores(n + 2)
                values_pe(L, n, i + 1, [(Vh, hd)], 64 * (hd % 2))
                if n + 1 < 64:
                    turn_pe(L, n + 1, (n + 1) % 4 + 1)
            pe.wait_ge(sem("out_read"), 64)
            L.take("mix2", 16)
            gemm_deep(L, cnt, 16, 16, 2, lambda k: zt(k), SEQ)
            rms_pe(L, cnt, DT, SEQ)
            rms_pe(L, cnt, DT, MEM)
            gemm_grid(L, cnt, 8, 8, n2, SEQ, src="hn")
            gemm_grid(L, cnt, 8, 8, lambda k: memt[:, k, :], MEM, src="memn")
            gemm_grid(L, cnt, 8, 8, lambda k: memt[:, k, :], MEM)
            L.take("qm", 24)
            for j in range(8):
                b = acc_open(L, cnt)
                for i in range(2):
                    mm = pe.transpose(ps[:, b, i * P:(i + 1) * P], vmT[:, j, i * P:(i + 1) * P], ident)
                L.put(mm, "acc_full")
            L.take("vm", 8)

            def mem_scores(n):
                hd, i = n // 4, n % 4
                units_at.append(cnt["acc"])
                b = acc_open(L, cnt)
                for k in range(2):
                    mm = pe.matmul(ps[:, b, 0:MEM], zt(2 * hd + k)[:, i * P:(i + 1) * P], kmT[:, 2 * hd + k, :],
                                   start=k == 0, stop=k == 1)
                L.put(mm, "acc_full")
            mem_scores(0)
            mem_scores(1)
            st_drain(L, cnt)
            turn_pe(L, 64, 2)
            for n in range(16):
                if n + 2 < 16:
                    mem_scores(n + 2)
                values_pe(L, 64 + n, 2, [(Vm, 2 * (n // 4)), (Vm, 2 * (n // 4) + 1)], 0)
                if n + 1 < 16:
                    turn_pe(L, 65 + n, 2)
            pe.wait_ge(sem("out_read"), 80)
            gemm_grid(L, cnt, 8, 8, n2, SEQ, src="memo")
            rms_pe(L, cnt, DT, SEQ)
            gemm_grid(L, cnt, 8, 44, n2, SEQ, src="hn")
            gemm_deep(L, cnt, FT2, FT2, 1, lambda k: zt(k), SEQ, src="hid2")
            rms_pe(L, cnt, DT, SEQ)

        def turn_pe(L, n, nb):
            L.take("prob")
            if n >= 1:
                L.eng.wait_ge(sem("turned"), n)
            for b in range(nb):
                mm = L.eng.transpose(ps[:, 6, b * P:(b + 1) * P], Pm[:, n % 2, b * P:(b + 1) * P], ident)
            L.put(mm, "pT")

        def values_pe(L, n, nb, vals, row):
            pe, Tb = L.eng, pT
            pe.wait_ge(sem("turned"), n + 1)
            if n >= 1:
                pe.wait_ge(sem("out_read"), n)
            for x, (Vx, j) in enumerate(vals):
                for b in range(nb):
                    if Vx is Vh:
                        mm = pe.matmul(ps[row:row + 64, 7, 0:P], Vh[:, j % 2, b, :], Tb[:, n % 2, b, :],
                                       start=b == 0, stop=b == nb - 1)
                    else:
                        mm = pe.matmul(ps[:, 7, x * P:(x + 1) * P], Vm[:, b, j * P:(j + 1) * P], Tb[:, n % 2, b, :],
                                       start=b == 0, stop=b == nb - 1)
            L.put(mm, "pv2")

        def spread_of(r, p):
            return ARe[:, r, p, :].rearrange("p (j a t) -> p j a t", j=2, a=2)

        @block.tensor
        def _(pe):
            L = Line(pe, sem, "pe_step")
            cnt = {"acc": 0, "slab": 0, "st": 0}
            pe.wait_ge(sem("in_c"), 48)
            rms_pe(L, cnt, DT, T0)
            gemm_grid(L, cnt, 8, 18, n1, T0, src="hn")
            L.take("ys", 14)
            for j in range(4):
                st_prod(L, cnt, bones, sq[:, j % 2, :], T0, src="kks")
            L.take("tg", 2)
            for j in range(4):
                b = acc_open(L, cnt)
                L.put(mm_T(L, b, sml[0:64, 0, j * P:(j + 1) * P], yv[0:64, 12, 1:YW], T0, True, True), "acc_full")
            for j in range(4):
                b = acc_open(L, cnt)
                L.put(mm_T(L, b, sml[64:P, 0, j * P:(j + 1) * P], yv[64:P, 12, 1:YW], T0, True, True), "acc_full")
            for j in range(4):
                b = acc_open(L, cnt)
                L.put(mm_T(L, b, sml[:, 1, j * P:(j + 1) * P], y(13), T0, True, True), "acc_full")
            for j in range(4):
                st_prod(L, cnt, bones, sq[:, j % 2, :], T0, src="rkr")
            for g in range(4):
                L.take("pool")
                b = acc_open(L, cnt)
                L.put(mm_T(L, b, sml[:, 2, g * P:(g + 1) * P], y(14 + g), T0, True, True), "acc_full")
            acc_drain(L, cnt)
            for c in range(NCH + 1):
                r, t0 = c % 2, c * CH
                rp = (c - 1) % 2
                if c < NCH:
                    L.take("exp")
                    if c == 0:
                        st_drain(L, cnt)
                    if c >= 1:
                        pe.wait_ge(sem("m"), 2 * c)
                    for p in range(4):
                        g = p // 2
                        pe.matmul(ps[:, 0, g * 32:g * 32 + 32], BKe[:, r, p, :], AR[:, p, :, t0:t0 + CH],
                                  start=p % 2 == 0, stop=p % 2 == 1)
                    for p in range(4):
                        g = p // 2
                        mm = pe.matmul(ps[64:P, 0, 64 + g * 64:128 + g * 64], Ve[:, r, p, :], C("stack"),
                                       start=p % 2 == 0, stop=p % 2 == 1)
                    L.put(mm, "pm")
                if c >= 1:
                    pe.wait_ge(sem("mpow"), 3 * c)
                    pe.wait_ge(sem("q"), 3 * c - 1)
                    L.put(pe.matmul(ps[:, 4, 2 * P:3 * P], M8, Q4, start=True, stop=True), "pq")
                if c < NCH:
                    if c >= 1:
                        pe.wait_ge(sem("tok"), c)
                    for p in range(4):
                        mm = pe.transpose(ps[:, 1, p * P:(p + 1) * P], BKe[:, r, p, :], ident)
                    L.put(mm, "ptok")
                if c >= 1:
                    if c >= 2:
                        L.take("S", 1)
                        L.take("oT", 2)
                        pe.wait_ge(sem("wu"), 3 * (c - 1))
                    L.take("exp_ar")
                    for p in range(4):
                        mm = pe.matmul(ps[0:64, 5, p * 32:(p + 1) * 32], St[:, rp, p, :],
                                       spread_of(rp, p)[:, :, 0, :], start=True, stop=True)
                    L.put(mm, "pAS")
                    for g in range(2):
                        pe.matmul(ps[64 * g:64 * g + 64, 7, 0:64], G[64:P, rp, g, 0, :], UV[64:P, rp, g, :],
                                  start=True, stop=False)
                if c < NCH:
                    pe.wait_ge(sem("m"), 2 * c + 1)
                    L.put(pe.transpose(ps[:, 2, 0:P], MT, ident), "pmb")
                if c >= 1:
                    pe.wait_ge(sem("as"), c)
                    L.put(pe.matmul(ps[:, 7, 0:64], AS[0:64, :], ident[0:64, 0:64], start=False, stop=True), "pW")
                if c < NCH:
                    pe.wait_ge(sem("mb"), c + 1)
                    if c:
                        pe.wait_ge(sem("mpow"), 3 * c)
                        pe.wait_ge(sem("q"), 3 * c)
                    pe.matmul(ps[:, 3, 0:P], MT, Mb, start=True, stop=True)
                    L.put(pe.matmul(ps[:, 3, P:2 * P], Mb, MT, start=True, stop=True), "pm2")
                if c >= 1:
                    pe.wait_ge(sem("wu"), 3 * (c - 1) + 1)
                    pe.wait_ge(sem("q"), 3 * c)
                    L.put(pe.matmul(ps[:, 7, 64:128], Q8[:, rp, :], Wc, start=True, stop=True), "pU")
                if c < NCH:
                    pe.wait_ge(sem("mpow"), 3 * c + 1)
                    pe.matmul(ps[:, 3, 2 * P:3 * P], M2[:, 1, :], M2[:, 0, :], start=True, stop=True)
                    L.put(pe.matmul(ps[:, 3, 3 * P:4 * P], M2[:, 0, :], M2[:, 1, :], start=True, stop=True), "pm2")
                    pe.wait_ge(sem("m"), 2 * c + 2)
                    L.put(pe.matmul(ps[:, 4, 0:P], M2[:, 0, :], Q1, start=True, stop=True), "pq")
                if c >= 1:
                    pe.wait_ge(sem("wu"), 3 * (c - 1) + 3)
                    for p in range(4):
                        mm = pe.matmul(ps[:, 6, p * 64:(p + 1) * 64], Bt[:, rp, p, :], UV[:, rp, p // 2, :],
                                       start=True, stop=True)
                    L.put(mm, "pS")
                    for p in range(4):
                        pe.matmul(ps[0:64, 5, P + p * 32:P + (p + 1) * 32], St[:, rp, p, :],
                                  spread_of(rp, p)[:, :, 1, :], start=p == 0, stop=False)
                    for g in range(2):
                        mm = pe.matmul(ps[0:64, 5, P + 64 * g:P + 64 * g + 64], UV[:, rp, g, :], G[:, rp, g, 1, :],
                                       start=False, stop=g == 1)
                    L.put(mm, "pO")
                if c < NCH:
                    pe.wait_ge(sem("mpow"), 3 * c + 2)
                    L.put(pe.matmul(ps[:, 3, 0:P], M4[:, 1, :], M4[:, 0, :], start=True, stop=True), "pm2")
                    pe.wait_ge(sem("q"), 3 * c + 1)
                    L.put(pe.matmul(ps[:, 4, P:2 * P], M4[:, 0, :], Q2, start=True, stop=True), "pq")
            L.take("S", 1)
            L.take("oT", 2)
            pe.wait_ge(sem("mpow"), 3 * NCH)
            for j in range(4):
                st_prod(L, cnt, bones, X[1][:, j, :], T0)
                st_prod(L, cnt, bones, sq[:, 0, :], T0, src="sqg")
            gemm_grid(L, cnt, 8, 8, lambda k: X[1][:, k, :] if k < 4 else X[0][:, k - 4, :], T0, src="mix")
            rms_pe(L, cnt, DT, T0)
            mlp_pe(L, cnt, n1, T0)
            rms_pe(L, cnt, DT, T0)

            def rope_after(m):
                if 1 <= m <= 16:
                    L.take("qk")
                    st_prod(L, cnt, C("rot"), qkv[:, m - 1, :], T0)
            gemm_grid(L, cnt, 8, 24, n1, T0, src="hn", after=rope_after)
            L.take("qk", 8)
            for hd in range(8):
                b = acc_open(L, cnt)
                for i in range(4):
                    pe.transpose(ps[:, b, i * P:(i + 1) * P], qkv[:, 16 + hd, META + i * P:META + (i + 1) * P], ident)
                L.put(pe.transpose(ps[0:META, b + 1, 0:P], qkv[:, 16 + hd, 0:META], ident), "acc_full")
            L.take("rope", 16)
            L.take("vtok", 16)
            st_drain(L, cnt)

            def l1_scores(n):
                hd, i = n // 4, n % 4
                q0 = META + i * P
                for c in range(2):
                    units_at.append(cnt["acc"])
                    b = acc_open(L, cnt)
                    q = qkv[c * 64:(c + 1) * 64, hd, q0:q0 + P]
                    pe.matmul(ps[:, b, 496:512], q, qkv[c * 64:(c + 1) * 64, 8 + hd, 0:META], start=True, stop=True)
                    pe.matmul(ps[:, b + 1, 0:(i + 1) * P], q, qkv[c * 64:(c + 1) * 64, 8 + hd, META:META + (i + 1) * P],
                              start=True, stop=False)
                    L.put(pe.matmul(ps[:, b + 1, i * P:(i + 1) * P], ident, C("causal"), start=False, stop=True),
                          "acc_full")

            def l1_turn_pe(n):
                i = n % 4
                L.take("attn")
                if n >= 1:
                    pe.wait_ge(sem("aT"), 2 * n)
                A = Pc[:, n % 2, 0, :]
                for b in range(i + 1):
                    pe.transpose(ps[:, 6, b * P:(b + 1) * P], A[:, META + b * P:META + (b + 1) * P], ident)
                if n >= 1:
                    pe.wait_ge(sem("l1_out"), n)
                L.put(pe.transpose(ps[0:META, 7, 0:P], A[:, 0:META], ident), "tT")

            def l1_values(n):
                hd, i = n // 4, n % 4
                pe.wait_ge(sem("aT"), 2 * n + 2)
                for b in range(i + 1):
                    pe.matmul(ps[:, 7, P:2 * P], Vtok[:, b, hd * P:(hd + 1) * P], aT[:, n % 2, b, :],
                              start=b == 0, stop=False)
                L.put(pe.matmul(ps[:, 7, P:2 * P], Vtok[0:META, 4, hd * P:(hd + 1) * P], aT[0:META, n % 2, 4, :],
                                start=False, stop=True), "pv")
            l1_scores(0)
            l1_scores(1)
            l1_turn_pe(0)
            for n in range(32):
                if n + 2 < 32:
                    l1_scores(n + 2)
                l1_values(n)
                if n + 1 < 32:
                    l1_turn_pe(n + 1)
            pe.wait_ge(sem("l1_out"), 32)
            acc_drain(L, cnt)
            for half in range(2):
                st_open(L, cnt)
                for q in range(4):
                    L.take("sqh")
                    mm = pe.matmul(ps[32 * q:32 * q + 32, 6, 0:SEQ], ones[:, 0:32], sq[:, q % 2, 0:SEQ],
                                   start=True, stop=True)
                    L.put(mm, "st_full" if q == 3 else "sqh_used")
                sub_full.append(L.made["st_full"])
                if half:
                    L.take("head_scaled", 4)
                L.take("rinv")
                for q in range(4):
                    L.put(pe.matmul(ps[:, q, 0:SEQ], ones[32 * q:32 * q + 1, :], rs[32 * q:32 * q + 1, 0:SEQ],
                                    start=True, stop=True), "norm_out")
            L.take("head_scaled", 4)
            gemm_grid(L, cnt, 8, 8, n2, SEQ, src="hn2")
            rms_pe(L, cnt, DT, SEQ)
            mlp_pe(L, cnt, n2, SEQ)
            second_pe(L, cnt)

        @block.sync
        def _(sp):
            sp.dma_start(h[:, :, :], xin).then_inc(sem("in_x"), 16)
            sp.dma_start(cst[:, :], consts).then_inc(sem("in_c"), 16)
            sp.dma_start(par[:, :], params).then_inc(sem("in_c"), 16)
            sp.dma_start(sml[:, :, :], small).then_inc(sem("in_c"), 16)
            q = 0
            for n in range(len(plan)):
                for lo, hi in halves_of(n):
                    if q >= 2:
                        sp.wait_ge(sem("half_used"), q - 1)
                    sp.dma_start(raw_w[:, q % 2, 0:hi - lo], slabs[n, :, lo:hi]).then_inc(sem(f"half{q % 2}"), 16)
                    q += 1
            sp.wait_ge(sem("yo"), DT)
            for j in range(DT):
                sp.dma_start(out[:, j, :], hn[:, j, 0:SEQ]).then_inc(sem("stored"), 16)
            sp.wait_ge(sem("stored"), 16 * DT)

        def mlp_act(L, cnt, hx, nx, T):
            act = L.eng
            rms_act(L, cnt, hx, DT, T, ready="hx")
            for m in range(32):
                if m >= 2:
                    L.take("hid")
                evac(L, cnt, T, lambda v: act.activation(halves(sq[:, m % 2, 0:T], T), v, ACT.Relu,
                                                         scale=1.0 / WSCALE))
                L.tell("relu")
                if m % 4 == 3:
                    split_hi(L, cnt)
            L.take("hid", 2)
            for m in range(8):
                if m % 2 == 0:
                    split_hi(L, cnt)
                evac(L, cnt, T, lambda v: unscaled(L, halves(nx(m), T), v))
                if m % 2:
                    split_hi(L, cnt)
            rms_act(L, cnt, nx, DT, T)

        def second_act(L, cnt):
            act = L.eng
            rms_act(L, cnt, h2, DT, SEQ, ready="hx")
            for m in range(30):
                b = acc_in(L, cnt)
                if m < 8:
                    L.fin(act.activation(zt(m), ps[:, b, :], ACT.Silu, scale=1.0 / WSCALE), "acc_free")
                elif m < 29:
                    L.fin(unscaled(L, zt(m), ps[:, b, :]), "acc_free")
                else:
                    L.fin(act.activation(zt(m)[0:16, :], ps[0:16, b, :], ACT.Identity,
                                         bias=V("ssd_dt_bias_2")[0:16, :], scale=1.0 / WSCALE), "misc")
                    L.fin(unscaled(L, zt(m)[64:96, :], ps[64:96, b, :]), "acc_free")
                L.tell("win")
                if 9 <= m < 25:
                    L.take("conv")
                    L.fin(act.activation(zt(m - 1), sc[:, (m - 1) % 2, 0:SEQ], ACT.Silu), "xbc")
                if m % 4 == 3 or m == 29:
                    split_hi(L, cnt)
            L.take("absx")
            L.step(act.activation(adT, adT, ACT.Exp, scale=-1.0))
            L.fin(act.activation(adT, adT, ACT.Ln, bias=1.0), "lnx")
            L.fin(act.activation(tiny[0:16, 9:10], V("ssd_a_log_2")[0:16, :], ACT.Exp), "lnx")
            b = acc_in(L, cnt)
            L.fin(act.copy(dtk.rearrange("p a b -> p (a b)"), ps[:, b, 0:64]), "dtk")
            L.fin(act.copy(adk.rearrange("p a b -> p (a b)"), ps[:, b, 64:128]), "dtk")
            L.tell("acc_free")
            b = acc_in(L, cnt)
            flat = lambda t: t.rearrange("p a b -> p (a b)")
            L.fin(act.copy(flat(cumk), ps[:, b, 0:64]), "cum")
            L.fin(act.activation(flat(ncum), ps[:, b, 0:64], ACT.Copy, scale=-1.0), "cum")
            L.fin(act.activation(flat(ecum), ps[:, b, 0:64], ACT.Exp), "cum")
            L.fin(act.activation(flat(cdec), ps[:, b, 64:128], ACT.Exp), "cum")
            L.fin(act.copy(flat(dlast), ps[:, b, 64:128]), "cum")
            L.fin(act.copy(cumT[0:16, :, :], ps[0:16, b + 1, :].rearrange("p (a b) -> p a b", a=4)), "cum")
            L.tell("acc_free")
            L.take("dl")
            L.fin(act.activation(flat(dlast), flat(dlast), ACT.Exp), "dle")
            for c in range(SSD_NC):
                L.take("pb")
                L.fin(act.copy(Btk, ps[:, 5, :].rearrange("p (a b) -> p a b", a=4)), "btk")
                for g in range(4):
                    n = 4 * c + g
                    L.take("pd")
                    if n >= 2:
                        L.take("mx")
                    for e in range(4):
                        L.step(act.activation(Dm[:, n % 2, e, :], ps[:, n % 2, e * P:(e + 1) * P], ACT.Exp,
                                              bias=ncum[:, c, 4 * g + e:4 * g + e + 1]))
                    L.tell("dm")
            L.take("gated", 8)
            for g in range(4):
                rms_act(L, cnt, lambda j: zt(2 * g + j), 2, SEQ)
            rms_act(L, cnt, lambda j: zt(24 + j), 3, SEQ)
            rms_act(L, cnt, lambda j: zt(27 + j), 2, SEQ)
            L.take("mla")
            act.dma_start(sc[64:96, 1, 0:SEQ].bitcast(I32), pos.partition_broadcast(32)).then_inc(sem("in_p"), 16)
            act.dma_start(memt, memx).then_inc(sem("in_m"), 16)
            L.take("ang")
            L.fin(act.activation(sinT[64:96, :], sinT[64:96, :], ACT.Sin), "sincos")
            L.fin(act.activation(cosT[64:96, :], cosT[64:96, :], ACT.Sin), "sincos")
            L.take("krope", 2)

            def head_act(hd):
                b = acc_in(L, cnt)
                L.fin(unscaled(L, qh[0:MLA_QK, hd % 2, :], ps[0:MLA_QK, b, :]), "acc_free")
                L.tell("qh")
                b = acc_in(L, cnt)
                L.step(unscaled(L, Kh[0:64, hd % 2, :], ps[0:64, b, :]))
                L.fin(unscaled(L, vT[64:P, :], ps[64:P, b, :]), "acc_free")
                L.tell("kvh")
                b = acc_in(L, cnt)
                L.fin(act.copy(Vh[:, hd % 2, :, :], ps[:, b, 0:256].rearrange("p (a b) -> p a b", a=4)), "acc_free")
                L.tell("vh")
                if hd % 8 == 7:
                    split_hi(L, cnt)
                    split_hi(L, cnt)

            def unit_exp(n, keys, scale):
                L.take("mx2")
                b = acc_slot(cnt["acc"])
                cnt["acc"] += 1
                L.fin(act.activation(Pm[:, n % 2, 0:keys], ps[:, b, 0:keys], ACT.Exp, bias=stm[:, n % 2, 0:1],
                                     scale=scale, accum_out=stm[:, n % 2, 1:2]), "acc_free")
                L.tell("ex2")

            def unit_turn(n, nb):
                L.take("pT")
                L.fin(act.copy(pT[:, n % 2, 0:nb, :], ps[:, 6, 0:nb * P].rearrange("p (a b) -> p a b", b=P)),
                      "turned")

            def unit_out(outs):
                L.take("pv2")
                for dst, src in outs[:-1]:
                    L.step(act.copy(dst, src))
                L.fin(act.copy(*outs[-1]), "out_read")
            head_act(0)
            unit_exp(0, P, MLA_QK ** -0.5)
            unit_exp(1, 2 * P, MLA_QK ** -0.5)
            unit_turn(0, 1)
            for n in range(64):
                hd, i = n // 4, n % 4
                if i == 1 and hd + 1 < 16:
                    head_act(hd + 1)
                if n + 2 < 64:
                    unit_exp(n + 2, ((n + 2) % 4 + 1) * P, MLA_QK ** -0.5)
                row = 64 * (hd % 2)
                unit_out([(ym(hd // 2)[row:row + 64, i * P:(i + 1) * P], ps[row:row + 64, 7, 0:P])])
                if n + 1 < 64:
                    unit_turn(n + 1, (n + 1) % 4 + 1)
            mt_act(L, cnt, 2)
            rms_act(L, cnt, h2, DT, SEQ, ready="hx")
            act.wait_ge(sem("in_m"), 16)
            rms_act(L, cnt, lambda j: memt[:, j, :], DT, MEM)
            for m in range(24):
                T = SEQ if m < 8 else MEM
                dst = zt(m) if m < 8 else kmT[:, m - 8, :] if m < 16 else vmT[:, m - 16, :]
                evac(L, cnt, T, lambda v: unscaled(L, dst, v))
                L.tell("qm")
                if m % 4 == 3:
                    split_hi(L, cnt)
            for j in range(8):
                b = acc_in(L, cnt)
                L.fin(act.copy(Vm[:, :, j * P:(j + 1) * P], ps[:, b, 0:256].rearrange("p (a b) -> p a b", a=2)),
                      "acc_free")
                L.tell("vm")
            unit_exp(64, MEM, 1.0 / 16.0)
            unit_exp(65, MEM, 1.0 / 16.0)
            unit_turn(64, 2)
            for n in range(64, 80):
                hd, i = (n - 64) // 4, n % 4
                if n + 2 < 80:
                    unit_exp(n + 2, MEM, 1.0 / 16.0)
                unit_out([(hn[:, 2 * hd + x, i * P:(i + 1) * P], ps[:, 7, x * P:(x + 1) * P]) for x in range(2)])
                if n + 1 < 80:
                    unit_turn(n + 1, 2)
            mt_act(L, cnt, 4)
            rms_act(L, cnt, h2, DT, SEQ, ready="hx")
            raw = wk[:, WK0:WK0 + 4 * SEQ].rearrange("p (a b) -> p a b", a=4)
            gat = wk[:, WK0 + 8 * SEQ:WK0 + 12 * SEQ].rearrange("p (a b) -> p a b", a=4)

            def gate(m):
                if m % 4 < 2:
                    L.take("gconv")
                    L.fin(act.activation(gat[:, m % 4, :], gat[:, m % 4, :], ACT.Silu), "gsilu")
            for m in range(44):
                b = acc_in(L, cnt)
                if m >= 4:
                    L.take("rawfree")
                L.fin(unscaled(L, raw[:, m % 4, :], ps[:, b, :]), "acc_free")
                L.tell("raw")
                if m >= 1:
                    gate(m - 1)
                if m % 4 == 3:
                    split_hi(L, cnt)
            gate(43)
            mt_act(L, cnt, 1)
            rms_act(L, cnt, h2, DT, SEQ, ready="hx")

        def mt_act(L, cnt, per):
            for m in range(8):
                b = acc_in(L, cnt)
                if m >= 2:
                    L.take("mtfree")
                L.fin(unscaled(L, sq[:, m % 2, 0:SEQ], ps[:, b, :]), "acc_free")
                L.tell("mt")
                if m % per == per - 1:
                    split_hi(L, cnt)
            L.take("mtfree", 2)

        @block.scalar
        def _(act):
            L = Line(act, sem, "act_step")
            cnt = {"acc": 0}
            act.wait_ge(sem("in_x"), 16)
            act.wait_ge(sem("in_c"), 48)
            rms_act(L, cnt, h1, DT, T0)
            for n in range(NW):
                split_hi(L, cnt)
            for m in range(18):
                evac(L, cnt, T0, lambda v: unscaled(L, halves(y(m), T0), v))
                if m % 4 == 3 or m == 17:
                    split_hi(L, cnt)
            L.take("ys", 14)
            L.fin(act.activation(yv[0:64, 12, 1:YW], yv[0:64, 12, 1:YW], ACT.Tanh), "tg")
            L.fin(act.activation(y(13), y(13), ACT.Sigmoid), "tg")
            for j in range(4):
                root_act(L, T0)
            for j in range(4):
                evac(L, cnt, T0, lambda v: act.activation(halves(X[0][:, j, :], T0), v, ACT.Sigmoid,
                                                          bias=V("ev_w0", j)))
            for j in range(4):
                evac(L, cnt, T0, lambda v: act.activation(halves(X[2][:, j, :], T0), v, ACT.Sigmoid,
                                                          bias=V("ev_a0", j)))
            for j in range(4):
                evac(L, cnt, T0, lambda v: act.copy(halves(X[3][:, j, :], T0), v))
            L.tell("waG")
            L.take("cumd")
            L.fin(act.activation(X[1][:, :, :], X[0][:, :, :], ACT.Exp, scale=-DECAY), "ecum1")
            L.fin(act.activation(X[0][:, :, :], X[0][:, :, :], ACT.Exp, scale=DECAY), "ecum1")
            L.take("bk")
            for g in range(4):
                evac(L, cnt, T0, lambda v: act.activation(halves(X[0][:, g, :], T0), v, ACT.Copy,
                                                          scale=V("ev_pool_scale", g)))
            for c in range(NCH + 1):
                r, rp = c % 2, (c - 1) % 2
                t0p = (c - 1) * CH
                out_t = ps[0:64, 5, P:2 * P].rearrange("v (q j t) -> v q j t", j=2, t=CH)
                if c < NCH:
                    L.take("ptok")
                    L.fin(act.copy(Bt[:, r, :, :], ps[:, 1, :].rearrange("p (a b) -> p a b", a=4)), "tok")
                if c >= 1:
                    L.take("pAS")
                    L.fin(act.copy(AS[0:64, :], ps[0:64, 5, 0:P]), "as")
                if c < NCH:
                    L.take("pmb")
                    L.fin(act.copy(Mb, ps[:, 2, 0:P]), "mb")
                if c >= 1:
                    L.take("pW")
                    L.fin(act.copy(Wc, ps[:, 7, 0:64]), "wu")
                if c < NCH:
                    L.take("pm2")
                    L.fin(act.copy(M2, ps[:, 3, 0:2 * P].rearrange("p (a b) -> p a b", a=2)), "mpow")
                if c >= 1:
                    L.take("pU")
                    for g in range(2):
                        L.fin(act.copy(UV[0:64, rp, g, :], ps[64 * g:64 * g + 64, 7, 64:128]), "wu")
                if c < NCH:
                    L.take("pm2")
                    L.fin(act.copy(M4, ps[:, 3, 2 * P:4 * P].rearrange("p (a b) -> p a b", a=2)), "mpow")
                if c >= 1:
                    L.take("pO")
                    for j in range(2):
                        L.fin(act.copy(X[1][64 * j:64 * j + 64, :, t0p:t0p + CH], out_t[:, :, j, :]), "oT")
                if c < NCH:
                    L.take("pm2")
                    L.fin(act.copy(M8, ps[:, 3, 0:P]), "mpow")
            for j in range(4):
                L.take("cen")
                L.fin(act.activation(sq[:, 0, :], X[1][:, j, :], ACT.Square), "sqg")
                root_act(L, T0)
            for m in range(8):
                evac(L, cnt, T0, lambda v: unscaled(L, halves(mo(m), T0), v))
                if m % 4 == 3:
                    split_hi(L, cnt)
            rms_act(L, cnt, mo, DT, T0)
            mlp_act(L, cnt, h1, n1, T0)
            rms_act(L, cnt, h1, DT, T0, ready="hx")
            act.dma_start(rope1, ropes).then_inc(sem("in_r"), 16)
            act.dma_start(lamt, lamv.rearrange("a b -> (a b)").partition_broadcast(P)).then_inc(sem("in_r"), 16)
            for m in range(24):
                b = acc_in(L, cnt)
                L.fin(unscaled(L, halves(qkv[:, m, :], T0), bank(b, T0)), "acc_free")
                L.tell("qk")
                if m % 4 == 3:
                    split_hi(L, cnt)
            for hd in range(8):
                b = acc_in(L, cnt)
                L.fin(act.copy(Vtok[:, 0:4, hd * P:(hd + 1) * P], ps[:, b, :].rearrange("p (a b) -> p a b", a=4)),
                      "vtok")
                L.fin(act.copy(Vtok[0:META, 4, hd * P:(hd + 1) * P], ps[0:META, b + 1, 0:P]), "vtok")
                L.tell("acc_free")

            L.take("lamsum")
            L.fin(act.activation(tiny[:, 10:12], tiny[:, 10:12], ACT.Exp), "lamexp")

            def l1_exp(n):
                i = n % 4
                lo, hi = l1_keys(i)
                for c in range(2):
                    L.take("mx1")
                    b = acc_slot(cnt["acc"])
                    cnt["acc"] += 1
                    flat = ps[:, b:b + 2, :].rearrange("p a b -> p (a b)")
                    L.fin(act.activation(Pc[:, n % 2, c, 0:hi - lo], flat[:, lo:hi], ACT.Exp,
                                         bias=stt[:, n % 2, c:c + 1], scale=0.125,
                                         accum_out=stt[:, n % 2, 2 + c:3 + c]), "acc_free")
                L.tell("ex1")

            def l1_turn(n):
                i = n % 4
                L.take("tT")
                L.fin(act.copy(aT[:, n % 2, 0:i + 1, :],
                               ps[:, 6, 0:(i + 1) * P].rearrange("p (a b) -> p a b", b=P)), "aT")
                L.fin(act.copy(aT[0:META, n % 2, 4, :], ps[0:META, 7, 0:P]), "aT")

            def l1_out(n):
                hd, i = n // 4, n % 4
                L.take("pv")
                L.fin(act.copy(hn[:, hd, i * P:(i + 1) * P], ps[:, 7, P:2 * P]), "l1_out")
            l1_exp(0)
            l1_exp(1)
            l1_turn(0)
            for n in range(32):
                if n + 2 < 32:
                    l1_exp(n + 2)
                l1_out(n)
                if n + 1 < 32:
                    l1_turn(n + 1)
            for half in range(2):
                if half:
                    act.wait_ge(sem("st_full"), sub_full[0])
                for q in range(4):
                    if q >= 2:
                        L.take("sqh_used")
                    L.fin(act.activation(sq[:, q % 2, 0:SEQ], n2(4 * half + q), ACT.Square), "sqh")
                L.take("sqh_used")
                root_act(L, SEQ)
            for m in range(8):
                evac(L, cnt, SEQ, lambda v: unscaled(L, zt(m), v))
                if m % 4 == 3:
                    split_hi(L, cnt)
            rms_act(L, cnt, zt, DT, SEQ)
            mlp_act(L, cnt, h2, n2, SEQ)
            second_act(L, cnt)

        dcnt = {}

        def kk_norm(L, j):
            L.take("st_full")
            L.fin(L.eng.tensor_scalar(halves(rs, T0), bank(6, T0), 1e-24, None, ALU.max), "st_free")
            invert_dve(L, T0)
            L.step(L.eng.tensor_tensor(AR[:, j, 0, :], AR[:, j, 0, :], rs, ALU.mult))

        def mlp_dve(L, hx, nx, T, g):
            rms_dve(L, D, T, 1e-6)
            scale_dve(L, nx, hx, DT, T, lambda j: V("norm_g", g + j), "hn")
            for m in range(32):
                L.take("relu")
                L.step(L.eng.tensor_tensor(sc[:, m % 2, 0:T], sq[:, m % 2, 0:T], sq[:, m % 2, 0:T], ALU.mult))
                split_dve(L, sc[:, m % 2, 0:T], big[:, m * T:(m + 1) * T], "hid")
                if m % 4 == 3:
                    split_lo(L, dcnt)
            for n in range(8):
                split_lo(L, dcnt)
            rms_dve(L, D, T, 1e-6)
            add_dve(L, nx, T, lambda j: V("norm_g", g + 8 + j), hx, "hx")

        def mt_dve(L, per):
            for m in range(8):
                L.take("mt")
                L.fin(L.eng.tensor_tensor(h2(m), h2(m), sq[:, m % 2, 0:SEQ], ALU.add), "hx")
                L.tell("mtfree")
                if m % per == per - 1:
                    split_lo(L, dcnt)

        def conv_dve(L, dst, src, name, tile, ntile, taps, bias):
            w = lambda j: V(name, j * ntile + tile)
            last = L.eng.tensor_scalar(dst, src, w(taps - 1), V(bias, tile), ALU.mult, ALU.add)
            for d in range(1, taps):
                L.step(last)
                last = L.eng.scalar_tensor_tensor(dst[:, d:SEQ], src[:, 0:SEQ - d], w(taps - 1 - d), dst[:, d:SEQ],
                                                  ALU.mult, ALU.add)
            return last

        def second_dve(L, acc_next):
            dve = L.eng
            tt, ts, stt_ = dve.tensor_tensor, dve.tensor_scalar, dve.scalar_tensor_tensor
            rms_dve(L, D, SEQ, 1e-6)
            scale_dve(L, n2, h2, DT, SEQ, lambda j: V("norm_mix_w_2", j), "hn")
            split_lo(L, dcnt)
            split_lo(L, dcnt)
            for m in range(8, 24):
                dve.wait_ge(sem("win"), m + 1)
                if m >= 10:
                    L.take("xbc")
                L.fin(conv_dve(L, sc[:, m % 2, 0:SEQ], zt(m), "ssd_conv_w_2", m - 8, 16, 4, "ssd_conv_b_2"), "conv")
                if m % 4 == 3:
                    split_lo(L, dcnt)
            split_lo(L, dcnt)
            dve.wait_ge(sem("win"), 30)
            split_lo(L, dcnt)
            dt = zt(29)[0:16, :]
            L.step(ts(adT, dt, -1.0, None, ALU.mult))
            L.step(tt(adT, adT, dt, ALU.max))
            L.tell("absx")
            L.take("lnx", 2)
            L.fin(stt_(dt, dt, 0.0, adT, ALU.max, ALU.add), "dtT")
            L.fin(ts(adT, dt, tiny[0:16, 9:10], -1.0, ALU.mult, ALU.mult), "dtT")
            L.take("cum", 6)
            flat = lambda t: t.rearrange("p a b -> p (a b)")
            L.step(tt(flat(dlast), flat(dlast), flat(cumk), ALU.subtract))
            L.tell("dl")
            L.take("dle")
            L.take("xbc", 2)
            for c in range(SSD_NC):
                for q in range(2):
                    L.take("px")
                    L.fin(tt(xdt[:, 8 * q:8 * q + 8, :], ps[:, 4, :].rearrange("p (a b) -> p a b", a=8),
                             dtk[:, c, 8 * q:8 * q + 8].unsqueeze(2).to_broadcast([P, 8, 64]), ALU.mult), "xdt")
                L.fin(tt(xw, xdt, dlast[:, c, :].unsqueeze(2).to_broadcast([P, 16, 64]), ALU.mult), "xw")
                for g in range(4):
                    n = 4 * c + g
                    L.take("dm")
                    L.fin(tt(Mx[:, n % 2, :, :], Dm[:, n % 2, :, :],
                             ps[:, 2 + n % 2, 0:P].unsqueeze(1).to_broadcast([P, 4, P]), ALU.mult), "mx")
                    L.take("py")
                    hs = slice(4 * g, 4 * g + 4)
                    yg = Ytk[:, g * 256:(g + 1) * 256]
                    v4 = lambda t: t.rearrange("p (a b) -> p a b", a=4)
                    if c:
                        L.step(tt(v4(yg), v4(ps[:, 7, 0:256]), ecum[:, c, hs].unsqueeze(2).to_broadcast([P, 4, 64]),
                                  ALU.mult))
                        last = tt(yg, yg, ps[:, 6, 0:256], ALU.add)
                    else:
                        last = dve.tensor_copy(yg, ps[:, 6, 0:256])
                    if c < SSD_NC - 1:
                        L.step(last)
                        if c:
                            L.step(tt(v4(prev[:, g, :]), v4(prev[:, g, :]),
                                      cdec[:, c, hs].unsqueeze(2).to_broadcast([P, 4, 64]), ALU.mult))
                            last = tt(prev[:, g, :], prev[:, g, :], ps[:, 7, 256:512], ALU.add)
                        else:
                            last = dve.tensor_copy(prev[:, g, :], ps[:, 7, 256:512])
                    L.fin(last, "ysum")
                for q in range(2):
                    L.take("pyT")
                    s0 = c * P
                    for j in range(4):
                        m = 4 * q + j
                        ins = stt_(sc[:, 0, j * P:(j + 1) * P], zt(8 + m)[:, s0:s0 + P], V("ssd_d_2", m),
                                   ps[:, 6, j * P:(j + 1) * P], ALU.mult, ALU.add)
                        L.fin(ins, "yT") if j == 3 else L.step(ins)
                    for j in range(4):
                        m = 4 * q + j
                        L.step(tt(zt(m)[:, s0:s0 + P], zt(m)[:, s0:s0 + P], sc[:, 0, j * P:(j + 1) * P], ALU.mult))
                    L.tell("gated")
            for g in range(4):
                rms_dve(L, 256, SEQ, 1e-6)
                for j in range(2):
                    m = 2 * g + j
                    L.step(stt_(sc[:, 0, 0:SEQ], zt(m), V("ssd_norm_w_2", m), rs[:, 0:SEQ], ALU.mult, ALU.mult))
                    split_dve(L, sc[:, 0, 0:SEQ], zt(m), "mix2")
            rms_dve(L, 384, SEQ, 1e-6)
            for j in range(3):
                L.step(stt_(sc[:, 0, 0:SEQ], zt(24 + j), V("mla_q_norm_w_2", j), rs[:, 0:SEQ], ALU.mult, ALU.mult))
                split_dve(L, sc[:, 0, 0:SEQ], zt(24 + j), "lat")
            rms_dve(L, 256, SEQ, 1e-6)
            for j in range(2):
                L.step(stt_(sc[:, 0, 0:SEQ], zt(27 + j), V("mla_kv_norm_w_2", j), rs[:, 0:SEQ], ALU.mult, ALU.mult))
                split_dve(L, sc[:, 0, 0:SEQ], zt(27 + j), "lat")
            L.tell("mla")
            dve.wait_ge(sem("in_p"), 16)
            R = slice(64, 96)
            A, S, Co, t = angT[R, :], sinT[R, :], cosT[R, :], sc[R, 0, 0:SEQ]
            L.step(dve.tensor_copy(A, sc[R, 1, 0:SEQ].bitcast(I32)))
            L.step(ts(A, A, C("invfreq")[R, :], None, ALU.mult))
            MAGIC = 12582912.0
            PI = 3.1415925
            C1 = 6.28125
            C2 = float(np.float32(np.floor((2 * np.pi - C1) * 2 ** 22) / 2 ** 22))
            C3 = float(np.float32(2 * np.pi - C1 - C2))
            for dst, quarter in ((S, 0.0), (Co, 0.25)):
                L.step(ts(t, A, 1.0 / (2 * np.pi), quarter, ALU.mult, ALU.add))
                L.step(ts(t, t, MAGIC, None, ALU.add))
                L.step(ts(t, t, -MAGIC, None, ALU.add))
                L.step(stt_(dst, t, -C1, A, ALU.mult, ALU.add))
                L.step(stt_(dst, t, -C2, dst, ALU.mult, ALU.add))
                L.step(stt_(dst, t, -C3, dst, ALU.mult, ALU.add))
                if quarter:
                    L.step(ts(dst, dst, np.pi / 2, None, ALU.add))
                L.step(ts(dst, dst, PI, -PI, ALU.min, ALU.max))
            L.tell("ang")
            L.step(dve.memset(Kh[0:64, 0, :], 0.0))
            L.fin(dve.tensor_copy(Kh[R, 0, :], zt(29)[R, :]), "krope")
            L.take("sincos", 2)
            L.take("st_full")
            L.fin(tt(t, ps[R, 5, :], S, ALU.mult), "st_free")
            L.step(tt(Kh[R, 0, :], Kh[R, 0, :], Co, ALU.mult))
            L.step(tt(Kh[R, 0, :], Kh[R, 0, :], t, ALU.add))
            L.fin(dve.tensor_copy(Kh[R, 1, :], Kh[R, 0, :]), "krope")

            def head_dve(hd):
                L.take("st_full")
                L.fin(tt(t, ps[R, 5, :], S, ALU.mult), "st_free")
                q = qh[R, hd % 2, :]
                L.step(tt(q, q, Co, ALU.mult))
                L.fin(tt(q, q, t, ALU.add), "qrope")
                if hd % 8 == 7:
                    split_lo(L, dcnt)
                    split_lo(L, dcnt)

            def unit_max(n, keys, scale, b):
                L.step(dve.tensor_reduce(stm[:, n % 2, 2:3], ps[:, b, 0:keys], AX, ALU.max))
                L.fin(ts(stm[:, n % 2, 0:1], stm[:, n % 2, 2:3], -scale, None, ALU.mult), "mx2")

            def unit_norm(n, keys):
                L.take("ex2")
                L.step(dve.reciprocal(stm[:, n % 2, 3:4], stm[:, n % 2, 1:2]))
                L.fin(ts(Pm[:, n % 2, 0:keys], Pm[:, n % 2, 0:keys], stm[:, n % 2, 3:4], None, ALU.mult), "prob")

            sq_ = MLA_QK ** -0.5
            head_dve(0)
            unit_max(0, P, sq_, acc_next())
            unit_max(1, 2 * P, sq_, acc_next())
            unit_norm(0, P)
            for n in range(64):
                hd, i = n // 4, n % 4
                if i == 1 and hd + 1 < 16:
                    head_dve(hd + 1)
                if n + 2 < 64:
                    unit_max(n + 2, ((n + 2) % 4 + 1) * P, sq_, acc_next())
                if n + 1 < 64:
                    unit_norm(n + 1, ((n + 1) % 4 + 1) * P)
            for j in range(8):
                if j == 0:
                    dve.wait_ge(sem("out_read"), 64)
                L.step(dve.tensor_copy(sc[:, j % 2, 0:SEQ], ym(j)))
                split_dve(L, sc[:, j % 2, 0:SEQ], ym(j), "mix2")
            mt_dve(L, 2)
            rms_dve(L, D, SEQ, 1e-6)
            scale_dve(L, n2, h2, DT, SEQ, lambda j: V("norm_memx_w_2", j), "hn")
            dve.wait_ge(sem("in_m"), 16)
            rms_dve(L, D, MEM, 1e-6)
            scale_dve(L, lambda j: memt[:, j, :], lambda j: memt[:, j, :], DT, MEM,
                      lambda j: V("norm_mem_w_2", j), "memn")
            for n in range(6):
                split_lo(L, dcnt)
            unit_max(64, MEM, 1.0 / 16, acc_next())
            unit_max(65, MEM, 1.0 / 16, acc_next())
            unit_norm(64, MEM)
            for n in range(64, 80):
                if n + 2 < 80:
                    unit_max(n + 2, MEM, 1.0 / 16, acc_next())
                if n + 1 < 80:
                    unit_norm(n + 1, MEM)
            dve.wait_ge(sem("out_read"), 80)
            for j in range(8):
                L.step(dve.tensor_copy(sc[:, j % 2, 0:SEQ], n2(j)))
                split_dve(L, sc[:, j % 2, 0:SEQ], n2(j), "memo")
            mt_dve(L, 4)
            rms_dve(L, D, SEQ, 1e-6)
            scale_dve(L, n2, h2, DT, SEQ, lambda j: V("norm_ffn_w_2", j), "hn")
            raw = wk[:, WK0:WK0 + 4 * SEQ].rearrange("p (a b) -> p a b", a=4)
            gat = wk[:, WK0 + 8 * SEQ:WK0 + 12 * SEQ].rearrange("p (a b) -> p a b", a=4)
            for m in range(44):
                j = 2 * (m // 4) + m % 2
                tile = j + (FT2 if m % 4 >= 2 else 0)
                L.take("raw")
                ins = conv_dve(L, gat[:, m % 4, :], raw[:, m % 4, :], "ffn_conv_w_2", tile, 44, 3, "ffn_conv_b_2")
                if m % 4 < 2:
                    L.fin(ins, "gconv")
                else:
                    L.step(ins)
                if m < 40:
                    L.tell("rawfree")
                if m % 4 >= 2:
                    L.take("gsilu")
                    L.step(tt(gat[:, m % 4, :], gat[:, m % 4 - 2, :], gat[:, m % 4, :], ALU.mult))
                    split_dve(L, gat[:, m % 4, :], zt(j), "hid2")
                if m % 4 == 3:
                    split_lo(L, dcnt)
            mt_dve(L, 1)
            rms_dve(L, D, SEQ, 1e-6)
            for j in range(DT):
                L.fin(stt_(n2(j), h2(j), V("norm_final_w_2", j), rs[:, 0:SEQ], ALU.mult, ALU.mult), "yo")

        @block.vector
        def _(dve):
            L = Line(dve, sem, "dve_step")
            tt, ts, stt_ = dve.tensor_tensor, dve.tensor_scalar, dve.scalar_tensor_tensor
            dve.wait_ge(sem("in_x"), 16)
            dve.wait_ge(sem("in_c"), 48)
            L.step(dve.memset(tiny[:, :], 0.0))
            L.step(dve.memset(yv[:, :, 0:1], 0.0))
            L.step(ts(omka, par[:, COL["ev_k_a"]:COL["ev_k_a"] + 4], -1.0, 1.0, ALU.mult, ALU.add))
            rms_dve(L, D, T0, 1e-6)
            split_lo(L, dcnt)
            scale_dve(L, n1, h1, DT, T0, lambda j: V("norm_g", j), "hn")
            split_lo(L, dcnt)
            for m in range(18):
                dve.wait_ge(sem("acc_free"), m + 1)
                if m < 14:
                    L.step(tt(sc[:, 0, :], yv[:, m, 0:T0], y(m), ALU.subtract))
                    L.fin(stt_(y(m), sc[:, 0, :], V("ev_mu", m), y(m), ALU.mult, ALU.add), "ys")
                if m % 4 == 3 or m == 17:
                    split_lo(L, dcnt)
            L.tell("uin")
            for j in range(4):
                L.step(ts(AR[:, j, 0, :], y(4 + j), V("ev_k_k", j), None, ALU.mult))
                if j >= 2:
                    L.eng.wait_ge(sem("st_full"), 1 + j - 1)
                L.fin(tt(sq[:, j % 2, :], AR[:, j, 0, :], AR[:, j, 0, :], ALU.mult), "kks")
                if j >= 1:
                    kk_norm(L, j - 1)
            kk_norm(L, 3)
            L.take("waG")
            ch = lambda i: X[i].rearrange("p m (c t) -> p (m c) t", t=CH)
            a, b = 0, 1
            for s in (1, 2, 4, 8):
                L.step(dve.tensor_copy(ch(b)[:, :, 0:s], ch(a)[:, :, 0:s]))
                L.step(tt(ch(b)[:, :, s:CH], ch(a)[:, :, s:CH], ch(a)[:, :, 0:CH - s], ALU.add))
                a, b = b, a
            L.tell("cumd")
            A_, R_ = AR[:, :, 0, :], AR[:, :, 1, :]
            for j in range(4):
                L.step(ts(sc[:, 0, :], X[2][:, j, :], V("ev_k_a", j), omka[:, j:j + 1], ALU.mult, ALU.add))
                L.step(tt(y(4 + j), y(4 + j), sc[:, 0, :], ALU.mult))
            L.step(tt(X[2], X[2], A_, ALU.mult))
            L.take("ecum1", 2)
            L.step(tt(X[2], X[2], X[0], ALU.mult))
            L.step(tt(R_, Rk, X[1], ALU.mult))
            for j in range(4):
                L.step(ts(sc[:, 0, :], y(j), V("ev_r_k", j), None, ALU.mult))
                L.fin(tt(sq[:, j % 2, :], sc[:, 0, :], y(4 + j), ALU.mult), "rkr")
                L.take("st_full")
                L.fin(tt(halves(y(j), T0), bank(6, T0), halves(y(8 + j), T0), ALU.mult), "st_free")
            L.step(tt(Kk, Kk, X[0], ALU.mult))
            L.tell("bk")
            for p in range(4):
                ac = AR[:, p, 0, :].rearrange("p (c t) -> p c t", t=CH)
                ec = X[1][:, p, :].rearrange("p (c t) -> p c t", t=CH)
                L.step(stt_(ac[:, :, 1:CH], ac[:, :, 1:CH], -1.0, ec[:, :, 0:CH - 1], ALU.mult, ALU.mult))
                L.step(ts(ac[:, :, 0:1], ac[:, :, 0:1], -1.0, None, ALU.mult))
                L.step(dve.tensor_copy(PC[:, p, :], ec[:, :, CH - 1]))
            L.step(dve.memset(St[:, 0, :, :], 0.0))
            L.take("pool", 4)
            L.step(dve.memset(EXPS, 0.0))
            L.tell("elem")
            for c in range(NCH + 1):
                r = c % 2
                rp = (c - 1) % 2
                if c < NCH:
                    L.take("pm")
                    for g in range(2):
                        ins = tt(MT[64 * g:64 * g + 64, 64 * g:64 * g + 64].rearrange("p (h s) -> p h s", s=CH),
                                 ps[0:64, 0, 32 * g:32 * g + CH].unsqueeze(1).to_broadcast([64, 4, CH]),
                                 C("mask_g")[0:64, 0:64].rearrange("p (h s) -> p h s", s=CH), ALU.mult)
                        if g:
                            L.fin(ins, "m")
                        else:
                            L.step(ins)
                if c >= 1:
                    L.take("pq")
                    L.fin(tt(Q8[:, rp, :], ps[:, 4, 2 * P:3 * P], Q4, ALU.add), "q")
                if c < NCH:
                    L.step(tt(Q1, MT, ident, ALU.add))
                    L.step(tt(G[:, r, :, :, :].rearrange("p g a (h s) -> p (g a) h s", s=CH),
                              ps[:, 0, 0:64].rearrange("p (g s) -> p g s", g=4).unsqueeze(2)
                              .to_broadcast([P, 4, 4, CH]),
                              C("mask_g").rearrange("p (g h s) -> p g h s", g=4, s=CH), ALU.mult))
                    L.fin(dve.tensor_copy(UV[64:P, r, :, :],
                                          ps[64:P, 0, 64:192].rearrange("p (g v) -> p g v", g=2)), "m")
                    L.take("pq")
                    L.fin(tt(Q2, ps[:, 4, 0:P], Q1, ALU.add), "q")
                if c >= 1:
                    L.take("pS")
                    L.step(tt(St[:, r, :, :], ps[:, 6, 0:256].rearrange("p (a b) -> p a b", a=4), St[:, rp, :, :],
                              ALU.add))
                    L.fin(tt(St[:, r, :, :], St[:, r, :, :],
                             PC[:, :, c - 1].unsqueeze(2).to_broadcast([P, 4, 64]), ALU.mult), "S")
                if c < NCH:
                    L.take("pq")
                    L.fin(tt(Q4, ps[:, 4, P:2 * P], Q2, ALU.add), "q")
            L.take("oT", 2 * NCH)
            for j in range(4):
                o = X[1][:, j, :]
                L.take("st_full")
                L.fin(stt_(halves(o, T0), bank(6, T0), -1.0 / 64, halves(o, T0), ALU.mult, ALU.add), "st_free")
                L.tell("cen")
                L.take("st_full")
                L.fin(ts(halves(rs, T0), bank(6, T0), 1.0 / 64, 64e-5, ALU.mult, ALU.add), "st_free")
                invert_dve(L, T0)
                L.step(tt(o, o, rs, ALU.mult))
                L.step(ts(o, o, V("ev_ln_w", j), V("ev_ln_b", j), ALU.mult, ALU.add))
                L.step(tt(o, o, y(j), ALU.add))
                L.step(tt(sc[:, 1, :], o, X[3][:, j, :], ALU.mult))
                split_dve(L, sc[:, 1, :], o, "mix")
            for j in range(4):
                L.step(dve.tensor_copy(sc[:, 1, :], X[0][:, j, :]))
                split_dve(L, sc[:, 1, :], X[0][:, j, :], "mix")
            split_lo(L, dcnt)
            split_lo(L, dcnt)
            rms_dve(L, D, T0, 1e-6)
            add_dve(L, mo, T0, lambda j: V("norm_g", 8 + j), h1, "hx")
            mlp_dve(L, h1, n1, T0, 16)
            rms_dve(L, D, T0, 1e-6)
            scale_dve(L, n1, h1, DT, T0, lambda j: V("norm_g", 32 + j), "hn")
            dve.wait_ge(sem("in_r"), 32)
            for m in range(16):
                L.take("st_full")
                t = sc[:, 0, :]
                L.fin(tt(halves(t, T0), bank(6, T0), halves(rope1[:, 1, :], T0), ALU.mult), "st_free")
                L.step(tt(qkv[:, m, :], qkv[:, m, :], rope1[:, 0, :], ALU.mult))
                L.fin(tt(qkv[:, m, :], qkv[:, m, :], t, ALU.add), "rope")
                if m % 4 == 3:
                    split_lo(L, dcnt)
            split_lo(L, dcnt)
            split_lo(L, dcnt)
            L.step(tt(lamt[:, 0:64], lamt[:, 0:64], lamt[:, 64:128], ALU.mult))
            L.step(tt(lamt[:, 128:192], lamt[:, 128:192], lamt[:, 192:256], ALU.mult))
            L.step(dve.tensor_reduce(tiny[:, 10:11], lamt[:, 0:64], AX, ALU.add))
            L.step(dve.tensor_reduce(tiny[:, 11:12], lamt[:, 128:192], AX, ALU.add))
            L.tell("lamsum")
            L.take("lamexp")
            L.step(stt_(lam, tiny[:, 10:11], LAM_INIT, tiny[:, 11:12], ALU.add, ALU.subtract))
            L.step(ts(lam, lam, -1.0, None, ALU.mult))
            L.step(ts(subw, V("od_subln_w"), 1.0 - LAM_INIT, None, ALU.mult))

            def l1_max(n):
                lo, hi = l1_keys(n % 4)
                for c in range(2):
                    b = acc_next()
                    flat = ps[:, b:b + 2, :].rearrange("p a b -> p (a b)")
                    L.step(dve.tensor_reduce(stt[:, n % 2, 4 + c:5 + c], flat[:, lo:hi], AX, ALU.max))
                    L.fin(ts(stt[:, n % 2, c:c + 1], stt[:, n % 2, 4 + c:5 + c], -0.125, None, ALU.mult), "mx1")

            def l1_mix(n):
                i = n % 4
                w = META + (i + 1) * P
                L.take("ex1")
                s = stt[:, n % 2, :]
                L.step(dve.reciprocal(s[:, 6:8], s[:, 2:4]))
                L.step(tt(s[:, 7:8], s[:, 7:8], lam, ALU.mult))
                L.step(ts(Pc[:, n % 2, 1, 0:w], Pc[:, n % 2, 1, 0:w], s[:, 7:8], None, ALU.mult))
                L.fin(stt_(Pc[:, n % 2, 0, 0:w], Pc[:, n % 2, 0, 0:w], s[:, 6:7], Pc[:, n % 2, 1, 0:w],
                           ALU.mult, ALU.add), "attn")
            units = iter(units_at)

            def acc_next():
                k = next(units)
                dve.wait_ge(sem("acc_full"), k + 1)
                return acc_slot(k)
            l1_max(0)
            l1_max(1)
            l1_mix(0)
            for n in range(32):
                if n + 2 < 32:
                    l1_max(n + 2)
                if n + 1 < 32:
                    l1_mix(n + 1)
            for half in range(2):
                rms_dve(L, P, SEQ, 1e-5)
                L.tell("rinv")
                for hd in range(4 * half, 4 * half + 4):
                    t = sc[:, hd % 2, 0:SEQ]
                    L.take("norm_out")
                    L.fin(stt_(t, n2(hd), subw, ps[:, hd % 4, 0:SEQ], ALU.mult, ALU.mult), "head_scaled")
                    split_dve(L, t, n2(hd), "hn2")
            split_lo(L, dcnt)
            split_lo(L, dcnt)
            rms_dve(L, D, SEQ, 1e-6)
            add_dve(L, zt, SEQ, lambda j: V("norm_g", 40 + j), h2, "hx")
            mlp_dve(L, h2, n2, SEQ, 48)
            second_dve(L, acc_next)

        def spread(flat, at, pairs, group, width):
            v = flat[:, at:at + width]
            dims = [[group, 2], [pairs, 2]] + ([[1, width]] if width == CH else [[CH, 2], [1, CH]])
            return bass.AP(tensor=v.tensor, offset=v.offset, ap=[list(v.ap[0])] + dims)

        @block.gpsimd
        def _(pool):
            L = Line(pool, sem, "pool_step")
            pool.wait_ge(sem("in_c"), 48)
            L.take("uin")
            tmp = [wk[:, WK0 + i * T0:WK0 + (i + 1) * T0] for i in range(2)]
            for g in range(4):
                u = y(14 + g)
                cur = u
                for i in range(g + 1):
                    s = 1 << i
                    nxt = tmp[i % 2]
                    L.step(pool.tensor_copy(nxt[:, 0:s], cur[:, 0:s]))
                    L.step(pool.tensor_tensor(nxt[:, s:T0], cur[:, s:T0], cur[:, 0:T0 - s], ALU.add))
                    cur = nxt
                w = 2 << g
                L.step(pool.tensor_tensor(cur[:, 0:16], cur[:, 0:16], C("invcnt")[:, g * 16:(g + 1) * 16], ALU.mult))
                L.step(pool.tensor_scalar(cur[:, 16:T0], cur[:, 16:T0], 1.0 / w, None, ALU.mult))
                L.fin(pool.tensor_tensor(u, cur, u, ALU.subtract), "pool")
            L.take("elem")
            for c in range(NCH):
                r, t0 = c % 2, c * CH
                if c >= 2:
                    L.take("ptok")
                for j in range(2):
                    rows = slice(64 * j, 64 * j + 64)
                    flat = [x[rows, r, :, :].rearrange("p q n -> p (q n)") for x in (BKe, Ve)]
                    for at, x, src in ((0, 0, X[2]), (64, 0, Kk), (0, 1, Vk)):
                        step = (P, 64)[x]
                        L.step(pool.tensor_copy(
                            spread(flat[x], at + j * CH, step + 2 * CH, 2 * step, CH),
                            src[rows, :, t0:t0 + CH].rearrange("p (g q) t -> p g q t", g=2)))
                L.tell("exp")
                if c >= 2:
                    L.take("pO")
                for j in range(2):
                    rows = slice(64 * j, 64 * j + 64)
                    L.step(pool.tensor_copy(ARe[rows, r, :, j * 32:j * 32 + 32].rearrange("p q (a t) -> p q a t", a=2),
                                            AR[rows, :, :, t0:t0 + CH]))
                L.tell("exp_ar")


def kernel(**inputs):
    import concourse.bacc as bacc
    from concourse.bass_utils import run_bass_kernel_spmd

    inputs = {k: np.ascontiguousarray(v) for k, v in inputs.items()}
    plan = slab_plan()
    feat = lambda a: np.ascontiguousarray(a.T.reshape(-1, P, a.shape[0]).transpose(1, 0, 2))
    arrays = {
        "slabs": lay_slabs(inputs, plan),
        "xin": feat(np.concatenate([inputs["meta"], inputs["x"][0]], 0)),
        "params": lay_params(inputs),
        "small": lay_small(inputs),
        "consts": constants(),
        "ropes": rope_constants().reshape(P, 2, T0),
        "lamv": inputs["od_lambda"][0],
        "memx": feat(inputs["mem_2"][0]),
        "pos": inputs["positions_2"][0].astype(np.int32),
    }
    nc = bacc.Bacc("TRN2", target_bir_lowering=False, num_devices=1)
    args = [nc.dram_tensor(n, a.shape, mybir.dt.from_np(a.dtype), kind="ExternalInput").ap()
            for n, a in arrays.items()]
    out = nc.dram_tensor("out", (P, DT, SEQ), F32, kind="ExternalOutput").ap()
    build(nc, *args, out, plan)
    r = run_bass_kernel_spmd(nc, [arrays], core_ids=[0]).results[0]["out"]
    return np.ascontiguousarray(r.transpose(2, 1, 0).reshape(1, SEQ, D))
```
